# Optimizing a Trainium2 kernel written in Bass

```python
import math
import jax, jax.numpy as jnp
from jax import lax
import numpy as np

D_MODEL = 2048
BATCH = 1
SEQ = 256
DEPTH = 2

HEAD_DIM = 64
BLOCK = 128
GROUP_WIDTH = D_MODEL // 4
MIX_WIDTH = 4 * GROUP_WIDTH
ROPE_THETA = 10000.0
NEG_INF = -1e30
LN_EPS = 1e-5
RMS_EPS = 1e-5

A_HEADS = GROUP_WIDTH // HEAD_DIM
A_KV_HEADS = 2
SWA_WINDOW = 128
B_HEADS = GROUP_WIDTH // (2 * HEAD_DIM)
B_VDIM = 2 * HEAD_DIM
C_HEADS = GROUP_WIDTH // HEAD_DIM
DILATION_PAIRS = ((128, 1), (512, 4), (2048, 16))
D_HEADS = GROUP_WIDTH // HEAD_DIM
IDX_HEADS = 8
IDX_DIM = 64
DSA_TOPK_MAX = 256
PEER_HEADS = 8
PEER_TOPK = 16
N_KEYS = 128
N_EXPERTS = N_KEYS * N_KEYS
PEER_QDIM = 256
PEER_HALF = PEER_QDIM // 2
PEER_BLOCK = 128
ALPHA = (2 * DEPTH) ** 0.25
BETA = (8 * DEPTH) ** -0.25

IN_SPLITS = (
    A_HEADS * HEAD_DIM, A_KV_HEADS * HEAD_DIM, A_KV_HEADS * HEAD_DIM,
    B_HEADS * 2 * HEAD_DIM, B_HEADS * 2 * HEAD_DIM, B_HEADS * B_VDIM,
    C_HEADS * HEAD_DIM, C_HEADS * HEAD_DIM, C_HEADS * HEAD_DIM,
    D_HEADS * HEAD_DIM, HEAD_DIM, HEAD_DIM,
    IDX_HEADS * IDX_DIM, IDX_DIM, IDX_HEADS,
)
VALUE_SLOTS = (2, 5, 8, 11)
IN_WIDTH = sum(IN_SPLITS)

kernel_name = 'hybrid_headgroup_swa_diff_dilated_dsa_peer_deepnorm'

def layer_norm(x, g, b):
    xf = x.astype(jnp.float32)
    mu = jnp.mean(xf, -1, keepdims=True)
    var = jnp.mean(jnp.square(xf - mu), -1, keepdims=True)
    y = (xf - mu) * lax.rsqrt(var + LN_EPS)
    return (y * g.astype(jnp.float32) + b.astype(jnp.float32)).astype(x.dtype)

def rope_tables(seq_len):
    half = HEAD_DIM // 2
    inv_freq = ROPE_THETA ** (-jnp.arange(half, dtype=jnp.float32) / half)
    ang = jnp.arange(seq_len, dtype=jnp.float32)[:, None] * inv_freq[None, :]
    return jnp.cos(ang), jnp.sin(ang)

def apply_rope(t, cos, sin):
    half = t.shape[-1] // 2
    tf = t.astype(jnp.float32)
    t1, t2 = tf[..., :half], tf[..., half:]
    return jnp.concatenate([t1 * cos - t2 * sin, t1 * sin + t2 * cos], -1).astype(t.dtype)

def banded_attention(q, k, v, max_dist):
    b, hk, g, L, hd = q.shape
    nb = -(-L // BLOCK)
    pad = nb * BLOCK - L
    qp = jnp.pad(q, ((0, 0), (0, 0), (0, 0), (0, pad), (0, 0))).reshape(b, hk, g, nb, BLOCK, hd)

    def key_blocks(t):
        tp = jnp.pad(t, ((0, 0), (0, 0), (BLOCK, pad), (0, 0))).reshape(b, hk, nb + 1, BLOCK, t.shape[-1])
        return jnp.concatenate([tp[:, :, :-1], tp[:, :, 1:]], axis=3)

    kb, vb = key_blocks(k), key_blocks(v)
    s = jnp.einsum('bhgnqd,bhnkd->bhgnqk', qp.astype(jnp.float32), kb.astype(jnp.float32)) * HEAD_DIM ** -0.5
    qi = jnp.arange(BLOCK)[:, None] + BLOCK
    ki = jnp.arange(2 * BLOCK)[None, :]
    dist = qi - ki
    kabs = jnp.arange(nb)[:, None, None] * BLOCK - BLOCK + ki[None]
    mask = ((dist >= 0) & (dist <= max_dist))[None] & (kabs >= 0)
    s = jnp.where(mask, s, NEG_INF)
    m = jnp.max(s, -1)
    p = jnp.exp(s - m[..., None])
    l = jnp.sum(p, -1)
    acc = jnp.einsum('bhgnqk,bhnkd->bhgnqd', p, vb.astype(jnp.float32))
    acc = acc.reshape(b, hk, g, nb * BLOCK, -1)[..., :L, :]
    m = m.reshape(b, hk, g, nb * BLOCK)[..., :L]
    l = l.reshape(b, hk, g, nb * BLOCK)[..., :L]
    return acc, m, l

def fold_residues(t, dil):
    bsz, h, L = t.shape[:3]
    rest = t.shape[3:]
    t = t.reshape(bsz, h, L // dil, dil, *rest)
    t = jnp.moveaxis(t, 3, 1)
    return t.reshape(bsz * dil, h, L // dil, *rest)

def unfold_residues(t, batch, dil):
    bd, h, ld = t.shape[:3]
    rest = t.shape[3:]
    t = t.reshape(batch, dil, h, ld, *rest)
    t = jnp.moveaxis(t, 1, 3)
    return t.reshape(batch, h, ld * dil, *rest)

def dilated_mixture(q, k, v):
    bsz = q.shape[0]
    accs, ms, ls = [], [], []
    for window, dil in DILATION_PAIRS:
        acc, m, l = banded_attention(fold_residues(q, dil)[:, :, None], fold_residues(k, dil),
                                     fold_residues(v, dil), window // dil)
        accs.append(unfold_residues(acc[:, :, 0], bsz, dil))
        ms.append(unfold_residues(m[:, :, 0], bsz, dil))
        ls.append(unfold_residues(l[:, :, 0], bsz, dil))
    m_all = jnp.stack(ms)
    w = jnp.exp(m_all - jnp.max(m_all, 0))
    num = jnp.sum(w[..., None] * jnp.stack(accs), 0)
    den = jnp.sum(w * jnp.stack(ls), 0)
    return num / den[..., None]

def diff_attention(q1, q2, k1, k2, v, lam):
    bsz, h, L, hd = q1.shape
    nb = L // BLOCK
    kpos = jnp.arange(L)
    k1f, k2f, vf = k1.astype(jnp.float32), k2.astype(jnp.float32), v.astype(jnp.float32)
    scale = HEAD_DIM ** -0.5

    def blk(inp):
        qb1, qb2, n = inp
        qpos = n * BLOCK + jnp.arange(BLOCK)
        causal = kpos[None, :] <= qpos[:, None]
        s1 = jnp.where(causal, jnp.einsum('bhqd,bhkd->bhqk', qb1.astype(jnp.float32), k1f) * scale, NEG_INF)
        s2 = jnp.where(causal, jnp.einsum('bhqd,bhkd->bhqk', qb2.astype(jnp.float32), k2f) * scale, NEG_INF)
        a = jax.nn.softmax(s1, -1) - lam * jax.nn.softmax(s2, -1)
        return jnp.einsum('bhqk,bhkd->bhqd', a, vf)

    def to_blocks(t):
        return t.reshape(bsz, h, nb, BLOCK, t.shape[-1]).transpose(2, 0, 1, 3, 4)

    out = lax.map(blk, (to_blocks(q1), to_blocks(q2), jnp.arange(nb)))
    return out.transpose(1, 2, 0, 3, 4).reshape(bsz, h, L, -1)

def dsa_attention(q, k, v, iq, ik, iw, topk):
    bsz, h, L, hd = q.shape
    nb = L // BLOCK
    kpos = jnp.arange(L)
    ikf = ik.astype(jnp.float32)

    def blk(inp):
        qb, iqb, iwb, n = inp
        qpos = n * BLOCK + jnp.arange(BLOCK)
        sc = jax.nn.relu(jnp.einsum('bhqd,bsd->bqhs', iqb.astype(jnp.float32), ikf) * IDX_DIM ** -0.5)
        score = jnp.einsum('bqh,bqhs->bqs', iwb.astype(jnp.float32) * IDX_HEADS ** -0.5, sc)
        causal = kpos[None, :] <= qpos[:, None]
        score = jnp.where(causal[None], score, NEG_INF)
        _, idx = lax.top_k(score, topk)
        ksel = jax.vmap(lambda kk, ii: kk[ii])(k, idx).astype(jnp.float32)
        vsel = jax.vmap(lambda vv, ii: vv[ii])(v, idx).astype(jnp.float32)
        valid = idx <= qpos[None, :, None]
        s = jnp.einsum('bhqd,bqkd->bhqk', qb.astype(jnp.float32), ksel) * HEAD_DIM ** -0.5
        s = jnp.where(valid[:, None], s, NEG_INF)
        p = jax.nn.softmax(s, -1)
        return jnp.einsum('bhqk,bqkd->bhqd', p, vsel)

    def to_blocks(t):
        return t.reshape(bsz, t.shape[1], nb, BLOCK, t.shape[-1]).transpose(2, 0, 1, 3, 4)

    iwb = iw.reshape(bsz, nb, BLOCK, IDX_HEADS).transpose(1, 0, 2, 3)
    out = lax.map(blk, (to_blocks(q), to_blocks(iq), iwb, jnp.arange(nb)))
    return out.transpose(1, 2, 0, 3, 4).reshape(bsz, h, L, hd)

def hybrid_mixer(x, w_in, sinks, lam_p, sub_g, w_out, layer_idx, cos, sin):
    b, L, _ = x.shape
    proj = jnp.einsum('bld,dk->blk', x, w_in)
    points = [int(p) for p in np.cumsum(IN_SPLITS)[:-1]]
    (aq, ak, av, bq, bk, bv, cq, ck, cv, dq, dk, dv, iq, ik, iw) = jnp.split(proj, points, axis=-1)

    def heads(t, n):
        return t.reshape(b, L, n, -1).transpose(0, 2, 1, 3)

    def merge(o):
        return o.transpose(0, 2, 1, 3).reshape(b, L, -1)

    qa = apply_rope(heads(aq, A_HEADS), cos, sin).reshape(b, A_KV_HEADS, A_HEADS // A_KV_HEADS, L, HEAD_DIM)
    ka = apply_rope(heads(ak, A_KV_HEADS), cos, sin)
    va = heads(av, A_KV_HEADS)
    acc, m, l = banded_attention(qa, ka, va, SWA_WINDOW - 1)
    sink = sinks.astype(jnp.float32).reshape(1, A_KV_HEADS, -1, 1)
    m_all = jnp.maximum(m, sink)
    corr = jnp.exp(m - m_all)
    den = l * corr + jnp.exp(sink - m_all)
    oa = (acc * (corr / den)[..., None]).reshape(b, A_HEADS, L, HEAD_DIM)

    bq2 = bq.reshape(b, L, B_HEADS, 2, HEAD_DIM).transpose(3, 0, 2, 1, 4)
    bk2 = bk.reshape(b, L, B_HEADS, 2, HEAD_DIM).transpose(3, 0, 2, 1, 4)
    lam_init = 0.8 - 0.6 * math.exp(-0.3 * layer_idx)
    lp = lam_p.astype(jnp.float32)
    lam = jnp.exp(jnp.sum(lp[0] * lp[1])) - jnp.exp(jnp.sum(lp[2] * lp[3])) + lam_init
    ob = diff_attention(apply_rope(bq2[0], cos, sin), apply_rope(bq2[1], cos, sin),
                        apply_rope(bk2[0], cos, sin), apply_rope(bk2[1], cos, sin),
                        heads(bv, B_HEADS), lam)
    ob = ob * lax.rsqrt(jnp.mean(jnp.square(ob), -1, keepdims=True) + RMS_EPS) \
        * sub_g.astype(jnp.float32) * (1.0 - lam_init)

    oc = dilated_mixture(apply_rope(heads(cq, C_HEADS), cos, sin), apply_rope(heads(ck, C_HEADS), cos, sin),
                         heads(cv, C_HEADS))

    topk = min(DSA_TOPK_MAX, L // 4)
    od = dsa_attention(apply_rope(heads(dq, D_HEADS), cos, sin), apply_rope(dk, cos, sin), dv,
                       apply_rope(heads(iq, IDX_HEADS), cos, sin), apply_rope(ik, cos, sin), iw, topk)

    mixed = jnp.concatenate([merge(oa), merge(ob), merge(oc), merge(od)], -1).astype(x.dtype)
    return jnp.einsum('blk,kd->bld', mixed, w_out)

def peer_ffn(x, wq, sub_keys, u, v):
    b, L, d = x.shape
    q = jnp.einsum('bld,dk->blk', x, wq).reshape(b, L, PEER_HEADS, 2, PEER_HALF).astype(jnp.float32)
    s = jnp.einsum('blhpc,hpnc->blhpn', q, sub_keys.astype(jnp.float32))
    s1, i1 = lax.top_k(s[..., 0, :], PEER_TOPK)
    s2, i2 = lax.top_k(s[..., 1, :], PEER_TOPK)
    cand = (s1[..., :, None] + s2[..., None, :]).reshape(b, L, PEER_HEADS, PEER_TOPK * PEER_TOPK)
    cidx = (i1[..., :, None] * N_KEYS + i2[..., None, :]).reshape(b, L, PEER_HEADS, PEER_TOPK * PEER_TOPK)
    top_s, pos = lax.top_k(cand, PEER_TOPK)
    eidx = jnp.take_along_axis(cidx, pos, axis=-1)
    g = jax.nn.softmax(top_s, -1)
    n_sel = PEER_HEADS * PEER_TOPK
    nb = (b * L) // PEER_BLOCK
    xb = x.reshape(nb, PEER_BLOCK, d)
    eb = eidx.reshape(nb, PEER_BLOCK, n_sel)
    gb = g.reshape(nb, PEER_BLOCK, n_sel)

    def blk(inp):
        xt, et, gt = inp
        h = jnp.einsum('td,tkd->tk', xt, u[et]).astype(jnp.float32)
        a = gt * jax.nn.gelu(h, approximate=False)
        return jnp.einsum('tk,tkd->td', a.astype(v.dtype), v[et])

    out = lax.map(blk, (xb, eb, gb))
    return out.reshape(b, L, d).astype(x.dtype)

def setup_inputs(seed: int = 0) -> dict:
    key = jax.random.key(seed)
    ks = jax.random.split(key, 14)
    f = jnp.float32
    offsets = np.concatenate([[0], np.cumsum(IN_SPLITS)])
    col_scale = np.ones((IN_WIDTH,), np.float32)
    for slot in VALUE_SLOTS:
        col_scale[offsets[slot]:offsets[slot + 1]] = BETA
    x = jax.random.normal(ks[0], (BATCH, SEQ, D_MODEL), f)
    w_in = jax.random.normal(ks[1], (DEPTH, D_MODEL, IN_WIDTH), f) * (D_MODEL ** -0.5) * jnp.asarray(col_scale)
    attn_sinks = 0.5 * jax.random.normal(ks[2], (DEPTH, A_HEADS), f)
    diff_lambda = 0.1 * jax.random.normal(ks[3], (DEPTH, 4, HEAD_DIM), f)
    diff_norm_g = 1.0 + 0.02 * jax.random.normal(ks[4], (DEPTH, B_VDIM), f)
    w_out = jax.random.normal(ks[5], (DEPTH, MIX_WIDTH, D_MODEL), f) * (MIX_WIDTH ** -0.5) * BETA
    ln1_g = 1.0 + 0.02 * jax.random.normal(ks[6], (DEPTH, D_MODEL), f)
    ln1_b = 0.02 * jax.random.normal(ks[7], (DEPTH, D_MODEL), f)
    peer_wq = jax.random.normal(ks[8], (DEPTH, D_MODEL, PEER_HEADS * PEER_QDIM), f) * (D_MODEL ** -0.5)
    peer_keys = jax.random.normal(ks[9], (DEPTH, PEER_HEADS, 2, N_KEYS, PEER_HALF), f) * (PEER_HALF ** -0.5)
    peer_u = jax.random.normal(ks[10], (DEPTH, N_EXPERTS, D_MODEL), f) * (D_MODEL ** -0.5)
    peer_v = jax.random.normal(ks[11], (DEPTH, N_EXPERTS, D_MODEL), f) * BETA * (PEER_HEADS ** -0.5)
    ln2_g = 1.0 + 0.02 * jax.random.normal(ks[12], (DEPTH, D_MODEL), f)
    ln2_b = 0.02 * jax.random.normal(ks[13], (DEPTH, D_MODEL), f)
    return {'x': x, 'w_in': w_in, 'attn_sinks': attn_sinks, 'diff_lambda': diff_lambda,
            'diff_norm_g': diff_norm_g, 'w_out': w_out, 'ln1_g': ln1_g, 'ln1_b': ln1_b,
            'peer_wq': peer_wq, 'peer_keys': peer_keys, 'peer_u': peer_u, 'peer_v': peer_v,
            'ln2_g': ln2_g, 'ln2_b': ln2_b}

def reference(x, w_in, attn_sinks, diff_lambda, diff_norm_g, w_out, ln1_g, ln1_b,
              peer_wq, peer_keys, peer_u, peer_v, ln2_g, ln2_b):
    L = x.shape[1]
    cos, sin = rope_tables(L)
    for i in range(DEPTH):
        y = hybrid_mixer(x, w_in[i], attn_sinks[i], diff_lambda[i], diff_norm_g[i], w_out[i], i, cos, sin)
        x = layer_norm(ALPHA * x + y, ln1_g[i], ln1_b[i])
        y = peer_ffn(x, peer_wq[i], peer_keys[i], peer_u[i], peer_v[i])
        x = layer_norm(ALPHA * x + y, ln2_g[i], ln2_b[i])
    return x


_drawn_inputs = setup_inputs


def setup_inputs(seed=0):
    import zlib

    import numpy as np

    out = dict(_drawn_inputs(seed))
    spreads = {}
    factors = {'attn_sinks': 8.0, 'diff_lambda': 5.29, 'diff_norm_g': 7.636}
    for name, (base, spread) in spreads.items():
        noise = np.random.default_rng([zlib.crc32(name.encode()), seed]).standard_normal(out[name].shape)
        drawn = base * np.exp(spread * noise) if base else spread * noise
        out[name] = __import__('jax').numpy.asarray(drawn.astype(out[name].dtype))
    for name, factor in factors.items():
        out[name] = (out[name] * factor).astype(out[name].dtype)
    return out
```

```python
from contextlib import ExitStack
import math

import numpy as np

import concourse.bass as bass
from concourse import mybir

F32 = mybir.dt.float32
F32R = mybir.dt.float32r
U32 = mybir.dt.uint32
ALU = mybir.AluOpType
ACT = mybir.ActivationFunctionType
AX = mybir.AxisListType.X

P = 128
DEPTH, D, L = 2, 2048, 256
NB = L // P
DC = D // P
W = 512
HD = 64
HALF = HD // 2
TILE = 2048
NRAW, NSPLIT = 4, 2
ALPHA = (2 * DEPTH) ** 0.25
NEG = -1e30
TAKEN = -3e38
EPS = 1e-5
SCALE = HD ** -0.5
TOPK = min(256, L // 4)
PH, PK, NKEY = 8, 16, 128
NSEL = PH * PK
NE = NKEY * NKEY

G_AQ, G_BQ, G_BK, G_CQ, G_CK, G_DQ, G_IQ, G_MIX, G_BV, G_CV = range(10)
NG_IN = 10
KC = 4
TPG = DC // KC
N_IN, N_OUT, N_WQ, N_U, N_V = NG_IN * TPG, D // W * TPG, D // W * TPG, NE // P, NE // P
AT_IN = 0
AT_OUT = AT_IN + N_IN
AT_WQ = AT_OUT + N_OUT
AT_U = AT_WQ + N_WQ
AT_V = AT_U + N_U
N_TILES = AT_V + N_V
PAIR = {"aq": 0, "bq": 4, "bk": 8, "cq": 12, "ck": 16, "dq": 20, "iq": 24, "ak": 28, "dk": 30, "ik": 31}
V_A, V_D, V_IW, V_B, V_C, V_END = 0, 128, 192, 200, 712, 1224
MIX_A, MIX_B, MIX_C, MIX_D = 0, 512, 1024, 1536


def units():
    out = []
    item = 0
    for kind, heads in (("A", 8), ("B", 4), ("C", 8), ("D", 8)):
        for h in range(heads):
            for b in range(NB):
                n = 2 if kind == "B" else 1
                out.append((kind, h, b, list(range(item, item + n))))
                item += n
    return out, item


def score_operands(kind, h, part):
    if kind == "A":
        return PAIR["aq"] + h // 2, PAIR["ak"] + h // 4, h % 2
    if kind == "B":
        return PAIR["bq"] + h, PAIR["bk"] + h, part
    if kind == "C":
        return PAIR["cq"] + h // 2, PAIR["ck"] + h // 2, h % 2
    return PAIR["dq"] + h // 2, PAIR["dk"], h % 2


def build(nc, x_in, w_in, w_out, wq, keys, u_t, v_t, ln, sinks, lamp, subg, layer_consts,
          rope, masks, eye, iota, out):
    UNITS, N_ITEMS = units()
    n_units = len(UNITS)
    a_dram = nc.dram_tensor("gates_scratch", [NKEY, P, L], F32, kind="Internal").ap()
    g_dram = nc.dram_tensor("gelu_scratch", [NKEY, P, L], F32, kind="Internal").ap()

    with ExitStack() as ctx:
        def sb(name, shape, dt=F32):
            return ctx.enter_context(nc.sbuf_tensor(name, shape, dt))

        x = sb("x", [P, NB, D])
        xh = sb("xh", [P, DC, L], F32R)
        xl = sb("xl", [P, DC, L], F32R)
        raw = [sb(f"raw{i}", [P, TILE]) for i in range(NRAW)]
        hi = [sb(f"hi{i}", [P, TILE], F32R) for i in range(NSPLIT)]
        lo = [sb(f"lo{i}", [P, TILE], F32R) for i in range(NSPLIT)]
        arena = sb("arena", [P, 16384])
        scr = sb("scr", [P, 4096])
        ident = sb("ident", [P, P])
        iota_k = sb("iota_k", [P, NKEY])
        par = sb("par", [P, 8 + 128 + 4])
        st = sb("st", [P, 4, N_ITEMS])
        small = sb("small", [P, 80])
        key_cols = [small[:, 64 + i * 8:72 + i * 8] for i in range(2)]
        stats = sb("stats", [P, 4 * 6 + 2 + 2])
        sel = sb("sel", [P, 3, NB, NSEL])
        sel_t = sb("sel_t", [P, 3, L])
        top_v = sb("top_v", [P, 2 * PH, PK])
        top_i = sb("top_i", [P, 2 * PH, PK], U32)
        ah = [sb(f"ah{i}", [P, L], F32R) for i in range(2)]
        al = [sb(f"al{i}", [P, L], F32R) for i in range(2)]

        sinks_b = par[:, 0:8]
        subg_b = par[:, 8:136]
        lay_b = par[:, 136:140]

        def region(base, *shape):
            n = int(np.prod(shape))
            v = arena[:, base:base + n]
            if len(shape) == 1:
                return v, base + n
            names = "abc"[:len(shape)]
            return v.rearrange(f"p ({' '.join(names)}) -> p {' '.join(names)}",
                               **{k: s for k, s in zip(names, shape)}), base + n

        qk_t, at = region(0, 32, L)
        vals, at = region(at, NB, V_END)
        mixed, at = region(at, NB, D)
        bias_causal, at = region(at, L)
        bias_swa, at = region(at, L)
        bias_dil, at = region(at, L)
        count_dil, at = region(at, L)
        trig, at = region(at, NB, 2, HD)
        lamp_b, at = region(at, 4 * HD)
        assert at <= 16384
        ln_gb, at = region(0, 2, D)
        q_t, at = region(at, 2 * PH, L)
        keys_sb, at = region(at, 2 * PH, NKEY)
        cand, at = region(at, PH, PK * PK)
        onehot, at = region(at, NSEL, PK)
        assert at <= 16384
        gates = arena[:, :].rearrange("p (i t) -> p i t", t=P)

        ra = [scr[:, b * W:(b + 1) * W] for b in range(NB)]
        rb = [scr[:, 1024 + b * W:1024 + (b + 1) * W] for b in range(NB)]
        rt = [scr[:, 2048 + b * W:2048 + (b + 1) * W] for b in range(NB)]
        masked = [scr[:, i * L:(i + 1) * L] for i in range(2)]
        probs = [scr[:, 512 + i * L:512 + (i + 1) * L] for i in range(4)]
        probs_t = [scr[:, 1536 + i * L:1536 + (i + 1) * L] for i in range(2)]
        relu = [scr[:, 2048 + i * L:2048 + (i + 1) * L] for i in range(2)]
        iscore = [scr[:, 2560 + b * L:2560 + (b + 1) * L] for b in range(NB)]
        iwork = [scr[:, 3072 + b * L:3072 + (b + 1) * L] for b in range(NB)]
        bias_dsa = [scr[:, 3584 + b * L:3584 + (b + 1) * L] for b in range(NB)]
        key_s = [scr[:, b * 2048:(b + 1) * 2048].rearrange("p (a n) -> p a n", n=NKEY) for b in range(NB)]
        TG = 8
        oh1 = [scr[:, i * 1024:(i + 1) * 1024].rearrange("p (t n) -> p t n", n=NKEY) for i in range(2)]
        oh2 = [scr[:, 2048 + i * 1024:2048 + (i + 1) * 1024].rearrange("p (t n) -> p t n", n=NKEY)
               for i in range(2)]
        gelu_out = [scr[:, i * L:(i + 1) * L] for i in range(2)]
        gelu_in = [scr[:, 512 + i * L:512 + (i + 1) * L] for i in range(4)]
        gate_in = [scr[:, 1536 + i * L:1536 + (i + 1) * L] for i in range(4)]
        prod = [scr[:, 2560 + i * L:2560 + (i + 1) * L] for i in range(2)]

        bank = [ctx.enter_context(nc.psum_tensor(f"bank{i}", [P, W], F32)) for i in range(8)]

        first_sem = ctx.enter_context(nc.semaphore("setup_loaded"))
        sems = []

        def sem(name):
            s = ctx.enter_context(nc.semaphore(name))
            sems.append(s)
            return s

        raw_in = [sem(f"raw_in{i}") for i in range(NRAW)]
        hi_done, lo_done, tile_used = sem("hi_done"), sem("lo_done"), sem("tile_used")
        par_in, mask_in = sem("par_in"), sem("mask_in")
        turned, turn_hi, turn_lo = sem("turned"), sem("turn_hi"), sem("turn_lo")
        group_done, rope_parts, rope_evac = sem("group_done"), sem("rope_parts"), sem("rope_evac")
        roped, rope_turned, qk_stored, v_stored = sem("roped"), sem("rope_turned"), sem("qk_stored"), sem("v_stored")
        iscored, irelu, iacc, bias_ready = sem("iscored"), sem("irelu"), sem("iacc"), sem("bias_ready")
        scored, masked_done, nbias_done = sem("scored"), sem("masked_done"), sem("nbias_done")
        exp_done, sink_exp = sem("exp_done"), sem("sink_exp")
        mixed_probs, p_turned, p_stored = sem("mixed_probs"), sem("p_turned"), sem("p_stored")
        pv_done, head_out = sem("pv_done"), sem("head_out")
        rms_sum, rms_root, mixed_done = sem("rms_sum"), sem("rms_root"), sem("mixed_done")
        lam_sum, lam_exp = sem("lam_sum"), sem("lam_exp")
        out_group, out_evac = sem("out_group"), sem("out_evac")
        ln_in, ln_var, ln_root, ln_done = sem("ln_in"), sem("ln_var"), sem("ln_root"), sem("ln_done")
        keys_in, q_group, q_stored = sem("keys_in"), sem("q_group"), sem("q_stored")
        keyed, keys_stored = sem("keyed"), sem("keys_stored")
        gate_arg, gate_exp, routed = sem("gate_arg"), sem("gate_exp"), sem("routed")
        sel_turned, sel_stored = sem("sel_turned"), sem("sel_stored")
        oh1_done, oh2_done, gate_mm, gate_evac = sem("oh1_done"), sem("oh2_done"), sem("gate_mm"), sem("gate_evac")
        gates_out, cols_done = sem("gates_out"), sem("cols_done")
        gelu_done = sem("gelu_done")
        gelu_stored = [sem(f"gelu_stored{i}") for i in range(2)]
        gelu_got = [sem(f"gelu_got{i}") for i in range(4)]
        gate_got = [sem(f"gate_got{i}") for i in range(4)]
        prod_done, ah_done, al_done = sem("prod_done"), sem("ah_done"), sem("al_done")
        y_done = sem("y_done")
        x_out = sem("x_out")
        dve_step = sem("dve_step")

        with nc.Block() as block:
            @block.sync
            def _(sp):
                sp.dma_start(x[:], x_in).then_inc(first_sem, 16)
                sp.dma_start(ident[:], eye).then_inc(first_sem, 16)
                sp.dma_start(iota_k[:], iota.partition_broadcast(P)).then_inc(first_sem, 16)
                sp.wait_ge(first_sem, 48)

        with nc.Fori(0, DEPTH) as layer:
            def of_layer(t):
                s = t[bass.ds(layer, 1)]
                if len(t.shape) == 2:
                    return s
                names = [f"d{i}" for i in range(len(t.shape) - 1)]
                return s.rearrange(f"a {' '.join(names)} -> (a {names[0]}) {' '.join(names[1:])}")

            with nc.Block() as block:
                @block.sync
                def _(sp):
                    def load(src, n, i, j, first=False):
                        if not first:
                            sp.wait_ge(lo_done, n - NRAW + 1)
                        sp.dma_start(raw[j][:], src(i * NRAW + j)).then_inc(raw_in[j], 16)

                    def tiles(t):
                        def src(m):
                            return t[bass.ds(layer, 1), bass.ds(m, 1)].rearrange("a b p n -> (a b p) n")
                        return src

                    def stream(t, at, count, lo_i=0):
                        with sp.Fori(lo_i, count // NRAW) as i:
                            for j in range(NRAW):
                                load(tiles(t), i * NRAW + (at + j), i, j)

                    for j in range(NRAW):
                        load(tiles(w_in), j, 0, j, first=True)
                    sp.dma_start(sinks_b, sinks[bass.ds(layer, 1)].partition_broadcast(P)).then_inc(par_in, 16)
                    sp.dma_start(lamp_b, lamp[bass.ds(layer, 1)].partition_broadcast(P)).then_inc(par_in, 16)
                    sp.dma_start(subg_b, subg[bass.ds(layer, 1)].partition_broadcast(P)).then_inc(par_in, 16)
                    sp.dma_start(lay_b, layer_consts[bass.ds(layer, 1)].partition_broadcast(P)).then_inc(par_in, 16)
                    sp.dma_start(trig.rearrange("p a b c -> p (a b c)"), rope).then_inc(par_in, 16)
                    sp.dma_start(bias_causal, masks[0]).then_inc(mask_in, 16)
                    sp.dma_start(bias_swa, masks[1]).then_inc(mask_in, 16)
                    sp.dma_start(bias_dil, masks[2]).then_inc(mask_in, 16)
                    sp.dma_start(count_dil, masks[3]).then_inc(mask_in, 16)
                    stream(w_in, AT_IN, N_IN, 1)
                    stream(w_out, AT_OUT, N_OUT)
                    sp.wait_ge(turn_lo, 16)
                    sp.dma_start(ln_gb, ln[bass.ds(layer, 1), 0:1].rearrange("a b c n -> (a b) (c n)").partition_broadcast(P)
                                 ).then_inc(ln_in, 16)
                    sp.dma_start(keys_sb, of_layer(keys)).then_inc(keys_in, 16)
                    stream(wq, AT_WQ, N_WQ)
                    stream_first = NRAW
                    for j in range(stream_first):
                        load(tiles(u_t), AT_U + j, 0, j)
                    for b in range(NB):
                        sp.wait_ge(gate_evac, (b + 1) * (P // TG))
                        for q in range(4):
                            sp.dma_start(a_dram[q * 32:(q + 1) * 32, :, b * P:(b + 1) * P].rearrange("i p t -> p i t"),
                                         gates[:, q * 32:(q + 1) * 32, :]).then_inc(gates_out, 16)
                    stream(u_t, AT_U, N_U, 1)
                    for j in range(NRAW):
                        load(tiles(v_t), AT_V + j, 0, j)
                    sp.wait_ge(gates_out, 16 * 4 * NB)
                    sp.dma_start(ln_gb, ln[bass.ds(layer, 1), 1:2].rearrange("a b c n -> (a b) (c n)").partition_broadcast(P)
                                 ).then_inc(ln_in, 16)
                    for s in gelu_stored:
                        sp.wait_ge(s, 16 * (N_U // 2))

                    def side(m, j, first=False):
                        if not first:
                            sp.wait_ge(prod_done, m - 3)
                        sp.dma_start(gelu_in[j], g_dram[bass.ds(m, 1)].rearrange("a p t -> (a p) t")).then_inc(gelu_got[j], 16)
                        sp.dma_start(gate_in[j], a_dram[bass.ds(m, 1)].rearrange("a p t -> (a p) t")).then_inc(gate_got[j], 16)

                    for j in range(NRAW):
                        side(j, j, first=True)
                    with sp.Fori(1, N_V // NRAW) as i:
                        for j in range(NRAW):
                            side(i * NRAW + j, j)
                            load(tiles(v_t), i * NRAW + (AT_V + j), i, j)
                    sp.wait_ge(ln_done, 2 * NB)
                    sp.dma_start(out, x[:]).then_inc(x_out, 16)
                    sp.wait_ge(x_out, 16)

                @block.tensor
                def _(pe):
                    def turn(r, src):
                        for k in range(DC // 2):
                            n = r * (DC // 2) + k
                            if n >= 2:
                                pe.wait_ge(turn_lo, n - 1)
                            for c in (2 * k, 2 * k + 1):
                                for b in range(NB):
                                    last = pe.transpose(bank[6 + k % 2][:, (c % 2) * L + b * P:(c % 2) * L + (b + 1) * P],
                                                        src[:, b, c * P:(c + 1) * P], ident[:])
                            last.then_inc(turned, 1)

                    def tokens_by_tile(n, j, kc, banks, first_c, last_c):
                        pe.wait_ge(lo_done, n + 1)
                        for c4 in range(KC):
                            c = kc * KC + c4
                            for b in range(NB):
                                st_h, st_l = xh[:, c, b * P:(b + 1) * P], xl[:, c, b * P:(b + 1) * P]
                                mh = hi[j % 2][:, c4 * W:(c4 + 1) * W]
                                ml = lo[j % 2][:, c4 * W:(c4 + 1) * W]
                                pe.matmul(banks[b][:], st_h, mh, start=(c == first_c), stop=False)
                                pe.matmul(banks[b][:], st_h, ml, start=False, stop=False)
                                last = pe.matmul(banks[b][:], st_l, mh, start=False, stop=(c == last_c))
                        last.then_inc(tile_used, 1)

                    def turn_rope(g, b):
                        pe.wait_ge(roped, g * NB + (b + 1))
                        if b_free_known(g):
                            pe.wait_ge(qk_stored, g * NB + (b + 1 - NB))
                        for j in range(4):
                            last = pe.transpose(bank[4 + b][:, j * P:(j + 1) * P], rt[b][:, j * P:(j + 1) * P], ident[:])
                        last.then_inc(rope_turned, 1)

                    def b_free_known(g):
                        return not (isinstance(g, int) and g == 0)

                    def in_group(g, par_, prev, free=True):
                        banks = [bank[2 * par_], bank[2 * par_ + 1]]
                        if free:
                            pe.wait_ge(rope_evac, g * NB - NB)
                        for kc in range(TPG):
                            tokens_by_tile(g * TPG + (AT_IN + kc), kc, kc, banks, 0, DC - 1)
                            if prev is not None and kc in (1, 2):
                                turn_rope(prev, kc - 1)

                    turn(0, x)
                    pe.wait_ge(turn_lo, 8)
                    in_group(0, 0, None, free=False)
                    in_group(1, 1, 0, free=False)
                    with pe.Fori(1, 4) as i:
                        in_group(i * 2, 0, i * 2 - 1)
                        in_group(i * 2 + 1, 1, i * 2)
                    in_group(8, 0, 7)
                    in_group(9, 1, None)

                    pe.wait_ge(qk_stored, 8 * NB)
                    k = 0
                    for b in range(NB):
                        K = (b + 1) * P
                        for h in range(8):
                            rows = slice(HD * (h % 2), HD * (h % 2) + HD)
                            if k >= 2:
                                pe.wait_ge(irelu, k - 1)
                            pe.matmul(bank[6 + k % 2][:, 0:K], qk_t[rows, PAIR["iq"] + h // 2, b * P:(b + 1) * P],
                                      qk_t[rows, PAIR["ik"], 0:K], start=True, stop=True).then_inc(iscored, 1)
                            k += 1

                    def scores(u):
                        kind, h, b, items = UNITS[u]
                        K = (b + 1) * P
                        for part, n in enumerate(items):
                            qp, kp, half = score_operands(kind, h, part)
                            rows = slice(HD * half, HD * half + HD)
                            if n >= 4:
                                pe.wait_ge(masked_done, n - 3)
                            pe.matmul(bank[n % 4][:, 0:K], qk_t[rows, qp, b * P:(b + 1) * P], qk_t[rows, kp, 0:K],
                                      start=True, stop=True).then_inc(scored, 1)

                    def turn_probs(u):
                        kind, h, b, items = UNITS[u]
                        if kind in "AD":
                            pe.wait_ge(exp_done, items[-1] + 1)
                        else:
                            pe.wait_ge(mixed_probs, n_mixed(u))
                        if u >= 2:
                            pe.wait_ge(p_stored, u - 1)
                        for kb in range(b + 1):
                            last = pe.transpose(bank[4 + u % 2][:, kb * P:(kb + 1) * P],
                                                probs[items[0] % 4][:, kb * P:(kb + 1) * P], ident[:])
                        last.then_inc(p_turned, 1)

                    def values(u):
                        kind, h, b, items = UNITS[u]
                        pe.wait_ge(p_stored, u + 1)
                        if u >= 2:
                            pe.wait_ge(head_out, u - 1)
                        at, width = value_columns(kind, h)
                        for kb in range(b + 1):
                            last = pe.matmul(bank[6 + u % 2][:, 0:width], probs_t[u % 2][:, kb * P:(kb + 1) * P],
                                             vals[:, kb, at:at + width], start=(kb == 0), stop=(kb == b))
                        last.then_inc(pv_done, 1)

                    def n_mixed(u):
                        return sum(UNITS[i][0] in "BC" for i in range(u + 1))

                    def value_columns(kind, h):
                        return {"A": (V_A + HD * (h // 4), HD), "B": (V_B + 2 * HD * h, 2 * HD),
                                "C": (V_C + HD * h, HD), "D": (V_D, HD)}[kind]

                    pe.wait_ge(v_stored, 2 * NB)
                    pe.wait_ge(rope_evac, 8 * NB)
                    pe.wait_ge(irelu, 16)
                    scores(0)
                    scores(1)
                    for u in range(n_units + 1):
                        if u + 2 < n_units:
                            scores(u + 2)
                        if u < n_units:
                            turn_probs(u)
                        if u >= 1:
                            values(u - 1)

                    pe.wait_ge(mixed_done, 1)
                    turn(1, mixed)
                    pe.wait_ge(turn_lo, 16)
                    for g in range(D // W):
                        if g >= 2:
                            pe.wait_ge(out_evac, NB * (g - 1))
                        for kc in range(TPG):
                            tokens_by_tile(AT_OUT + g * TPG + kc, kc, kc, [bank[2 * (g % 2)], bank[2 * (g % 2) + 1]], 0, DC - 1)

                    pe.wait_ge(ln_done, NB)
                    turn(2, x)
                    pe.wait_ge(turn_lo, 24)
                    for g in range(D // W):
                        if g >= 2:
                            pe.wait_ge(q_stored, 4 * (g - 1))
                        for kc in range(TPG):
                            pe.wait_ge(lo_done, AT_WQ + g * TPG + kc + 1)
                            for j in range(4):
                                q_bank = bank[4 * (g % 2) + j][:, 0:L]
                                for c4 in range(KC):
                                    c = kc * KC + c4
                                    at = c4 * W + j * P
                                    wh, wl = hi[kc % 2][:, at:at + P], lo[kc % 2][:, at:at + P]
                                    pe.matmul(q_bank, wh, xh[:, c, :], start=(c == 0), stop=False)
                                    pe.matmul(q_bank, wh, xl[:, c, :], start=False, stop=False)
                                    last = pe.matmul(q_bank, wl, xh[:, c, :], start=False, stop=(c == DC - 1))
                            last.then_inc(tile_used, 1)

                    pe.wait_ge(keys_in, 16)
                    pe.wait_ge(q_stored, 16)
                    for b in range(NB):
                        for k in range(4):
                            for j in range(4):
                                last = pe.matmul(bank[4 * b + k][:, j * P:(j + 1) * P], q_t[:, 4 * k + j, b * P:(b + 1) * P],
                                                 keys_sb[:, 4 * k + j, :], start=True, stop=True)
                            last.then_inc(keyed, 1)

                    pe.wait_ge(routed, NB)
                    for s in range(3):
                        for b in range(NB):
                            last = pe.transpose(bank[s][:, b * P:(b + 1) * P], sel[:, s, b, :], ident[:])
                        last.then_inc(sel_turned, 1)

                    def gate_step(s, p, first):
                        pe.wait_ge(oh1_done, s + 1)
                        pe.wait_ge(oh2_done, s + 1)
                        if not first:
                            pe.wait_ge(gate_evac, s - 1)
                        for t in range(TG):
                            last = pe.matmul(bank[4 + 2 * p + t // 4][:, (t % 4) * P:(t % 4 + 1) * P], oh1[p][:, t, :],
                                             oh2[p][:, t, :], start=True, stop=True)
                        last.then_inc(gate_mm, 1)

                    gate_step(0, 0, True)
                    gate_step(1, 1, True)
                    with pe.Fori(1, L // TG // 2) as i:
                        gate_step(i * 2, 0, False)
                        gate_step(i * 2 + 1, 1, False)

                    def hidden(n, m, j, first=False):
                        pe.wait_ge(lo_done, n + 1)
                        if not first:
                            pe.wait_ge(gelu_done, m - 1)
                        h = bank[j % 2][:, 0:L]
                        for c in range(DC):
                            wh, wl = hi[j % 2][:, c * P:(c + 1) * P], lo[j % 2][:, c * P:(c + 1) * P]
                            pe.matmul(h, wh, xh[:, c, :], start=(c == 0), stop=False)
                            pe.matmul(h, wh, xl[:, c, :], start=False, stop=False)
                            last = pe.matmul(h, wl, xh[:, c, :], start=False, stop=(c == DC - 1))
                        last.then_inc(tile_used, 1)

                    for j in range(2):
                        hidden(AT_U + j, j, j, first=True)
                    for j in range(2, NRAW):
                        hidden(AT_U + j, j, j)
                    with pe.Fori(1, N_U // NRAW) as i:
                        for j in range(NRAW):
                            hidden(i * NRAW + (AT_U + j), i * NRAW + j, j)

                    def gather(m, j, start=False, stop=False):
                        pe.wait_ge(al_done, m + 1)
                        for b in range(NB):
                            a_h, a_l = ah[j % 2][:, b * P:(b + 1) * P], al[j % 2][:, b * P:(b + 1) * P]
                            for q in range(4):
                                y = bank[4 * b + q][:]
                                vh, vl = hi[j % 2][:, q * W:(q + 1) * W], lo[j % 2][:, q * W:(q + 1) * W]
                                pe.matmul(y, a_h, vh, start=start, stop=False)
                                pe.matmul(y, a_h, vl, start=False, stop=False)
                                last = pe.matmul(y, a_l, vh, start=False, stop=stop)
                        last.then_inc(tile_used, 1)

                    pe.wait_ge(gelu_done, N_U)
                    for j in range(NRAW):
                        gather(j, j, start=(j == 0))
                    with pe.Fori(1, N_V // NRAW - 1) as i:
                        for j in range(NRAW):
                            gather(i * NRAW + j, j)
                    for j in range(NRAW):
                        gather(N_V - NRAW + j, j, stop=(j == NRAW - 1))

                @block.scalar
                def _(act):
                    def split_hi(n, i, j, at=0, first=False):
                        act.wait_ge(raw_in[j], i * 16 + 16)
                        if not first:
                            act.wait_ge(tile_used, n - 1)
                        act.activation(hi[j % 2][:], raw[j][:], ACT.Copy).then_inc(hi_done, 1)

                    def turn_high(r):
                        for k in range(DC // 2):
                            act.wait_ge(turned, r * (DC // 2) + k + 1)
                            act.activation(xh[:, 2 * k:2 * k + 2, :].rearrange("p a b -> p (a b)"), bank[6 + k % 2][:],
                                           ACT.Copy).then_inc(turn_hi, 1)

                    def store_qk(g, b):
                        act.wait_ge(rope_turned, NB * g + b + 1)
                        act.activation(qk_t[:, 4 * g:4 * g + 4, b * P:(b + 1) * P],
                                       bank[4 + b][:].rearrange("p (a b) -> p a b", a=4), ACT.Copy).then_inc(qk_stored, 1)

                    def store_v(g, at):
                        act.wait_ge(tile_used, AT_IN + TPG * (g + 1))
                        for b in range(NB):
                            act.activation(vals[:, b, at:at + W], bank[2 * (g % 2) + b][:], ACT.Copy).then_inc(v_stored, 1)

                    def store_q_group(g):
                        act.wait_ge(tile_used, AT_WQ + TPG * (g + 1))
                        for j in range(4):
                            act.activation(q_t[:, 4 * g + j, :], bank[4 * (g % 2) + j][:, 0:L], ACT.Copy).then_inc(q_stored, 1)

                    split_hi(0, 0, 0, first=True)
                    split_hi(1, 0, 1, first=True)
                    turn_high(0)
                    for g in range(NG_IN):
                        for kc in range(TPG):
                            if g or kc >= 2:
                                split_hi(AT_IN + g * TPG + kc, g, kc)
                            if 1 <= g <= 8 and kc >= 2:
                                store_qk(g - 1, kc - 2)
                            if g == 9 and kc == 2:
                                store_v(8, V_B)
                    for j in range(2):
                        split_hi(AT_OUT + j, AT_OUT // NRAW, j)
                    store_v(9, V_C)

                    act.wait_ge(lam_sum, 2)
                    act.activation(small[:, 2:4], small[:, 0:2], ACT.Exp).then_inc(lam_exp, 1)
                    k = 0
                    for b in range(NB):
                        K = (b + 1) * P
                        for h in range(8):
                            act.wait_ge(iscored, k + 1)
                            if k >= 2:
                                act.wait_ge(iacc, k - 1)
                            act.activation(relu[k % 2][:, 0:K], bank[6 + k % 2][:, 0:K], ACT.Relu).then_inc(irelu, 1)
                            k += 1

                    def exps(u):
                        kind, h, b, items = UNITS[u]
                        K = (b + 1) * P
                        for n in items:
                            act.wait_ge(nbias_done, n + 1)
                            if n >= 4:
                                act.wait_ge(p_turned, unit_of(n - 4) + 1)
                            act.activation(probs[n % 4][:, 0:K], masked[n % 2][:, 0:K], ACT.Exp, bias=st[:, 1, n:n + 1],
                                           scale=SCALE, accum_out=st[:, 2, n:n + 1]).then_inc(exp_done, 1)
                            if kind == "A":
                                act.activation(small[:, 16 + n:17 + n], sinks_b[:, h:h + 1], ACT.Exp,
                                               bias=st[:, 1, n:n + 1]).then_inc(sink_exp, 1)

                    def unit_of(n):
                        return next(i for i, w in enumerate(UNITS) if n in w[3])

                    exps(0)
                    for u in range(n_units):
                        if u + 1 < n_units:
                            exps(u + 1)
                        K = (UNITS[u][2] + 1) * P
                        act.wait_ge(p_turned, u + 1)
                        if u >= 2:
                            act.wait_ge(pv_done, u - 1)
                        act.activation(probs_t[u % 2][:, 0:K], bank[4 + u % 2][:, 0:K], ACT.Copy).then_inc(p_stored, 1)
                    act.wait_ge(rms_sum, 8)
                    act.activation(small[:, 48:56], small[:, 40:48], ACT.Sqrt, bias=lay_b[:, 2:3],
                                   scale=1.0 / (2 * HD)).then_inc(rms_root, 1)
                    turn_high(1)
                    for m in range(2, N_OUT):
                        split_hi(AT_OUT + m, (AT_OUT + m) // NRAW, m % NRAW)
                    for m in range(2):
                        split_hi(AT_WQ + m, AT_WQ // NRAW, m)

                    def root(k):
                        act.wait_ge(ln_var, k + 1)
                        act.activation(stats[:, 26:27], stats[:, 25:26], ACT.Sqrt, bias=lay_b[:, 2:3]).then_inc(ln_root, 1)

                    for b in range(NB):
                        root(b)
                    turn_high(2)
                    for m in range(2, N_WQ):
                        split_hi(AT_WQ + m, (AT_WQ + m) // NRAW, m % NRAW)
                        if m >= 4 and m % 4 == 1:
                            store_q_group(m // 4 - 1)
                    for m in range(2):
                        split_hi(AT_U + m, AT_U // NRAW, m)
                    store_q_group(3)
                    for k in range(8):
                        act.wait_ge(keyed, k + 1)
                        act.activation(key_s[k // 4][:, 4 * (k % 4):4 * (k % 4) + 4, :],
                                       bank[k][:].rearrange("p (a n) -> p a n", a=4), ACT.Copy).then_inc(keys_stored, 1)
                    for b in range(NB):
                        act.wait_ge(gate_arg, b + 1)
                        act.activation(sel[:, 2, b, :], sel[:, 2, b, :], ACT.Exp).then_inc(gate_exp, 1)
                    for s in range(3):
                        act.wait_ge(sel_turned, s + 1)
                        act.activation(sel_t[:, s, :], bank[s][:, 0:L], ACT.Copy).then_inc(sel_stored, 1)

                    for b in range(NB):
                        with act.Fori(0, P // TG // 2) as i:
                            for p in range(2):
                                s = i * 2 + (b * (P // TG) + p)
                                act.wait_ge(gate_mm, s + 1)
                                if b:
                                    act.wait_ge(gates_out, 16 * 4)
                                else:
                                    act.wait_ge(routed, NB)
                                view = gates.rearrange("p i t -> p t i")
                                for q in range(2):
                                    last = act.activation(view[:, bass.ds(i * (2 * TG) + (p * TG + q * 4), 4), :],
                                                          bank[4 + 2 * p + q][:].rearrange("p (t i) -> p t i", t=4), ACT.Copy)
                                last.then_inc(gate_evac, 1)

                    def gelu(m, rounds, j, first=False):
                        act.wait_ge(tile_used, m + (AT_U + 1))
                        if not first:
                            act.wait_ge(gelu_stored[j % 2], rounds * 16)
                        act.activation(gelu_out[j % 2], bank[j % 2][:, 0:L], ACT.Gelu).then_inc(gelu_done, 1)
                        act.wait_ge(gelu_done, m + 1)
                        act.dma_start(g_dram[bass.ds(m, 1)].rearrange("a p t -> (a p) t"), gelu_out[j % 2]).then_inc(gelu_stored[j % 2], 16)

                    gelu(0, 0, 0, first=True)
                    split_hi(AT_U + 2, AT_U // NRAW, 2)
                    gelu(1, 0, 1, first=True)
                    split_hi(AT_U + 3, AT_U // NRAW, 3)
                    with act.Fori(1, N_U // NRAW) as i:
                        for j in range(NRAW):
                            gelu(i * NRAW + (j - 2), i * 2 + (j - 2) // 2, (j - 2) % NRAW)
                            split_hi(i * NRAW + (AT_U + j), i + AT_U // NRAW, j)
                    for j in range(2):
                        gelu(N_U - 2 + j, N_U // 2 - 1, 2 + j)
                        split_hi(AT_V + j, AT_V // NRAW, j)

                    def a_high(m, j):
                        act.wait_ge(prod_done, m + 1)
                        act.activation(ah[j % 2][:], prod[j % 2], ACT.Copy).then_inc(ah_done, 1)

                    a_high(0, 0)
                    a_high(1, 1)
                    for j in range(2, NRAW):
                        split_hi(AT_V + j, AT_V // NRAW, j)
                        a_high(j, j)
                    with act.Fori(1, N_V // NRAW) as i:
                        for j in range(NRAW):
                            split_hi(i * NRAW + (AT_V + j), i + AT_V // NRAW, j)
                            a_high(i * NRAW + j, j)
                    for b in range(NB):
                        root(NB + b)

                @block.gpsimd
                def _(pool):
                    for g in range(8):
                        for b in range(NB):
                            pool.wait_ge(rope_parts, NB * g + b + 1)
                            if g:
                                pool.wait_ge(rope_turned, NB * (g - 1) + b + 1)
                            if g < G_MIX:
                                pool.tensor_tensor(rt[b], ra[b], rb[b], ALU.add).then_inc(roped, 1)
                            else:
                                dup = rt[b].rearrange("p (h r e) -> p h r e", r=2, e=HD)
                                a4 = ra[b][:, 0:4 * HD].rearrange("p (h e) -> p h e", e=HD)
                                b4 = rb[b][:, 0:4 * HD].rearrange("p (h e) -> p h e", e=HD)
                                pool.tensor_tensor(dup[:, :, 0, :], a4, b4, ALU.add)
                                pool.tensor_tensor(dup[:, :, 1, :], a4, b4, ALU.add).then_inc(roped, 1)

                    def first_keys(s, p, first):
                        if not first:
                            pool.wait_ge(gate_mm, s - 1)
                        pool.wait_ge(sel_stored, 3)
                        pool.tensor_copy(key_cols[p], sel_t[:, 0, bass.ds(s * TG, TG)]).then_inc(cols_done, 1)
                        pool.wait_ge(sel_stored, 3)
                        pool.wait_ge(cols_done, 1)
                        for t in range(TG):
                            last = pool.tensor_scalar(oh1[p][:, t, :], iota_k[:], key_cols[p][:, t:t + 1], None, ALU.is_equal)
                        last.then_inc(oh1_done, 1)
                        pool.sem_clear(cols_done)

                    first_keys(0, 0, True)
                    first_keys(1, 1, True)
                    with pool.Fori(1, L // TG // 2) as i:
                        first_keys(i * 2, 0, False)
                        first_keys(i * 2 + 1, 1, False)

                @block.vector
                def _(dve):
                    step = [0]

                    def mark(ins):
                        step[0] += 1
                        ins.then_inc(dve_step, 1)
                        return step[0]

                    def own(n):
                        dve.wait_ge(dve_step, n)

                    def split_lo(n, j):
                        dve.wait_ge(hi_done, n + 1)
                        dve.tensor_tensor(lo[j % 2][:], raw[j][:], hi[j % 2][:].bitcast(F32), ALU.subtract).then_inc(lo_done, 1)

                    def turn_low(r):
                        for k in range(DC // 2):
                            dve.wait_ge(turn_hi, r * (DC // 2) + k + 1)
                            two = slice(2 * k, 2 * k + 2)
                            dve.tensor_tensor(xl[:, two, :].rearrange("p a b -> p (a b)"), bank[6 + k % 2][:],
                                              xh[:, two, :].rearrange("p a b -> p (a b)").bitcast(F32),
                                              ALU.subtract).then_inc(turn_lo, 1)

                    def rotate(g, b, heads=8, first=False):
                        dve.wait_ge(tile_used, g * TPG + (AT_IN + TPG))
                        if not first:
                            dve.wait_ge(roped, g * NB + (b + 1 - NB))
                        src = bank[2 * parity(g) + b][:, 0:heads * HD].rearrange("p (h e) -> p h e", e=HD)
                        a = ra[b][:, 0:heads * HD].rearrange("p (h e) -> p h e", e=HD)
                        r = rb[b][:, 0:heads * HD].rearrange("p (h e) -> p h e", e=HD)
                        cos = trig[:, b, 0:1, :].to_broadcast([P, heads, HD])
                        sin = trig[:, b, 1:2, :].to_broadcast([P, heads, HD])
                        dve.tensor_tensor(a, src, cos, ALU.mult)
                        dve.tensor_tensor(r[:, :, 0:HALF], src[:, :, HALF:HD], sin[:, :, 0:HALF], ALU.mult)
                        return dve.tensor_tensor(r[:, :, HALF:HD], src[:, :, 0:HALF], sin[:, :, HALF:HD], ALU.mult
                                                 ).then_inc(rope_parts, 1)

                    def parity(g):
                        return g % 2 if isinstance(g, int) else g.par

                    split_lo(0, 0)
                    split_lo(1, 1)
                    turn_low(0)
                    dve.wait_ge(par_in, 16 * 5)
                    mark(dve.tensor_tensor_reduce(out=lamp_b[:, 0:HD], in0=lamp_b[:, 0:HD], in1=lamp_b[:, HD:2 * HD], scale=1.0,
                                                  scalar=0.0, op0=ALU.mult, op1=ALU.add, accum_out=small[:, 0:1]))
                    dve.tensor_tensor_reduce(out=lamp_b[:, 2 * HD:3 * HD], in0=lamp_b[:, 2 * HD:3 * HD], in1=lamp_b[:, 3 * HD:4 * HD],
                                             scale=1.0, scalar=0.0, op0=ALU.mult, op1=ALU.add,
                                             accum_out=small[:, 1:2]).then_inc(lam_sum, 2)
                    for g in range(NG_IN):
                        for kc in range(TPG):
                            if g or kc >= 2:
                                split_lo(AT_IN + g * TPG + kc, kc)
                            if 1 <= g <= 8 and kc in (1, 2):
                                pg, b = g - 1, kc - 1
                                rotate(pg, b, heads=8 if pg < G_MIX else 4, first=pg == 0)
                                if pg < G_MIX:
                                    dve.wait_ge(rope_parts, NB * pg + b + 1)
                                    dve.sem_inc(rope_evac, 1)
                                else:
                                    dve.tensor_copy(vals[:, b, 0:V_B], bank[2 * (pg % 2) + b][:, 4 * HD:4 * HD + V_B]
                                                    ).then_inc(rope_evac, 1)
                    for j in range(2):
                        split_lo(AT_OUT + j, j)

                    dve.wait_ge(lam_exp, 1)
                    n = mark(dve.tensor_tensor(small[:, 4:5], small[:, 2:3], small[:, 3:4], ALU.subtract))
                    own(n)
                    n = mark(dve.tensor_tensor(small[:, 5:6], small[:, 4:5], lay_b[:, 0:1], ALU.add))
                    dve.wait_ge(rope_evac, 8 * NB)
                    for b in range(NB):
                        n = mark(dve.tensor_scalar(small[:, 56:64] if b else small[:, 6:14], vals[:, b, V_IW:V_IW + 8],
                                                   8 ** -0.5 * SCALE, None, ALU.mult))
                    own(n)
                    n = mark(dve.tensor_scalar(small[:, 5:6], small[:, 5:6], -1.0, None, ALU.mult))
                    neg_lam = small[:, 5:6]
                    own(n)
                    n = mark(dve.tensor_scalar(subg_b, subg_b, lay_b[:, 1:2], None, ALU.mult))
                    own(n)

                    dve.wait_ge(mask_in, 16 * 4)
                    k = 0
                    for b in range(NB):
                        K = (b + 1) * P
                        causal = bias_causal[:, L - K:L]
                        iw = small[:, 56:64] if b else small[:, 6:14]
                        for h in range(8):
                            dve.wait_ge(irelu, k + 1)
                            if h:
                                dve.wait_ge(iacc, k)
                            dve.scalar_tensor_tensor(out=iscore[b][:, 0:K], in0=relu[k % 2][:, 0:K], scalar=iw[:, h:h + 1],
                                                     in1=causal if h == 0 else iscore[b][:, 0:K], op0=ALU.mult,
                                                     op1=ALU.add).then_inc(iacc, 1)
                            k += 1
                    for b in range(NB):
                        K = (b + 1) * P
                        dve.wait_ge(iacc, 8 * (b + 1))
                        for r in range(TOPK // 8):
                            n = mark(dve.max(out=small[:, 24:32], in_=iscore[b][:, 0:K]))
                            own(n)
                            n = mark(dve.match_replace(out=iscore[b][:, 0:K], in_to_replace=small[:, 24:32],
                                                       in_values=iscore[b][:, 0:K], imm_value=TAKEN))
                            own(n)
                        n = mark(dve.tensor_scalar(iwork[b][:, 0:K], iscore[b][:, 0:K], TAKEN / 2, NEG, ALU.is_gt, ALU.mult))
                        own(n)
                        n = mark(dve.tensor_tensor(bias_dsa[b][:, 0:K], iwork[b][:, 0:K], bias_causal[:, L - K:L], ALU.add))
                        own(n)
                    n = mark(dve.tensor_scalar(small[:, 32:40], sinks_b, 1.0 / SCALE, None, ALU.mult))
                    own(n)

                    def row_max(u):
                        kind, h, b, items = UNITS[u]
                        K = (b + 1) * P
                        for i in items:
                            dve.wait_ge(scored, i + 1)
                            if i >= 2:
                                dve.wait_ge(exp_done, i - 1)
                            bias = {"A": bias_swa, "B": bias_causal, "C": bias_dil}.get(kind)
                            bias = bias_dsa[b][:, 0:K] if bias is None else bias[:, L - K:L]
                            dve.tensor_tensor_reduce(out=masked[i % 2][:, 0:K], in0=bank[i % 4][:, 0:K], in1=bias, scale=1.0,
                                                     scalar=small[:, 32 + h:33 + h] if kind == "A" else TAKEN,
                                                     op0=ALU.add, op1=ALU.max, accum_out=st[:, 0, i:i + 1]).then_inc(masked_done, 1)
                            dve.wait_ge(masked_done, i + 1)
                            dve.tensor_scalar(st[:, 1, i:i + 1], st[:, 0, i:i + 1], -SCALE, None, ALU.mult).then_inc(nbias_done, 1)

                    def finish_probs(u):
                        kind, h, b, items = UNITS[u]
                        K = (b + 1) * P
                        i = items[0]
                        dve.wait_ge(exp_done, items[-1] + 1)
                        if kind == "A":
                            dve.wait_ge(sink_exp, i + 1)
                            own(mark(dve.tensor_tensor(st[:, 2, i:i + 1], st[:, 2, i:i + 1], small[:, 16 + i:17 + i], ALU.add)))
                        if kind == "C":
                            dve.scalar_tensor_tensor(out=probs[i % 4][:, 0:K], in0=probs[i % 4][:, 0:K], scalar=1.0,
                                                     in1=count_dil[:, L - K:L], op0=ALU.mult, op1=ALU.mult,
                                                     accum_out=st[:, 2, i:i + 1]).then_inc(mixed_probs, 1)
                            dve.wait_ge(mixed_probs, n_mixed(u))
                        own(mark(dve.reciprocal(st[:, 3, i:i + len(items)], st[:, 2, i:i + len(items)])))
                        if kind == "B":
                            j = items[1]
                            own(mark(dve.tensor_scalar(probs[j % 4][:, 0:K], probs[j % 4][:, 0:K], st[:, 3, j:j + 1], neg_lam,
                                                       ALU.mult, ALU.mult)))
                            dve.scalar_tensor_tensor(out=probs[i % 4][:, 0:K], in0=probs[i % 4][:, 0:K], scalar=st[:, 3, i:i + 1],
                                                     in1=probs[j % 4][:, 0:K], op0=ALU.mult, op1=ALU.add).then_inc(mixed_probs, 1)

                    def n_mixed(u):
                        return sum(UNITS[i][0] in "BC" for i in range(u + 1))

                    def take_out(u):
                        kind, h, b, items = UNITS[u]
                        dve.wait_ge(pv_done, u + 1)
                        src = bank[6 + u % 2]
                        if kind == "B":
                            at = MIX_B + 2 * HD * h
                            dve.tensor_copy(mixed[:, b, at:at + 2 * HD], src[:, 0:2 * HD]).then_inc(head_out, 1)
                        else:
                            at = {"A": MIX_A, "C": MIX_C, "D": MIX_D}[kind] + HD * h
                            dve.tensor_scalar(mixed[:, b, at:at + HD], src[:, 0:HD], st[:, 3, items[0]:items[0] + 1], None,
                                              ALU.mult).then_inc(head_out, 1)

                    row_max(0)
                    for u in range(n_units + 1):
                        if u + 1 < n_units:
                            row_max(u + 1)
                        if u < n_units:
                            finish_probs(u)
                        if u >= 1:
                            take_out(u - 1)

                    dve.wait_ge(head_out, n_units)
                    for j in range(8):
                        h, b = j // 2, j % 2
                        at = MIX_B + 2 * HD * h
                        dve.tensor_tensor_reduce(out=relu[0][:, 0:2 * HD] if j % 2 else relu[1][:, 0:2 * HD], in0=mixed[:, b, at:at + 2 * HD],
                                                 in1=mixed[:, b, at:at + 2 * HD], scale=1.0, scalar=0.0, op0=ALU.mult, op1=ALU.add,
                                                 accum_out=small[:, 40 + j:41 + j]).then_inc(rms_sum, 1)
                        dve.wait_ge(rms_sum, j + 1)
                    dve.wait_ge(rms_root, 1)
                    own(mark(dve.reciprocal(small[:, 40:48], small[:, 48:56])))
                    for j in range(8):
                        h, b = j // 2, j % 2
                        at = MIX_B + 2 * HD * h
                        last = dve.scalar_tensor_tensor(out=mixed[:, b, at:at + 2 * HD], in0=mixed[:, b, at:at + 2 * HD],
                                                        scalar=small[:, 40 + j:41 + j], in1=subg_b, op0=ALU.mult, op1=ALU.mult)
                    last.then_inc(mixed_done, 1)
                    turn_low(1)

                    def take_out_group(g):
                        dve.wait_ge(tile_used, AT_OUT + TPG * (g + 1))
                        for b in range(NB):
                            cols = x[:, b, g * W:(g + 1) * W]
                            dve.scalar_tensor_tensor(out=cols, in0=cols, scalar=ALPHA, in1=bank[2 * (g % 2) + b][:], op0=ALU.mult,
                                                     op1=ALU.add).then_inc(out_evac, 1)

                    for m in range(2, N_OUT):
                        split_lo(AT_OUT + m, m % NRAW)
                        if m >= 4 and m % 4 == 1:
                            take_out_group(m // 4 - 1)
                    for m in range(2):
                        split_lo(AT_WQ + m, m)
                    take_out_group(3)
                    dve.wait_ge(out_evac, 8)

                    def layer_norm(k, b):
                        for q in range(D // W):
                            n = mark(dve.bn_stats(stats[:, 6 * q:6 * q + 6], x[:, b, q * W:(q + 1) * W]))
                        own(n)
                        dve.bn_aggr(stats[:, 24:26], stats[:, 0:24]).then_inc(ln_var, 1)
                        dve.wait_ge(ln_root, k * NB + b + 1)
                        own(mark(dve.reciprocal(stats[:, 27:28], stats[:, 26:27])))
                        own(mark(dve.tensor_scalar(x[:, b, :], x[:, b, :], stats[:, 24:25], stats[:, 27:28], ALU.subtract, ALU.mult)))
                        dve.wait_ge(ln_in, 16 * (k + 1))
                        own(mark(dve.tensor_tensor(x[:, b, :], x[:, b, :], ln_gb[:, 0, :], ALU.mult)))
                        dve.tensor_tensor(x[:, b, :], x[:, b, :], ln_gb[:, 1, :], ALU.add).then_inc(ln_done, 1)
                        dve.wait_ge(ln_done, k * NB + b + 1)

                    for b in range(NB):
                        layer_norm(0, b)
                    turn_low(2)
                    for m in range(2, N_WQ):
                        split_lo(AT_WQ + m, m % NRAW)
                    for m in range(2):
                        split_lo(AT_U + m, m)

                    def top16(scores_, v, idx):
                        own(mark(dve.max(out=v[:, 0:8], in_=scores_)))
                        own(mark(dve.max_index(out=idx[:, 0:8], in_max=v[:, 0:8], in_values=scores_)))
                        own(mark(dve.match_replace(out=scores_, in_to_replace=v[:, 0:8], in_values=scores_, imm_value=TAKEN)))
                        own(mark(dve.max(out=v[:, 8:16], in_=scores_)))
                        own(mark(dve.max_index(out=idx[:, 8:16], in_max=v[:, 8:16], in_values=scores_)))

                    for b in range(NB):
                        dve.wait_ge(keys_stored, 4 * (b + 1))
                        for s in range(2 * PH):
                            top16(key_s[b][:, s, :], top_v[:, s, :], top_i[:, s, :])
                        tv = top_v[:, :, :].rearrange("p (h s) k -> p h s k", s=2)
                        for h in range(PH):
                            n = mark(dve.tensor_tensor(cand[:, h, :].rearrange("p (a c) -> p a c", c=PK),
                                                       tv[:, h, 0, :].unsqueeze(2).to_broadcast([P, PK, PK]),
                                                       tv[:, h, 1, :].unsqueeze(1).to_broadcast([P, PK, PK]), ALU.add))
                        own(n)
                        num = key_s[b].rearrange("p a n -> p (a n)")
                        key_num = num[:, 0:2 * NSEL].rearrange("p (h s k) -> p h s k", s=2, k=PK)
                        own(mark(dve.tensor_copy(num[:, 0:2 * NSEL], top_i[:, :, :].rearrange("p a k -> p (a k)"))))
                        top_s = sel[:, 2, b, :].rearrange("p (h k) -> p h k", k=PK)
                        pos = top_i[:, 0:PH, :]
                        for h in range(PH):
                            top16(cand[:, h, :], top_s[:, h, :], pos[:, h, :])
                        flat = pos.rearrange("p h k -> p (h k)")
                        nib = top_i[:, PH:2 * PH, :].rearrange("p h k -> p (h k)")
                        for side_, (op, val) in enumerate(((ALU.logical_shift_right, 4), (ALU.bitwise_and, 15))):
                            own(mark(dve.tensor_scalar(nib, flat, val, None, op)))
                            own(mark(dve.tensor_copy(num[:, 512:512 + NSEL], nib)))
                            own(mark(dve.tensor_tensor(onehot, iota_k[:, 0:PK].unsqueeze(1).to_broadcast([P, NSEL, PK]),
                                                       num[:, 512:512 + NSEL].unsqueeze(2).to_broadcast([P, NSEL, PK]),
                                                       ALU.is_equal)))
                            oh4 = onehot.rearrange("p (h k) c -> p h k c", k=PK)
                            for h in range(PH):
                                n = mark(dve.tensor_tensor(oh4[:, h], oh4[:, h],
                                                           key_num[:, h, side_, :].unsqueeze(1).to_broadcast([P, PK, PK]), ALU.mult))
                            own(n)
                            own(mark(dve.reduce_sum(sel[:, side_, b, :], onehot, AX)))
                        own(mark(dve.tensor_copy(num[:, 640:640 + PH], top_s[:, :, 0])))
                        dve.tensor_tensor(top_s, top_s, num[:, 640:640 + PH].unsqueeze(2).to_broadcast([P, PH, PK]),
                                          ALU.subtract).then_inc(gate_arg, 1)
                        dve.wait_ge(gate_exp, b + 1)
                        own(mark(dve.reduce_sum(num[:, 648:648 + PH], top_s, AX)))
                        own(mark(dve.reciprocal(num[:, 656:656 + PH], num[:, 648:648 + PH])))
                        dve.tensor_tensor(top_s, top_s, num[:, 656:656 + PH].unsqueeze(2).to_broadcast([P, PH, PK]),
                                          ALU.mult).then_inc(routed, 1)

                    def second_keys(s, p, first):
                        if not first:
                            dve.wait_ge(gate_mm, s - 1)
                        for t in range(TG):
                            col = s * TG + t
                            last = dve.tensor_scalar(oh2[p][:, t, :], iota_k[:], sel_t[:, 1, bass.ds(col, 1)],
                                                     sel_t[:, 2, bass.ds(col, 1)], ALU.is_equal, ALU.mult)
                        last.then_inc(oh2_done, 1)

                    dve.wait_ge(sel_stored, 3)
                    second_keys(0, 0, True)
                    second_keys(1, 1, True)
                    with dve.Fori(1, L // TG // 2) as i:
                        second_keys(i * 2, 0, False)
                        second_keys(i * 2 + 1, 1, False)

                    for j in range(2, NRAW):
                        split_lo(AT_U + j, j)
                    with dve.Fori(1, N_U // NRAW) as i:
                        for j in range(NRAW):
                            split_lo(i * NRAW + (AT_U + j), j)

                    def product(m, i, j, first=False):
                        dve.wait_ge(gelu_got[j], i * 16 + 16)
                        dve.wait_ge(gate_got[j], i * 16 + 16)
                        if not first:
                            dve.wait_ge(al_done, m - 1)
                        dve.tensor_tensor(prod[j % 2], gelu_in[j], gate_in[j], ALU.mult).then_inc(prod_done, 1)

                    def a_low(m, j):
                        dve.wait_ge(ah_done, m + 1)
                        dve.tensor_tensor(al[j % 2][:], prod[j % 2], ah[j % 2][:].bitcast(F32), ALU.subtract).then_inc(al_done, 1)

                    for j in range(NRAW):
                        product(j, 0, j, first=j < 2)
                        split_lo(AT_V + j, j)
                        a_low(j, j)
                    with dve.Fori(1, N_V // NRAW) as i:
                        for j in range(NRAW):
                            product(i * NRAW + j, i, j)
                            split_lo(i * NRAW + (AT_V + j), j)
                            a_low(i * NRAW + j, j)
                    dve.wait_ge(tile_used, N_TILES)
                    for b in range(NB):
                        for q in range(4):
                            cols = x[:, b, q * W:(q + 1) * W]
                            n = mark(dve.scalar_tensor_tensor(out=cols, in0=cols, scalar=ALPHA, in1=bank[4 * b + q][:],
                                                              op0=ALU.mult, op1=ALU.add))
                    own(n)
                    for b in range(NB):
                        layer_norm(1, b)

            nc.all_engine_barrier()
            nc.gpsimd.sem_clear(range(sems[0].num, sems[-1].num + 1))
            nc.all_engine_barrier()


_SPLITS = (512, 128, 128, 512, 512, 512, 512, 512, 512, 512, 64, 64, 512, 64, 8)


def _masks():
    q, k = np.arange(P)[:, None] + P, np.arange(2 * P)[None, :]
    d = q - k
    causal = d >= 0
    count = (causal & (d <= 128)).astype(np.float32) + (causal & (d % 4 == 0)) + (causal & (d % 16 == 0))
    swa = causal & (d <= 127)
    return np.stack([np.where(causal, 0, NEG), np.where(swa, 0, NEG), np.where(count > 0, 0, NEG), count]).astype(np.float32)


def _rope():
    inv = (10000.0 ** (-np.arange(HALF, dtype=np.float32) / np.float32(HALF))).astype(np.float32)
    ang = np.arange(L, dtype=np.float32)[:, None] * inv[None, :]
    c, s = np.cos(ang).astype(np.float32), np.sin(ang).astype(np.float32)
    t = np.stack([np.concatenate([c, c], -1), np.concatenate([-s, s], -1)], 1)
    return np.ascontiguousarray(t.reshape(NB, P, 2, HD).transpose(1, 0, 2, 3).reshape(P, NB * 2 * HD))


def _row_tiles(w):
    n = w.shape[-1] // W
    t = w.reshape(DEPTH, TPG, KC, P, n, W).transpose(0, 4, 1, 3, 2, 5)
    return np.ascontiguousarray(t).reshape(DEPTH, n * TPG, P, KC * W)


def kernel(x, w_in, attn_sinks, diff_lambda, diff_norm_g, w_out, ln1_g, ln1_b, peer_wq, peer_keys, peer_u, peer_v,
           ln2_g, ln2_b):
    import concourse.bacc as bacc
    from concourse.bass_utils import run_bass_kernel_spmd

    x, w_in, w_out, peer_wq, peer_keys, peer_u, peer_v = (
        np.asarray(a) for a in (x, w_in, w_out, peer_wq, peer_keys, peer_u, peer_v))
    cuts = np.cumsum(_SPLITS)[:-1]
    aq, ak, av, bq, bk, bv, cq, ck, cv, dq, dk, dv, iq, ik, iw = np.split(w_in, cuts, axis=-1)
    pad = np.zeros((DEPTH, D, NG_IN * W - w_in.shape[-1]), np.float32)
    w_in_cols = np.concatenate([aq, bq, bk, cq, ck, dq, iq, ak, dk, ik, av, dv, iw, pad, bv, cv], -1)
    lam_init = [0.8 - 0.6 * math.exp(-0.3 * i) for i in range(DEPTH)]
    arrays = {
        "x_in": x.reshape(NB, P, D).transpose(1, 0, 2),
        "w_in": _row_tiles(w_in_cols),
        "w_out": _row_tiles(w_out),
        "wq": _row_tiles(peer_wq),
        "keys": peer_keys.reshape(DEPTH, 2 * PH, NKEY, P).transpose(0, 3, 1, 2),
        "u_t": peer_u.reshape(DEPTH, NKEY, NKEY, DC, P).transpose(0, 2, 4, 3, 1).reshape(DEPTH, NKEY, P, DC * NKEY),
        "v_t": peer_v.reshape(DEPTH, NKEY, NKEY, D).transpose(0, 2, 1, 3),
        "ln": np.stack([np.stack([ln1_g, ln1_b], 1), np.stack([ln2_g, ln2_b], 1)], 1),
        "sinks": np.asarray(attn_sinks),
        "lamp": np.asarray(diff_lambda).reshape(DEPTH, 4 * HD),
        "subg": np.asarray(diff_norm_g),
        "layer_consts": np.array([[v, 1.0 - v, EPS, 0.0] for v in lam_init], np.float32),
        "rope": _rope(),
        "masks": _masks(),
        "eye": np.eye(P, dtype=np.float32),
        "iota": np.arange(NKEY, dtype=np.float32)[None, :],
    }
    arrays = {k: np.ascontiguousarray(v) for k, v in arrays.items()}
    nc = bacc.Bacc("TRN2", target_bir_lowering=False, num_devices=1)
    aps = {k: nc.dram_tensor(k, v.shape, F32, kind="ExternalInput").ap() for k, v in arrays.items()}
    out = nc.dram_tensor("out", [P, NB, D], F32, kind="ExternalOutput").ap()
    build(nc, out=out, **aps)
    r = run_bass_kernel_spmd(nc, [arrays], core_ids=[0])
    got = r.results[0]["out"]
    return np.ascontiguousarray(np.asarray(got).reshape(P, NB, D).transpose(1, 0, 2)).reshape(1, L, D)
```

```python
from contextlib import ExitStack
import math

import numpy as np

import concourse.bass as bass
from concourse import mybir

F32 = mybir.dt.float32
F32R = mybir.dt.float32r
U32 = mybir.dt.uint32
ALU = mybir.AluOpType
ACT = mybir.ActivationFunctionType
AX = mybir.AxisListType.X

P = 128
DEPTH, D, L = 2, 2048, 256
NB = L // P
DC = D // P
W = 512
HD = 64
HALF = HD // 2
TILE = 2048
HT = TILE // 2
NRAW, NSPLIT = 4, 4
BODY = 2 * NRAW
ALPHA = (2 * DEPTH) ** 0.25
NEG = -1e30
TAKEN = -3e38
EPS = 1e-5
SCALE = HD ** -0.5
TOPK = min(256, L // 4)
PH, PK, NKEY = 8, 16, 128
NSEL = PH * PK
NE = NKEY * NKEY

G_AQ, G_BQ, G_BK, G_CQ, G_CK, G_DQ, G_IQ, G_MIX, G_BV, G_CV = range(10)
NG_IN = 10
KC = HT // W
HPG = DC // KC
NT = NE // P
N_IN, N_OUT, N_WQ, N_U, N_V = NG_IN * HPG, D // W * HPG, D // W * HPG, 2 * NT, 2 * NT
AT_IN = 0
AT_OUT = AT_IN + N_IN
AT_WQ = AT_OUT + N_OUT
AT_U = AT_WQ + N_WQ
AT_V = AT_U + N_U
N_HALVES = AT_V + N_V
PAIR = {"aq": 0, "bq": 4, "bk": 8, "cq": 12, "ck": 16, "dq": 20, "iq": 24, "ak": 28, "dk": 30, "ik": 31}
V_A, V_D, V_IW, V_B, V_C, V_END = 0, 128, 192, 200, 712, 1224
MIX_A, MIX_B, MIX_C, MIX_D = 0, 512, 1024, 1536


def units():
    out = []
    item = 0
    for kind, heads in (("A", 8), ("B", 4), ("C", 8), ("D", 8)):
        for h in range(heads):
            for b in range(NB):
                n = 2 if kind == "B" else 1
                out.append((kind, h, b, list(range(item, item + n))))
                item += n
    return out, item


def score_operands(kind, h, part):
    if kind == "A":
        return PAIR["aq"] + h // 2, PAIR["ak"] + h // 4, h % 2
    if kind == "B":
        return PAIR["bq"] + h, PAIR["bk"] + h, part
    if kind == "C":
        return PAIR["cq"] + h // 2, PAIR["ck"] + h // 2, h % 2
    return PAIR["dq"] + h // 2, PAIR["dk"], h % 2


def build(nc, x_in, w_in, w_out, wq, keys, u_t, v_t, ln, sinks, lamp, subg, layer_consts,
          rope, masks, eye, iota, out):
    UNITS, N_ITEMS = units()
    n_units = len(UNITS)
    a_dram = nc.dram_tensor("gates_scratch", [NKEY, P, P], F32, kind="Internal").ap()
    g_dram = nc.dram_tensor("gelu_scratch", [NKEY, P, L], F32, kind="Internal").ap()

    with ExitStack() as ctx:
        def sb(name, shape, dt=F32):
            return ctx.enter_context(nc.sbuf_tensor(name, shape, dt))

        x = sb("x", [P, NB, D])
        xh = sb("xh", [P, DC, L], F32R)
        xl = sb("xl", [P, DC, L], F32R)
        raw = [sb(f"raw{i}", [P, TILE]) for i in range(NRAW)]
        hi = [sb(f"hi{i}", [P, HT], F32R) for i in range(NSPLIT)]
        lo = [sb(f"lo{i}", [P, HT], F32R) for i in range(NSPLIT)]
        arena = sb("arena", [P, 16384])
        scr = sb("scr", [P, 4096])
        ident = sb("ident", [P, P])
        iota_k = sb("iota_k", [P, NKEY])
        par = sb("par", [P, 8 + 128 + 4])
        st = sb("st", [P, 4, N_ITEMS])
        small = sb("small", [P, 80])
        key_cols = [small[:, 64 + i * 4:68 + i * 4] for i in range(2)]
        stats = sb("stats", [P, NB, 4, 6])
        norm = sb("norm", [P, NB, 5])
        sel = sb("sel", [P, 3, NB, NSEL])
        sel_t = sb("sel_t", [P, 3, L])
        gelu_out = [sb(f"gelu_out{i}", [P, L]) for i in range(2)]
        key_now = sb("key_now", [P, 2, NKEY])
        cand = sb("cand", [P, PK * PK])
        top_v = sb("top_v", [P, 2, PK])
        top_i = sb("top_i", [P, 2, PK], U32)
        key_num = sb("key_num", [P, 2, PK])
        pos = sb("pos", [P, 2, PK], U32)
        pos_num = sb("pos_num", [P, PK])
        ah = [xh[:, i, :] for i in range(2)]
        al = [xl[:, i, :] for i in range(2)]

        sinks_b = par[:, 0:8]
        subg_b = par[:, 8:136]
        lay_b = par[:, 136:140]

        def region(base, *shape):
            n = int(np.prod(shape))
            v = arena[:, base:base + n]
            if len(shape) == 1:
                return v, base + n
            names = "abc"[:len(shape)]
            return v.rearrange(f"p ({' '.join(names)}) -> p {' '.join(names)}",
                               **{k: s for k, s in zip(names, shape)}), base + n

        qk_t, at = region(0, 32, L)
        vals, at = region(at, NB, V_END)
        mixed, at = region(at, NB, D)
        bias_causal, at = region(at, L)
        bias_swa, at = region(at, L)
        bias_dil, at = region(at, L)
        count_dil, at = region(at, L)
        trig, at = region(at, NB, 2, HD)
        lamp_b, at = region(at, 4 * HD)
        assert at <= 16384
        ln_gb, at = region(0, 2, D)
        q_t, at = region(at, 2 * PH, L)
        keys_sb, at = region(at, 2 * PH, NKEY)
        assert at <= 16384
        gates = arena[:, :].rearrange("p (i t) -> p i t", t=P)

        ra = [scr[:, b * W:(b + 1) * W] for b in range(NB)]
        rb = [scr[:, 1024 + b * W:1024 + (b + 1) * W] for b in range(NB)]
        rt = [scr[:, 2048 + b * W:2048 + (b + 1) * W] for b in range(NB)]
        masked = [scr[:, i * L:(i + 1) * L] for i in range(2)]
        probs = [scr[:, 512 + i * L:512 + (i + 1) * L] for i in range(4)]
        probs_t = [scr[:, 1536 + i * L:1536 + (i + 1) * L] for i in range(2)]
        relu = [scr[:, 2048 + i * L:2048 + (i + 1) * L] for i in range(2)]
        iscore = [scr[:, 2560 + b * L:2560 + (b + 1) * L] for b in range(NB)]
        iwork = [scr[:, 3072 + b * L:3072 + (b + 1) * L] for b in range(NB)]
        bias_dsa = [scr[:, 3584 + b * L:3584 + (b + 1) * L] for b in range(NB)]
        key_s = [scr[:, b * 2048:(b + 1) * 2048].rearrange("p (a n) -> p a n", n=NKEY) for b in range(NB)]
        TG = 4
        STEPS = P // TG
        quarter = N_U // BODY // 4
        assert quarter == PH and STEPS == quarter * NRAW
        PIECES = 16
        ROWS = NKEY // PIECES
        oh1 = [scr[:, i * 512:(i + 1) * 512].rearrange("p (t n) -> p t n", n=NKEY) for i in range(2)]
        oh2 = [scr[:, 1024 + i * 512:1024 + (i + 1) * 512].rearrange("p (t n) -> p t n", n=NKEY)
               for i in range(2)]
        gelu_in = [scr[:, 2048 + i * L:2048 + (i + 1) * L] for i in range(4)]
        gate_in = [scr[:, 3072 + i * P:3072 + (i + 1) * P] for i in range(4)]
        prod = [scr[:, 3584 + i * L:3584 + (i + 1) * L] for i in range(2)]

        bank = [ctx.enter_context(nc.psum_tensor(f"bank{i}", [P, W], F32)) for i in range(8)]

        first_sem = ctx.enter_context(nc.semaphore("setup_loaded"))
        first_in = [ctx.enter_context(nc.semaphore(f"first_in{i}")) for i in range(NRAW)]
        sems = []

        def sem(name):
            s = ctx.enter_context(nc.semaphore(name))
            sems.append(s)
            return s

        raw_in = [sem(f"raw_in{i}") for i in range(NRAW)]
        hi_done, lo_done, half_used = sem("hi_done"), sem("lo_done"), sem("half_used")
        par_in, mask_in = sem("par_in"), sem("mask_in")
        turned, turn_hi, turn_lo = sem("turned"), sem("turn_hi"), sem("turn_lo")
        group_done, rope_parts, rope_evac = sem("group_done"), sem("rope_parts"), sem("rope_evac")
        roped, rope_turned, qk_stored, v_stored = sem("roped"), sem("rope_turned"), sem("qk_stored"), sem("v_stored")
        iscored, irelu, iacc, bias_ready = sem("iscored"), sem("irelu"), sem("iacc"), sem("bias_ready")
        scored, masked_done, nbias_done = sem("scored"), sem("masked_done"), sem("nbias_done")
        exp_done, sink_exp = sem("exp_done"), sem("sink_exp")
        mixed_probs, p_turned, p_stored = sem("mixed_probs"), sem("p_turned"), sem("p_stored")
        pv_done, head_out = sem("pv_done"), sem("head_out")
        rms_sum, rms_root, mixed_done = sem("rms_sum"), sem("rms_root"), sem("mixed_done")
        lam_sum, lam_exp = sem("lam_sum"), sem("lam_exp")
        out_group, out_evac = sem("out_group"), sem("out_evac")
        ln_in, ln_var, ln_root, ln_factors = sem("ln_in"), sem("ln_var"), sem("ln_root"), sem("ln_factors")
        ln_normed, ln_scaled = sem("ln_normed"), sem("ln_scaled")
        ln_done = [sem(f"ln_done{b}") for b in range(NB)]
        keys_in, q_group, q_stored = sem("keys_in"), sem("q_group"), sem("q_stored")
        keyed, keys_stored = sem("keyed"), sem("keys_stored")
        key_copied, key_read = sem("key_copied"), sem("key_read")
        gate_arg, gate_exp, routed = sem("gate_arg"), sem("gate_exp"), sem("routed")
        route_step = sem("route_step")
        sel_turned, sel_stored = sem("sel_turned"), sem("sel_stored")
        oh1_done, oh2_done, gate_mm, gate_evac = sem("oh1_done"), sem("oh2_done"), sem("gate_mm"), sem("gate_evac")
        gates_out, cols_done = sem("gates_out"), sem("cols_done")
        gelu_done = sem("gelu_done")
        gelu_stored = [sem(f"gelu_stored{i}") for i in range(2)]
        gelu_got = [sem(f"gelu_got{i}") for i in range(4)]
        gate_got = [sem(f"gate_got{i}") for i in range(4)]
        prod_done, ah_done, al_done = sem("prod_done"), sem("ah_done"), sem("al_done")
        y_done = sem("y_done")
        dve_step = sem("dve_step")

        with nc.Block() as block:
            @block.sync
            def _(sp):
                sp.dma_start(x[:], x_in).then_inc(first_sem, 16)
                sp.dma_start(ident[:], eye).then_inc(first_sem, 16)
                sp.dma_start(iota_k[:], iota.partition_broadcast(P)).then_inc(first_sem, 16)
                for j in range(NRAW):
                    sp.dma_start(raw[j][:], w_in[0, j]).then_inc(first_in[j], 16)
                sp.wait_ge(first_sem, 48)

        with nc.Fori(0, DEPTH) as layer:
            def of_layer(t):
                s = t[bass.ds(layer, 1)]
                if len(t.shape) == 2:
                    return s
                names = [f"d{i}" for i in range(len(t.shape) - 1)]
                return s.rearrange(f"a {' '.join(names)} -> (a {names[0]}) {' '.join(names[1:])}")

            with nc.Block() as block:
                @block.sync
                def _(sp):
                    def load(src, at, i, j):
                        sp.wait_ge(lo_done, i * BODY + (at + 2 * j + 2 - BODY))
                        sp.dma_start(raw[j][:], src(i * NRAW + j)).then_inc(raw_in[j], 16)

                    def tiles(t):
                        def src(m):
                            return t[bass.ds(layer, 1), bass.ds(m, 1)].rearrange("a b p n -> (a b p) n")
                        return src

                    def stream(t, at, count, lo_i=0):
                        with sp.Fori(lo_i, count // BODY) as i:
                            for j in range(NRAW):
                                load(tiles(t), at, i, j)

                    sp.dma_start(sinks_b, sinks[bass.ds(layer, 1)].partition_broadcast(P)).then_inc(par_in, 16)
                    sp.dma_start(lamp_b, lamp[bass.ds(layer, 1)].partition_broadcast(P)).then_inc(par_in, 16)
                    sp.dma_start(subg_b, subg[bass.ds(layer, 1)].partition_broadcast(P)).then_inc(par_in, 16)
                    sp.dma_start(lay_b, layer_consts[bass.ds(layer, 1)].partition_broadcast(P)).then_inc(par_in, 16)
                    sp.dma_start(trig.rearrange("p a b c -> p (a b c)"), rope).then_inc(par_in, 16)
                    sp.dma_start(bias_causal, masks[0]).then_inc(mask_in, 16)
                    sp.dma_start(bias_swa, masks[1]).then_inc(mask_in, 16)
                    sp.dma_start(bias_dil, masks[2]).then_inc(mask_in, 16)
                    sp.dma_start(count_dil, masks[3]).then_inc(mask_in, 16)
                    stream(w_in, AT_IN, N_IN, 1)
                    stream(w_out, AT_OUT, N_OUT)
                    sp.wait_ge(turn_lo, 16)
                    sp.dma_start(ln_gb, ln[bass.ds(layer, 1), 0:1].rearrange("a b c n -> (a b) (c n)").partition_broadcast(P)
                                 ).then_inc(ln_in, 16)
                    sp.dma_start(keys_sb, of_layer(keys)).then_inc(keys_in, 16)
                    stream(wq, AT_WQ, N_WQ)
                    with sp.Fori(0, 2 * quarter + 1) as i:
                        for j in range(NRAW):
                            load(tiles(u_t), AT_U, i, j)
                    sp.wait_ge(gate_evac, STEPS)
                    with sp.Fori(0, PIECES // NRAW) as i:
                        for j in range(NRAW):
                            load(tiles(u_t), AT_U, i + (2 * quarter + 1), j)
                            row = i * (NRAW * ROWS) + j * ROWS
                            sp.dma_start(a_dram[bass.ds(row, ROWS)].rearrange("i p t -> p i t"),
                                         gates[:, bass.ds(row, ROWS), :]).then_inc(gates_out, 16)
                    with sp.Fori(2 * quarter + 1 + PIECES // NRAW, 4 * quarter) as i:
                        for j in range(NRAW):
                            load(tiles(u_t), AT_U, i, j)
                    sp.wait_ge(gates_out, 16 * PIECES)

                    def side(m, j, first=False):
                        if not first:
                            sp.wait_ge(prod_done, m - 3)
                        sp.dma_start(gelu_in[j], g_dram[bass.ds(m, 1)].rearrange("a p t -> (a p) t")).then_inc(gelu_got[j], 16)
                        sp.dma_start(gate_in[j], a_dram[bass.ds(m, 1)].rearrange("a p t -> (a p) t")).then_inc(gate_got[j], 16)

                    sp.wait_ge(key_copied, NB * PH)
                    for s in gelu_stored:
                        sp.wait_ge(s, 16 * (NT // 2 - 2 * NRAW))
                    for j in range(NRAW):
                        side(j, j, first=True)
                    for j in range(NRAW):
                        load(tiles(v_t), AT_V, 0, j)
                    for s in gelu_stored:
                        sp.wait_ge(s, 16 * (NT // 2))

                    def second(i):
                        for j in range(NRAW):
                            side(i * NRAW + j, j)
                            load(tiles(v_t), AT_V, i, j)

                    with sp.Fori(1, 12) as i:
                        second(i)
                    sp.dma_start(ln_gb, ln[bass.ds(layer, 1), 1:2].rearrange("a b c n -> (a b) (c n)").partition_broadcast(P)
                                 ).then_inc(ln_in, 16)
                    with sp.Fori(12, NT // NRAW) as i:
                        second(i)
                    for j in range(NRAW):
                        sp.wait_ge(lo_done, N_HALVES - BODY + 2 * j + 2)
                        sp.dma_start(raw[j][:], w_in[bass.ds((layer + 1) % DEPTH, 1), j].rearrange("a p n -> (a p) n")
                                     ).then_inc(first_in[j], 16)

                @block.tensor
                def _(pe):
                    def turn(r, src):
                        for k in range(DC // 2):
                            n = r * (DC // 2) + k
                            if n >= 2:
                                pe.wait_ge(turn_lo, n - 1)
                            if r == 2 and k % 2 == 0:
                                for b in range(NB):
                                    pe.wait_ge(ln_done[b], k // 2 + 1)
                            for c in (2 * k, 2 * k + 1):
                                for b in range(NB):
                                    last = pe.transpose(bank[6 + k % 2][:, (c % 2) * L + b * P:(c % 2) * L + (b + 1) * P],
                                                        src[:, b, c * P:(c + 1) * P], ident[:])
                            last.then_inc(turned, 1)

                    def tokens_by_half(n, j, kc, banks, first_c, last_c):
                        pe.wait_ge(lo_done, n + 1)
                        for c4 in range(KC):
                            c = kc * KC + c4
                            for b in range(NB):
                                st_h, st_l = xh[:, c, b * P:(b + 1) * P], xl[:, c, b * P:(b + 1) * P]
                                mh = hi[j % NSPLIT][:, c4 * W:(c4 + 1) * W]
                                ml = lo[j % NSPLIT][:, c4 * W:(c4 + 1) * W]
                                pe.matmul(banks[b][:], st_h, mh, start=(c == first_c), stop=False)
                                pe.matmul(banks[b][:], st_h, ml, start=False, stop=False)
                                last = pe.matmul(banks[b][:], st_l, mh, start=False, stop=(c == last_c))
                        last.then_inc(half_used, 1)

                    def turn_rope(g, b):
                        pe.wait_ge(roped, g * NB + (b + 1))
                        if b_free_known(g):
                            pe.wait_ge(qk_stored, g * NB + (b + 1 - NB))
                        for j in range(4):
                            last = pe.transpose(bank[4 + b][:, j * P:(j + 1) * P], rt[b][:, j * P:(j + 1) * P], ident[:])
                        last.then_inc(rope_turned, 1)

                    def b_free_known(g):
                        return not (isinstance(g, int) and g == 0)

                    def in_group(g, par_, prev, free=True):
                        banks = [bank[2 * par_], bank[2 * par_ + 1]]
                        if free:
                            pe.wait_ge(rope_evac, g * NB - NB)
                        for kc in range(HPG):
                            tokens_by_half(g * HPG + (AT_IN + kc), kc, kc, banks, 0, DC - 1)
                            if prev is not None and kc in (2, 3):
                                turn_rope(prev, kc - 2)

                    turn(0, x)
                    pe.wait_ge(turn_lo, 8)
                    in_group(0, 0, None, free=False)
                    in_group(1, 1, 0, free=False)
                    with pe.Fori(1, 4) as i:
                        in_group(i * 2, 0, i * 2 - 1)
                        in_group(i * 2 + 1, 1, i * 2)
                    in_group(8, 0, 7)
                    in_group(9, 1, None)

                    pe.wait_ge(qk_stored, 8 * NB)
                    k = 0
                    for b in range(NB):
                        K = (b + 1) * P
                        for h in range(8):
                            rows = slice(HD * (h % 2), HD * (h % 2) + HD)
                            if k >= 2:
                                pe.wait_ge(irelu, k - 1)
                            pe.matmul(bank[6 + k % 2][:, 0:K], qk_t[rows, PAIR["iq"] + h // 2, b * P:(b + 1) * P],
                                      qk_t[rows, PAIR["ik"], 0:K], start=True, stop=True).then_inc(iscored, 1)
                            k += 1

                    def scores(u):
                        kind, h, b, items = UNITS[u]
                        K = (b + 1) * P
                        for part, n in enumerate(items):
                            qp, kp, half = score_operands(kind, h, part)
                            rows = slice(HD * half, HD * half + HD)
                            if n >= 4:
                                pe.wait_ge(masked_done, n - 3)
                            pe.matmul(bank[n % 4][:, 0:K], qk_t[rows, qp, b * P:(b + 1) * P], qk_t[rows, kp, 0:K],
                                      start=True, stop=True).then_inc(scored, 1)

                    def turn_probs(u):
                        kind, h, b, items = UNITS[u]
                        if kind in "AD":
                            pe.wait_ge(exp_done, items[-1] + 1)
                        else:
                            pe.wait_ge(mixed_probs, n_mixed(u))
                        if u >= 2:
                            pe.wait_ge(p_stored, u - 1)
                        for kb in range(b + 1):
                            last = pe.transpose(bank[4 + u % 2][:, kb * P:(kb + 1) * P],
                                                probs[items[0] % 4][:, kb * P:(kb + 1) * P], ident[:])
                        last.then_inc(p_turned, 1)

                    def values(u):
                        kind, h, b, items = UNITS[u]
                        pe.wait_ge(p_stored, u + 1)
                        if u >= 2:
                            pe.wait_ge(head_out, u - 1)
                        at, width = value_columns(kind, h)
                        for kb in range(b + 1):
                            last = pe.matmul(bank[6 + u % 2][:, 0:width], probs_t[u % 2][:, kb * P:(kb + 1) * P],
                                             vals[:, kb, at:at + width], start=(kb == 0), stop=(kb == b))
                        last.then_inc(pv_done, 1)

                    def n_mixed(u):
                        return sum(UNITS[i][0] in "BC" for i in range(u + 1))

                    def value_columns(kind, h):
                        return {"A": (V_A + HD * (h // 4), HD), "B": (V_B + 2 * HD * h, 2 * HD),
                                "C": (V_C + HD * h, HD), "D": (V_D, HD)}[kind]

                    pe.wait_ge(v_stored, 2 * NB)
                    pe.wait_ge(rope_evac, 8 * NB)
                    pe.wait_ge(irelu, 16)
                    scores(0)
                    scores(1)
                    for u in range(n_units + 1):
                        if u + 2 < n_units:
                            scores(u + 2)
                        if u < n_units:
                            turn_probs(u)
                        if u >= 1:
                            values(u - 1)

                    pe.wait_ge(mixed_done, 1)
                    turn(1, mixed)
                    pe.wait_ge(turn_lo, 16)
                    for g in range(D // W):
                        if g >= 2:
                            pe.wait_ge(out_evac, NB * (g - 1))
                        for kc in range(HPG):
                            tokens_by_half(AT_OUT + g * HPG + kc, kc, kc, [bank[2 * (g % 2)], bank[2 * (g % 2) + 1]], 0, DC - 1)

                    turn(2, x)
                    pe.wait_ge(turn_lo, 24)
                    for g in range(D // W):
                        if g >= 2:
                            pe.wait_ge(q_stored, 4 * (g - 1))
                        for kc in range(HPG):
                            pe.wait_ge(lo_done, AT_WQ + g * HPG + kc + 1)
                            for j in range(4):
                                q_bank = bank[4 * (g % 2) + j][:, 0:L]
                                for c4 in range(KC):
                                    c = kc * KC + c4
                                    at = c4 * W + j * P
                                    wh, wl = hi[kc % NSPLIT][:, at:at + P], lo[kc % NSPLIT][:, at:at + P]
                                    pe.matmul(q_bank, wh, xh[:, c, :], start=(c == 0), stop=False)
                                    pe.matmul(q_bank, wh, xl[:, c, :], start=False, stop=False)
                                    last = pe.matmul(q_bank, wl, xh[:, c, :], start=False, stop=(c == DC - 1))
                            last.then_inc(half_used, 1)

                    pe.wait_ge(keys_in, 16)
                    pe.wait_ge(q_stored, 16)
                    for b in range(NB):
                        for k in range(4):
                            for j in range(4):
                                last = pe.matmul(bank[4 * b + k][:, j * P:(j + 1) * P], q_t[:, 4 * k + j, b * P:(b + 1) * P],
                                                 keys_sb[:, 4 * k + j, :], start=True, stop=True)
                            last.then_inc(keyed, 1)

                    def hidden(i, j, first=False):
                        pe.wait_ge(lo_done, i * BODY + (AT_U + j + 1))
                        if j % 2 == 0 and not first:
                            pe.wait_ge(gelu_done, i * NRAW + (j // 2 - 1))
                        h = bank[j // 2 % 2][:, 0:L]
                        for c8 in range(DC // 2):
                            c = (j % 2) * (DC // 2) + c8
                            wh, wl = hi[j % NSPLIT][:, c8 * P:(c8 + 1) * P], lo[j % NSPLIT][:, c8 * P:(c8 + 1) * P]
                            pe.matmul(h, wh, xh[:, c, :], start=(c == 0), stop=False)
                            pe.matmul(h, wh, xl[:, c, :], start=False, stop=False)
                            last = pe.matmul(h, wl, xh[:, c, :], start=False, stop=(c == DC - 1))
                        last.then_inc(half_used, 1)

                    def gate_step(s, p, first=False):
                        pe.wait_ge(oh1_done, s + 1)
                        pe.wait_ge(oh2_done, s + 1)
                        if not first:
                            pe.wait_ge(gate_evac, s - 1)
                        for t in range(TG):
                            last = pe.matmul(bank[4 + p][:, t * P:(t + 1) * P], oh1[p][:, t, :], oh2[p][:, t, :],
                                             start=True, stop=True)
                        last.then_inc(gate_mm, 1)

                    pe.wait_ge(keys_stored, 8)
                    for b in range(NB):
                        if b == 0:
                            for j in range(BODY):
                                hidden(0, j, first=j < 4)
                        with pe.Fori(2 * b * quarter + (b == 0), (2 * b + 1) * quarter) as i:
                            for j in range(BODY):
                                hidden(i, j)
                        for j in range(BODY):
                            hidden((2 * b + 1) * quarter, j)
                            if j == 3:
                                pe.wait_ge(routed, b + 1)
                                for k in range(3):
                                    last = pe.transpose(bank[2][:, k * P:(k + 1) * P], sel[:, k, b, :], ident[:])
                                last.then_inc(sel_turned, 1)
                            if j >= 4:
                                gate_step(b * STEPS + j - 4, j % 2, first=(b == 0 and j < 6))
                        with pe.Fori(1, quarter) as i:
                            for j in range(BODY):
                                hidden(i + (2 * b + 1) * quarter, j)
                                if j % 2:
                                    gate_step(i * 4 + (b * STEPS + j // 2), j // 2 % 2)

                    def gather(i, j, start=False, stop=False):
                        m, half = j // 2, j % 2
                        pe.wait_ge(lo_done, i * BODY + (AT_V + j + 1))
                        if half == 0:
                            pe.wait_ge(al_done, i * NRAW + (m + 1))
                        for b in range(NB):
                            a_h, a_l = ah[m % 2][:, b * P:(b + 1) * P], al[m % 2][:, b * P:(b + 1) * P]
                            for q in range(2):
                                y = bank[4 * b + 2 * half + q][:]
                                vh, vl = hi[j % NSPLIT][:, q * W:(q + 1) * W], lo[j % NSPLIT][:, q * W:(q + 1) * W]
                                pe.matmul(y, a_h, vh, start=start, stop=False)
                                pe.matmul(y, a_h, vl, start=False, stop=False)
                                last = pe.matmul(y, a_l, vh, start=False, stop=stop)
                        last.then_inc(half_used, 1)

                    pe.wait_ge(gelu_done, NT)
                    for j in range(BODY):
                        gather(0, j, start=(j < 2))
                    with pe.Fori(1, N_V // BODY - 1) as i:
                        for j in range(BODY):
                            gather(i, j)
                    for j in range(BODY):
                        gather(N_V // BODY - 1, j, stop=(j >= BODY - 2))

                @block.scalar
                def _(act):
                    def split_hi(at, i, j, first=False):
                        if at == AT_IN and isinstance(i, int) and i == 0:
                            act.wait_ge(first_in[j // 2], layer * 16 + 16)
                        else:
                            act.wait_ge(raw_in[j // 2], i * 16 + at // BODY * 16)
                        if not first:
                            act.wait_ge(half_used, i * BODY + (at + j + 1 - NSPLIT))
                        half = raw[j // 2][:, (j % 2) * HT:(j % 2 + 1) * HT]
                        act.activation(hi[j % NSPLIT][:], half, ACT.Copy).then_inc(hi_done, 1)

                    def turn_high(r):
                        for k in range(DC // 2):
                            act.wait_ge(turned, r * (DC // 2) + k + 1)
                            act.activation(xh[:, 2 * k:2 * k + 2, :].rearrange("p a b -> p (a b)"), bank[6 + k % 2][:],
                                           ACT.Copy).then_inc(turn_hi, 1)

                    def store_qk(g, b):
                        act.wait_ge(rope_turned, NB * g + b + 1)
                        act.activation(qk_t[:, 4 * g:4 * g + 4, b * P:(b + 1) * P],
                                       bank[4 + b][:].rearrange("p (a b) -> p a b", a=4), ACT.Copy).then_inc(qk_stored, 1)

                    def store_v(g, at):
                        act.wait_ge(half_used, AT_IN + HPG * (g + 1))
                        for b in range(NB):
                            act.activation(vals[:, b, at:at + W], bank[2 * (g % 2) + b][:], ACT.Copy).then_inc(v_stored, 1)

                    def store_q_group(g):
                        act.wait_ge(half_used, AT_WQ + HPG * (g + 1))
                        for j in range(4):
                            act.activation(q_t[:, 4 * g + j, :], bank[4 * (g % 2) + j][:, 0:L], ACT.Copy).then_inc(q_stored, 1)

                    for j in range(NSPLIT):
                        split_hi(AT_IN, 0, j, first=True)
                    turn_high(0)
                    for g in range(NG_IN):
                        for kc in range(HPG):
                            if g or kc >= NSPLIT:
                                split_hi(AT_IN, g, kc)
                            if 1 <= g <= 8 and kc >= 6:
                                store_qk(g - 1, kc - 6)
                            if g == 9 and kc == 4:
                                store_v(8, V_B)
                    for j in range(NSPLIT):
                        split_hi(AT_OUT, 0, j)
                    store_v(9, V_C)

                    act.wait_ge(lam_sum, 2)
                    act.activation(small[:, 2:4], small[:, 0:2], ACT.Exp).then_inc(lam_exp, 1)
                    k = 0
                    for b in range(NB):
                        K = (b + 1) * P
                        for h in range(8):
                            act.wait_ge(iscored, k + 1)
                            if k >= 2:
                                act.wait_ge(iacc, k - 1)
                            act.activation(relu[k % 2][:, 0:K], bank[6 + k % 2][:, 0:K], ACT.Relu).then_inc(irelu, 1)
                            k += 1

                    def exps(u):
                        kind, h, b, items = UNITS[u]
                        K = (b + 1) * P
                        for n in items:
                            act.wait_ge(nbias_done, n + 1)
                            if n >= 4:
                                act.wait_ge(p_turned, unit_of(n - 4) + 1)
                            act.activation(probs[n % 4][:, 0:K], masked[n % 2][:, 0:K], ACT.Exp, bias=st[:, 1, n:n + 1],
                                           scale=SCALE, accum_out=st[:, 2, n:n + 1]).then_inc(exp_done, 1)
                            if kind == "A":
                                act.activation(small[:, 16 + n:17 + n], sinks_b[:, h:h + 1], ACT.Exp,
                                               bias=st[:, 1, n:n + 1]).then_inc(sink_exp, 1)

                    def unit_of(n):
                        return next(i for i, w in enumerate(UNITS) if n in w[3])

                    exps(0)
                    for u in range(n_units):
                        if u + 1 < n_units:
                            exps(u + 1)
                        K = (UNITS[u][2] + 1) * P
                        act.wait_ge(p_turned, u + 1)
                        if u >= 2:
                            act.wait_ge(pv_done, u - 1)
                        act.activation(probs_t[u % 2][:, 0:K], bank[4 + u % 2][:, 0:K], ACT.Copy).then_inc(p_stored, 1)
                    act.wait_ge(rms_sum, 8)
                    act.activation(small[:, 48:56], small[:, 40:48], ACT.Sqrt, bias=lay_b[:, 2:3],
                                   scale=1.0 / (2 * HD)).then_inc(rms_root, 1)
                    turn_high(1)
                    for m in range(NSPLIT, N_OUT):
                        split_hi(AT_OUT, m // BODY, m % BODY)
                    for j in range(NSPLIT):
                        split_hi(AT_WQ, 0, j)

                    def layer_norm(k):
                        for b in range(NB):
                            act.wait_ge(ln_var, k * NB + b + 1)
                            act.activation(norm[:, b, 2:3], norm[:, b, 1:2], ACT.Sqrt, bias=lay_b[:, 2:3]).then_inc(ln_root, 1)
                        act.wait_ge(ln_factors, k + 1)
                        for q in range(4):
                            cols = x[:, 1, q * W:(q + 1) * W]
                            act.activation(cols, cols, ACT.Identity, bias=norm[:, 1, 4:5], scale=norm[:, 1, 3:4]).then_inc(ln_normed, 1)

                    layer_norm(0)
                    turn_high(2)
                    for m in range(NSPLIT, N_WQ):
                        split_hi(AT_WQ, m // BODY, m % BODY)
                        if m >= BODY and m % BODY == NSPLIT - 1:
                            store_q_group(m // BODY - 1)
                    for j in range(NSPLIT):
                        split_hi(AT_U, 0, j)
                    store_q_group(3)
                    for k in range(8):
                        act.wait_ge(keyed, k + 1)
                        act.activation(key_s[k // 4][:, 4 * (k % 4):4 * (k % 4) + 4, :],
                                       bank[k][:].rearrange("p (a n) -> p a n", a=4), ACT.Copy).then_inc(keys_stored, 1)

                    def gelu(i, m, rounds, first=False):
                        act.wait_ge(half_used, i * BODY + (AT_U + 2 * m + 2))
                        if not first:
                            act.wait_ge(gelu_stored[m % 2], rounds * 16)
                        act.activation(gelu_out[m % 2][:], bank[m % 2][:, 0:L], ACT.Gelu).then_inc(gelu_done, 1)
                        act.wait_ge(gelu_done, i * NRAW + (m + 1))
                        act.dma_start(g_dram[bass.ds(i * NRAW + m, 1)].rearrange("a p t -> (a p) t"), gelu_out[m % 2][:]
                                      ).then_inc(gelu_stored[m % 2], 16)

                    def place_gates(s, col, p, b):
                        act.wait_ge(gate_mm, s + 1)
                        if b:
                            act.wait_ge(gates_out, 16 * PIECES)
                        else:
                            act.wait_ge(keyed, 8)
                        act.activation(gates.rearrange("p i t -> p t i")[:, bass.ds(col, TG), :],
                                       bank[4 + p][:].rearrange("p (t i) -> p t i", t=TG), ACT.Copy).then_inc(gate_evac, 1)

                    def half_body(i, j, first=False, last=False):
                        if j % 2:
                            gelu(i, j // 2, i * 2 + j // 2 // 2, first=first and j < 4)
                        ahead = j + NSPLIT
                        if not last or ahead < BODY:
                            split_hi(AT_U, i + ahead // BODY, ahead % BODY)
                        else:
                            split_hi(AT_V, 0, ahead % BODY)

                    for b in range(NB):
                        if b == 0:
                            for j in range(BODY):
                                half_body(0, j, first=True)
                        with act.Fori(2 * b * quarter + (b == 0), (2 * b + 1) * quarter) as i:
                            for j in range(BODY):
                                half_body(i, j)
                        for j in range(BODY):
                            half_body((2 * b + 1) * quarter, j)
                            if j == 0:
                                act.wait_ge(gate_arg, b + 1)
                                act.activation(sel[:, 2, b, :], sel[:, 2, b, :], ACT.Exp).then_inc(gate_exp, 1)
                            if j == 3:
                                act.wait_ge(sel_turned, b + 1)
                                act.activation(sel_t[:, :, b * P:(b + 1) * P], bank[2][:, 0:3 * P].rearrange("p (s t) -> p s t", s=3),
                                               ACT.Copy).then_inc(sel_stored, 1)
                            if j >= 4:
                                place_gates(b * STEPS + j - 4, (j - 4) * TG, j % 2, b)
                        with act.Fori(1, quarter - (b == 1)) as i:
                            for j in range(BODY):
                                half_body(i + (2 * b + 1) * quarter, j)
                                if j % 2:
                                    place_gates(i * 4 + (b * STEPS + j // 2), i * (4 * TG) + j // 2 * TG, j // 2 % 2, b)
                    for j in range(BODY):
                        half_body(4 * quarter - 1, j, last=True)
                        if j % 2:
                            place_gates(2 * STEPS - 4 + j // 2, P - 4 * TG + j // 2 * TG, j // 2 % 2, 1)

                    def a_high(i, m):
                        act.wait_ge(prod_done, i * NRAW + (m + 1))
                        act.activation(ah[m % 2], prod[m % 2], ACT.Copy).then_inc(ah_done, 1)

                    def second_body(i, j, last=False):
                        if j % 2 == 0 and not (last and j + 2 >= BODY):
                            act.wait_ge(half_used, i * BODY + (AT_V + j))
                            a_high(i + (j // 2 + 1) // NRAW, (j // 2 + 1) % NRAW)
                        ahead = j + NSPLIT
                        if not last or ahead < BODY:
                            split_hi(AT_V, i + ahead // BODY, ahead % BODY)

                    a_high(0, 0)
                    with act.Fori(0, N_V // BODY - 1) as i:
                        for j in range(BODY):
                            second_body(i, j)
                    for j in range(BODY):
                        second_body(N_V // BODY - 1, j, last=True)
                    layer_norm(1)

                @block.gpsimd
                def _(pool):
                    for g in range(8):
                        for b in range(NB):
                            pool.wait_ge(rope_parts, NB * g + b + 1)
                            if g:
                                pool.wait_ge(rope_turned, NB * (g - 1) + b + 1)
                            if g < G_MIX:
                                pool.tensor_tensor(rt[b], ra[b], rb[b], ALU.add).then_inc(roped, 1)
                            else:
                                dup = rt[b].rearrange("p (h r e) -> p h r e", r=2, e=HD)
                                a4 = ra[b][:, 0:4 * HD].rearrange("p (h e) -> p h e", e=HD)
                                b4 = rb[b][:, 0:4 * HD].rearrange("p (h e) -> p h e", e=HD)
                                pool.tensor_tensor(dup[:, :, 0, :], a4, b4, ALU.add)
                                pool.tensor_tensor(dup[:, :, 1, :], a4, b4, ALU.add).then_inc(roped, 1)

                    def first_keys(s, p, first=False):
                        if not first:
                            pool.wait_ge(gate_mm, s - 1)
                        pool.tensor_copy(key_cols[p], sel_t[:, 0, bass.ds(s * TG, TG)]).then_inc(cols_done, 1)
                        pool.wait_ge(cols_done, 1)
                        for t in range(TG):
                            last = pool.tensor_scalar(oh1[p][:, t, :], iota_k[:], key_cols[p][:, t:t + 1], None, ALU.is_equal)
                        last.then_inc(oh1_done, 1)
                        pool.sem_clear(cols_done)

                    def layer_norm(k):
                        pool.wait_ge(ln_in, 16 * (k + 1))
                        for q in range(4):
                            cols = x[:, 1, q * W:(q + 1) * W]
                            pool.wait_ge(ln_normed, 4 * k + q + 1)
                            pool.tensor_tensor(cols, cols, ln_gb[:, 0, q * W:(q + 1) * W], ALU.mult).then_inc(ln_scaled, 1)
                            pool.wait_ge(ln_scaled, 4 * k + q + 1)
                            pool.tensor_tensor(cols, cols, ln_gb[:, 1, q * W:(q + 1) * W], ALU.add).then_inc(ln_done[1], 1)

                    layer_norm(0)
                    pool.wait_ge(keys_stored, 8)
                    for b in range(NB):
                        def copy_keys(h):
                            pool.tensor_copy(key_now[:], key_s[b][:, bass.ds(h * 2, 2), :]).then_inc(key_copied, 1)
                        if b:
                            pool.wait_ge(key_read, PH)
                        copy_keys(0)
                        with pool.Fori(1, PH) as h:
                            pool.wait_ge(key_read, h + b * PH)
                            copy_keys(h)
                        pool.wait_ge(key_copied, (b + 1) * PH)
                        pool.wait_ge(sel_stored, b + 1)
                        first_keys(b * STEPS, 0, first=(b == 0))
                        first_keys(b * STEPS + 1, 1, first=(b == 0))
                        with pool.Fori(1, STEPS // 2) as i:
                            first_keys(i * 2 + b * STEPS, 0)
                            first_keys(i * 2 + (b * STEPS + 1), 1)
                    layer_norm(1)

                @block.vector
                def _(dve):
                    step = [0]

                    def mark(ins):
                        step[0] += 1
                        ins.then_inc(dve_step, 1)
                        return step[0]

                    def own(n):
                        dve.wait_ge(dve_step, n)

                    def split_lo(at, i, j):
                        dve.wait_ge(hi_done, i * BODY + (at + j + 1))
                        half = raw[j // 2][:, (j % 2) * HT:(j % 2 + 1) * HT]
                        dve.tensor_tensor(lo[j % NSPLIT][:], half, hi[j % NSPLIT][:].bitcast(F32), ALU.subtract).then_inc(lo_done, 1)

                    def turn_low(r):
                        for k in range(DC // 2):
                            dve.wait_ge(turn_hi, r * (DC // 2) + k + 1)
                            two = slice(2 * k, 2 * k + 2)
                            dve.tensor_tensor(xl[:, two, :].rearrange("p a b -> p (a b)"), bank[6 + k % 2][:],
                                              xh[:, two, :].rearrange("p a b -> p (a b)").bitcast(F32),
                                              ALU.subtract).then_inc(turn_lo, 1)

                    def rotate(g, b, heads=8, first=False):
                        dve.wait_ge(half_used, g * HPG + (AT_IN + HPG))
                        if not first:
                            dve.wait_ge(roped, g * NB + (b + 1 - NB))
                        src = bank[2 * parity(g) + b][:, 0:heads * HD].rearrange("p (h e) -> p h e", e=HD)
                        a = ra[b][:, 0:heads * HD].rearrange("p (h e) -> p h e", e=HD)
                        r = rb[b][:, 0:heads * HD].rearrange("p (h e) -> p h e", e=HD)
                        cos = trig[:, b, 0:1, :].to_broadcast([P, heads, HD])
                        sin = trig[:, b, 1:2, :].to_broadcast([P, heads, HD])
                        dve.tensor_tensor(a, src, cos, ALU.mult)
                        dve.tensor_tensor(r[:, :, 0:HALF], src[:, :, HALF:HD], sin[:, :, 0:HALF], ALU.mult)
                        return dve.tensor_tensor(r[:, :, HALF:HD], src[:, :, 0:HALF], sin[:, :, HALF:HD], ALU.mult
                                                 ).then_inc(rope_parts, 1)

                    def parity(g):
                        return g % 2 if isinstance(g, int) else g.par

                    for j in range(NSPLIT):
                        split_lo(AT_IN, 0, j)
                    turn_low(0)
                    dve.wait_ge(par_in, 16 * 5)
                    mark(dve.tensor_tensor_reduce(out=lamp_b[:, 0:HD], in0=lamp_b[:, 0:HD], in1=lamp_b[:, HD:2 * HD], scale=1.0,
                                                  scalar=0.0, op0=ALU.mult, op1=ALU.add, accum_out=small[:, 0:1]))
                    dve.tensor_tensor_reduce(out=lamp_b[:, 2 * HD:3 * HD], in0=lamp_b[:, 2 * HD:3 * HD], in1=lamp_b[:, 3 * HD:4 * HD],
                                             scale=1.0, scalar=0.0, op0=ALU.mult, op1=ALU.add,
                                             accum_out=small[:, 1:2]).then_inc(lam_sum, 2)
                    for g in range(NG_IN):
                        for kc in range(HPG):
                            if g or kc >= NSPLIT:
                                split_lo(AT_IN, g, kc)
                            if 1 <= g <= 8 and kc in (3, 4):
                                pg, b = g - 1, kc - 3
                                rotate(pg, b, heads=8 if pg < G_MIX else 4, first=pg == 0)
                                if pg < G_MIX:
                                    dve.wait_ge(rope_parts, NB * pg + b + 1)
                                    dve.sem_inc(rope_evac, 1)
                                else:
                                    dve.tensor_copy(vals[:, b, 0:V_B], bank[2 * (pg % 2) + b][:, 4 * HD:4 * HD + V_B]
                                                    ).then_inc(rope_evac, 1)
                    for j in range(NSPLIT):
                        split_lo(AT_OUT, 0, j)

                    dve.wait_ge(lam_exp, 1)
                    n = mark(dve.tensor_tensor(small[:, 4:5], small[:, 2:3], small[:, 3:4], ALU.subtract))
                    own(n)
                    n = mark(dve.tensor_tensor(small[:, 5:6], small[:, 4:5], lay_b[:, 0:1], ALU.add))
                    dve.wait_ge(rope_evac, 8 * NB)
                    for b in range(NB):
                        n = mark(dve.tensor_scalar(small[:, 56:64] if b else small[:, 6:14], vals[:, b, V_IW:V_IW + 8],
                                                   8 ** -0.5 * SCALE, None, ALU.mult))
                    own(n)
                    n = mark(dve.tensor_scalar(small[:, 5:6], small[:, 5:6], -1.0, None, ALU.mult))
                    neg_lam = small[:, 5:6]
                    own(n)
                    n = mark(dve.tensor_scalar(subg_b, subg_b, lay_b[:, 1:2], None, ALU.mult))
                    own(n)

                    dve.wait_ge(mask_in, 16 * 4)
                    k = 0
                    for b in range(NB):
                        K = (b + 1) * P
                        causal = bias_causal[:, L - K:L]
                        iw = small[:, 56:64] if b else small[:, 6:14]
                        for h in range(8):
                            dve.wait_ge(irelu, k + 1)
                            if h:
                                dve.wait_ge(iacc, k)
                            dve.scalar_tensor_tensor(out=iscore[b][:, 0:K], in0=relu[k % 2][:, 0:K], scalar=iw[:, h:h + 1],
                                                     in1=causal if h == 0 else iscore[b][:, 0:K], op0=ALU.mult,
                                                     op1=ALU.add).then_inc(iacc, 1)
                            k += 1
                    for b in range(NB):
                        K = (b + 1) * P
                        dve.wait_ge(iacc, 8 * (b + 1))
                        for r in range(TOPK // 8):
                            n = mark(dve.max(out=small[:, 24:32], in_=iscore[b][:, 0:K]))
                            own(n)
                            n = mark(dve.match_replace(out=iscore[b][:, 0:K], in_to_replace=small[:, 24:32],
                                                       in_values=iscore[b][:, 0:K], imm_value=TAKEN))
                            own(n)
                        n = mark(dve.tensor_scalar(iwork[b][:, 0:K], iscore[b][:, 0:K], TAKEN / 2, NEG, ALU.is_gt, ALU.mult))
                        own(n)
                        n = mark(dve.tensor_tensor(bias_dsa[b][:, 0:K], iwork[b][:, 0:K], bias_causal[:, L - K:L], ALU.add))
                        own(n)
                    n = mark(dve.tensor_scalar(small[:, 32:40], sinks_b, 1.0 / SCALE, None, ALU.mult))
                    own(n)

                    def row_max(u):
                        kind, h, b, items = UNITS[u]
                        K = (b + 1) * P
                        for i in items:
                            dve.wait_ge(scored, i + 1)
                            if i >= 2:
                                dve.wait_ge(exp_done, i - 1)
                            bias = {"A": bias_swa, "B": bias_causal, "C": bias_dil}.get(kind)
                            bias = bias_dsa[b][:, 0:K] if bias is None else bias[:, L - K:L]
                            dve.tensor_tensor_reduce(out=masked[i % 2][:, 0:K], in0=bank[i % 4][:, 0:K], in1=bias, scale=1.0,
                                                     scalar=small[:, 32 + h:33 + h] if kind == "A" else TAKEN,
                                                     op0=ALU.add, op1=ALU.max, accum_out=st[:, 0, i:i + 1]).then_inc(masked_done, 1)
                            dve.wait_ge(masked_done, i + 1)
                            dve.tensor_scalar(st[:, 1, i:i + 1], st[:, 0, i:i + 1], -SCALE, None, ALU.mult).then_inc(nbias_done, 1)

                    def finish_probs(u):
                        kind, h, b, items = UNITS[u]
                        K = (b + 1) * P
                        i = items[0]
                        dve.wait_ge(exp_done, items[-1] + 1)
                        if kind == "A":
                            dve.wait_ge(sink_exp, i + 1)
                            own(mark(dve.tensor_tensor(st[:, 2, i:i + 1], st[:, 2, i:i + 1], small[:, 16 + i:17 + i], ALU.add)))
                        if kind == "C":
                            dve.scalar_tensor_tensor(out=probs[i % 4][:, 0:K], in0=probs[i % 4][:, 0:K], scalar=1.0,
                                                     in1=count_dil[:, L - K:L], op0=ALU.mult, op1=ALU.mult,
                                                     accum_out=st[:, 2, i:i + 1]).then_inc(mixed_probs, 1)
                            dve.wait_ge(mixed_probs, n_mixed(u))
                        own(mark(dve.reciprocal(st[:, 3, i:i + len(items)], st[:, 2, i:i + len(items)])))
                        if kind == "B":
                            j = items[1]
                            own(mark(dve.tensor_scalar(probs[j % 4][:, 0:K], probs[j % 4][:, 0:K], st[:, 3, j:j + 1], neg_lam,
                                                       ALU.mult, ALU.mult)))
                            dve.scalar_tensor_tensor(out=probs[i % 4][:, 0:K], in0=probs[i % 4][:, 0:K], scalar=st[:, 3, i:i + 1],
                                                     in1=probs[j % 4][:, 0:K], op0=ALU.mult, op1=ALU.add).then_inc(mixed_probs, 1)

                    def n_mixed(u):
                        return sum(UNITS[i][0] in "BC" for i in range(u + 1))

                    def take_out(u):
                        kind, h, b, items = UNITS[u]
                        dve.wait_ge(pv_done, u + 1)
                        src = bank[6 + u % 2]
                        if kind == "B":
                            at = MIX_B + 2 * HD * h
                            dve.tensor_copy(mixed[:, b, at:at + 2 * HD], src[:, 0:2 * HD]).then_inc(head_out, 1)
                        else:
                            at = {"A": MIX_A, "C": MIX_C, "D": MIX_D}[kind] + HD * h
                            dve.tensor_scalar(mixed[:, b, at:at + HD], src[:, 0:HD], st[:, 3, items[0]:items[0] + 1], None,
                                              ALU.mult).then_inc(head_out, 1)

                    row_max(0)
                    for u in range(n_units + 1):
                        if u + 1 < n_units:
                            row_max(u + 1)
                        if u < n_units:
                            finish_probs(u)
                        if u >= 1:
                            take_out(u - 1)

                    dve.wait_ge(head_out, n_units)
                    for j in range(8):
                        h, b = j // 2, j % 2
                        at = MIX_B + 2 * HD * h
                        dve.tensor_tensor_reduce(out=relu[0][:, 0:2 * HD] if j % 2 else relu[1][:, 0:2 * HD], in0=mixed[:, b, at:at + 2 * HD],
                                                 in1=mixed[:, b, at:at + 2 * HD], scale=1.0, scalar=0.0, op0=ALU.mult, op1=ALU.add,
                                                 accum_out=small[:, 40 + j:41 + j]).then_inc(rms_sum, 1)
                        dve.wait_ge(rms_sum, j + 1)
                    dve.wait_ge(rms_root, 1)
                    own(mark(dve.reciprocal(small[:, 40:48], small[:, 48:56])))
                    for j in range(8):
                        h, b = j // 2, j % 2
                        at = MIX_B + 2 * HD * h
                        last = dve.scalar_tensor_tensor(out=mixed[:, b, at:at + 2 * HD], in0=mixed[:, b, at:at + 2 * HD],
                                                        scalar=small[:, 40 + j:41 + j], in1=subg_b, op0=ALU.mult, op1=ALU.mult)
                    last.then_inc(mixed_done, 1)
                    turn_low(1)

                    def onto_residual(b, q, src):
                        cols = x[:, b, q * W:(q + 1) * W]
                        return mark(dve.scalar_tensor_tensor(out=cols, in0=cols, scalar=ALPHA, in1=src, op0=ALU.mult, op1=ALU.add))

                    def moments(b, q, n):
                        own(n)
                        return mark(dve.bn_stats(stats[:, b, q, :], x[:, b, q * W:(q + 1) * W]))

                    def layer_norm(k, n):
                        own(n)
                        for b in range(NB):
                            dve.bn_aggr(norm[:, b, 0:2], stats[:, b, :, :].rearrange("p q s -> p (q s)")).then_inc(ln_var, 1)
                        for b in (1, 0):
                            dve.wait_ge(ln_root, k * NB + b + 1)
                            own(mark(dve.reciprocal(norm[:, b, 3:4], norm[:, b, 2:3])))
                            if b == 1:
                                dve.scalar_tensor_tensor(out=norm[:, b, 4:5], in0=norm[:, b, 0:1], scalar=-1.0, in1=norm[:, b, 3:4],
                                                         op0=ALU.mult, op1=ALU.mult).then_inc(ln_factors, 1)
                        dve.wait_ge(ln_in, 16 * (k + 1))

                        def quarter_of(t, q):
                            return t[:, 0, q * W:(q + 1) * W]

                        def center(q):
                            return mark(dve.scalar_tensor_tensor(out=quarter_of(x, q), in0=quarter_of(x, q), scalar=norm[:, 0, 0:1],
                                                                 in1=ln_gb[:, 0, q * W:(q + 1) * W], op0=ALU.subtract, op1=ALU.mult))

                        n = center(0)
                        for q in range(4):
                            ahead = center(q + 1) if q < 3 else None
                            own(n)
                            dve.scalar_tensor_tensor(out=quarter_of(x, q), in0=quarter_of(x, q), scalar=norm[:, 0, 3:4],
                                                     in1=ln_gb[:, 1, q * W:(q + 1) * W], op0=ALU.mult, op1=ALU.add
                                                     ).then_inc(ln_done[0], 1)
                            n = ahead

                    def take_out_group(g):
                        dve.wait_ge(half_used, AT_OUT + HPG * (g + 1))
                        n = []
                        for b in range(NB):
                            n.append(onto_residual(b, g, bank[2 * (g % 2) + b][:]))
                        for b in range(NB):
                            last = moments(b, g, n[b])
                            if g < 2:
                                dve.sem_inc(out_evac, 1)
                        return last

                    for m in range(NSPLIT, N_OUT):
                        split_lo(AT_OUT, m // BODY, m % BODY)
                        if m >= BODY and m % BODY == NSPLIT - 1:
                            take_out_group(m // BODY - 1)
                    for j in range(NSPLIT):
                        split_lo(AT_WQ, 0, j)
                    layer_norm(0, take_out_group(3))
                    turn_low(2)
                    for m in range(NSPLIT, N_WQ):
                        split_lo(AT_WQ, m // BODY, m % BODY)
                    for j in range(NSPLIT):
                        split_lo(AT_U, 0, j)

                    def route_body(i, b, h):
                        done = [0]

                        def then(ins):
                            done[0] += 1
                            ins.then_inc(route_step, 1)
                            dve.wait_ge(route_step, done[0])

                        def top8(src, v, idx, k):
                            then(dve.max(out=v[:, k:k + 8], in_=src))
                            then(dve.max_index(out=idx[:, k:k + 8], in_max=v[:, k:k + 8], in_values=src))

                        def drop8(src, v):
                            then(dve.match_replace(out=src, in_to_replace=v[:, 0:8], in_values=src, imm_value=TAKEN))

                        def side(s):
                            return key_now[:, s, :], top_v[:, s, :], top_i[:, s, :]

                        def lookup(s):
                            oh = cand[:].rearrange("p (k c) -> p k c", c=PK)
                            then(dve.tensor_copy(pos_num[:], pos[:, s, :]))
                            then(dve.tensor_tensor(oh, iota_k[:, 0:PK].unsqueeze(1).to_broadcast([P, PK, PK]),
                                                   pos_num[:].unsqueeze(2).to_broadcast([P, PK, PK]), ALU.is_equal))
                            then(dve.tensor_tensor(oh, oh, key_num[:, s, :].unsqueeze(1).to_broadcast([P, PK, PK]), ALU.mult))
                            then(dve.reduce_sum(sel[:, s, b, bass.ds(h * PK, PK)], oh, AX))

                        dve.wait_ge(key_copied, h + (b * PH + 1))
                        for j in range(BODY):
                            ahead = j + NSPLIT
                            split_lo(AT_U, i + ahead // BODY, ahead % BODY)
                            if j == 0:
                                top8(*side(0), 0)
                                drop8(side(0)[0], side(0)[1])
                            elif j == 1:
                                top8(*side(0), 8)
                                top8(*side(1), 0)
                            elif j == 2:
                                drop8(side(1)[0], side(1)[1])
                                top8(*side(1), 8)
                                dve.tensor_copy(key_num[:], top_i[:]).then_inc(key_read, 1)
                                dve.wait_ge(key_read, h + (b * PH + 1))
                            elif j == 3:
                                then(dve.tensor_tensor(cand[:].rearrange("p (a c) -> p a c", c=PK),
                                                       top_v[:, 0, :].unsqueeze(2).to_broadcast([P, PK, PK]),
                                                       top_v[:, 1, :].unsqueeze(1).to_broadcast([P, PK, PK]), ALU.add))
                                top8(cand[:], top_v[:, 0, :], top_i[:, 0, :], 0)
                            elif j == 4:
                                drop8(cand[:], top_v[:, 0, :])
                                top8(cand[:], top_v[:, 0, :], top_i[:, 0, :], 8)
                            elif j == 5:
                                then(dve.tensor_copy(sel[:, 2, b, bass.ds(h * PK, PK)], top_v[:, 0, :]))
                                then(dve.tensor_scalar(pos[:, 0, :], top_i[:, 0, :], 4, None, ALU.logical_shift_right))
                                then(dve.tensor_scalar(pos[:, 1, :], top_i[:, 0, :], PK - 1, None, ALU.bitwise_and))
                            else:
                                lookup(j - 6)
                        dve.sem_clear(route_step)

                    def gate_weights(b):
                        top_s = sel[:, 2, b, :].rearrange("p (h k) -> p h k", k=PK)
                        own(mark(dve.tensor_copy(small[:, 40:48], top_s[:, :, 0])))
                        dve.tensor_tensor(top_s, top_s, small[:, 40:48].unsqueeze(2).to_broadcast([P, PH, PK]),
                                          ALU.subtract).then_inc(gate_arg, 1)

                    def gate_sums(b):
                        top_s = sel[:, 2, b, :].rearrange("p (h k) -> p h k", k=PK)
                        dve.wait_ge(gate_exp, b + 1)
                        own(mark(dve.reduce_sum(small[:, 48:56], top_s, AX)))
                        own(mark(dve.reciprocal(small[:, 56:64], small[:, 48:56])))
                        dve.tensor_tensor(top_s, top_s, small[:, 56:64].unsqueeze(2).to_broadcast([P, PH, PK]),
                                          ALU.mult).then_inc(routed, 1)

                    def second_keys(s, p, first=False):
                        if not first:
                            dve.wait_ge(gate_mm, s - 1)
                        for t in range(TG):
                            col = s * TG + t
                            last = dve.tensor_scalar(oh2[p][:, t, :], iota_k[:], sel_t[:, 1, bass.ds(col, 1)],
                                                     sel_t[:, 2, bass.ds(col, 1)], ALU.is_equal, ALU.mult)
                        last.then_inc(oh2_done, 1)

                    def build_split(i, b, j, last=False):
                        ahead = j + NSPLIT
                        if b == NB - 1 and last and ahead >= BODY:
                            split_lo(AT_V, 0, ahead % BODY)
                        else:
                            split_lo(AT_U, i + (2 * b + 1) * quarter + ahead // BODY, ahead % BODY)

                    def build_body(i, b, last=False):
                        for j in range(BODY):
                            build_split(i, b, j, last=last)
                            if j % 2 and not (last and j == BODY - 1):
                                second_keys(i * NRAW + (b * STEPS + j // 2 + 1), (j // 2 + 1) % 2)

                    def first_build_body(b):
                        gate_weights(b)
                        for j in range(BODY):
                            build_split(0, b, j)
                            if j == 1:
                                gate_sums(b)
                            if j == 3:
                                dve.wait_ge(sel_stored, b + 1)
                            if j >= 3:
                                second_keys(b * STEPS + j - 3, (j - 3) % 2, first=(b == 0 and j < 5))

                    for b in range(NB):
                        with dve.Fori(0, PH) as h:
                            route_body(h + 2 * b * quarter, b, h)
                        first_build_body(b)
                        with dve.Fori(1, quarter - 1) as i:
                            build_body(i, b)
                        build_body(quarter - 1, b, last=True)

                    def product(i, m, first=False):
                        dve.wait_ge(gelu_got[m], i * 16 + 16)
                        dve.wait_ge(gate_got[m], i * 16 + 16)
                        if not first:
                            dve.wait_ge(al_done, i * NRAW + (m - 1))
                        dve.tensor_tensor(prod[m % 2][:, 0:P], gelu_in[m][:, 0:P], gate_in[m], ALU.mult)
                        dve.tensor_tensor(prod[m % 2][:, P:L], gelu_in[m][:, P:L], gates[:, i * NRAW + m, :] if isinstance(i, int)
                                          else gates[:, bass.ds(i * NRAW + m, 1), :].rearrange("p a t -> p (a t)"),
                                          ALU.mult).then_inc(prod_done, 1)

                    def a_low(i, m):
                        dve.wait_ge(ah_done, i * NRAW + (m + 1))
                        dve.tensor_tensor(al[m % 2], prod[m % 2], ah[m % 2].bitcast(F32), ALU.subtract).then_inc(al_done, 1)

                    def second_body(i, last=False):
                        for j in range(BODY):
                            m = j // 2
                            if j % 2 == 0 and not (last and m + 2 >= NRAW):
                                product(i + (m + 2) // NRAW, (m + 2) % NRAW)
                            if j % 2 == 0 and not (last and m + 1 >= NRAW):
                                a_low(i + (m + 1) // NRAW, (m + 1) % NRAW)
                            ahead = j + NSPLIT
                            if not last or ahead < BODY:
                                split_lo(AT_V, i + ahead // BODY, ahead % BODY)

                    dve.wait_ge(gate_evac, NB * STEPS)
                    product(0, 0, first=True)
                    product(0, 1, first=True)
                    a_low(0, 0)
                    with dve.Fori(0, N_V // BODY - 1) as i:
                        second_body(i)
                    second_body(N_V // BODY - 1, last=True)
                    pending = []
                    for q in range(4):
                        dve.wait_ge(half_used, N_HALVES - 1 + q // 2)
                        for b in range(NB):
                            pending.append((b, q, onto_residual(b, q, bank[4 * b + q][:])))
                            if len(pending) > 1:
                                moments(*pending.pop(0))
                    layer_norm(1, moments(*pending.pop(0)))

            nc.all_engine_barrier()
            nc.gpsimd.sem_clear(range(sems[0].num, sems[-1].num + 1))
            nc.all_engine_barrier()

        with nc.Block() as block:
            @block.sync
            def _(sp):
                sp.dma_start(out, x[:]).then_inc(first_sem, 16)
                sp.wait_ge(first_sem, 48 + 16)
                for s in first_in:
                    sp.wait_ge(s, 16 * (DEPTH + 1))


_SPLITS = (512, 128, 128, 512, 512, 512, 512, 512, 512, 512, 64, 64, 512, 64, 8)


def _masks():
    q, k = np.arange(P)[:, None] + P, np.arange(2 * P)[None, :]
    d = q - k
    causal = d >= 0
    count = (causal & (d <= 128)).astype(np.float32) + (causal & (d % 4 == 0)) + (causal & (d % 16 == 0))
    swa = causal & (d <= 127)
    return np.stack([np.where(causal, 0, NEG), np.where(swa, 0, NEG), np.where(count > 0, 0, NEG), count]).astype(np.float32)


def _rope():
    inv = (10000.0 ** (-np.arange(HALF, dtype=np.float32) / np.float32(HALF))).astype(np.float32)
    ang = np.arange(L, dtype=np.float32)[:, None] * inv[None, :]
    c, s = np.cos(ang).astype(np.float32), np.sin(ang).astype(np.float32)
    t = np.stack([np.concatenate([c, c], -1), np.concatenate([-s, s], -1)], 1)
    return np.ascontiguousarray(t.reshape(NB, P, 2, HD).transpose(1, 0, 2, 3).reshape(P, NB * 2 * HD))


def _row_tiles(w):
    n = w.shape[-1] // W
    rows = TILE // W
    t = w.reshape(DEPTH, DC // rows, rows, P, n, W).transpose(0, 4, 1, 3, 2, 5)
    return np.ascontiguousarray(t).reshape(DEPTH, n * DC // rows, P, TILE)


def kernel(x, w_in, attn_sinks, diff_lambda, diff_norm_g, w_out, ln1_g, ln1_b, peer_wq, peer_keys, peer_u, peer_v,
           ln2_g, ln2_b):
    import concourse.bacc as bacc
    from concourse.bass_utils import run_bass_kernel_spmd

    x, w_in, w_out, peer_wq, peer_keys, peer_u, peer_v = (
        np.asarray(a) for a in (x, w_in, w_out, peer_wq, peer_keys, peer_u, peer_v))
    cuts = np.cumsum(_SPLITS)[:-1]
    aq, ak, av, bq, bk, bv, cq, ck, cv, dq, dk, dv, iq, ik, iw = np.split(w_in, cuts, axis=-1)
    pad = np.zeros((DEPTH, D, NG_IN * W - w_in.shape[-1]), np.float32)
    w_in_cols = np.concatenate([aq, bq, bk, cq, ck, dq, iq, ak, dk, ik, av, dv, iw, pad, bv, cv], -1)
    lam_init = [0.8 - 0.6 * math.exp(-0.3 * i) for i in range(DEPTH)]
    arrays = {
        "x_in": x.reshape(NB, P, D).transpose(1, 0, 2),
        "w_in": _row_tiles(w_in_cols),
        "w_out": _row_tiles(w_out),
        "wq": _row_tiles(peer_wq),
        "keys": peer_keys.reshape(DEPTH, 2 * PH, NKEY, P).transpose(0, 3, 1, 2),
        "u_t": peer_u.reshape(DEPTH, NKEY, NKEY, DC, P).transpose(0, 2, 4, 3, 1).reshape(DEPTH, NKEY, P, DC * NKEY),
        "v_t": peer_v.reshape(DEPTH, NKEY, NKEY, D).transpose(0, 2, 1, 3),
        "ln": np.stack([np.stack([ln1_g, ln1_b], 1), np.stack([ln2_g, ln2_b], 1)], 1),
        "sinks": np.asarray(attn_sinks),
        "lamp": np.asarray(diff_lambda).reshape(DEPTH, 4 * HD),
        "subg": np.asarray(diff_norm_g),
        "layer_consts": np.array([[v, 1.0 - v, EPS, 0.0] for v in lam_init], np.float32),
        "rope": _rope(),
        "masks": _masks(),
        "eye": np.eye(P, dtype=np.float32),
        "iota": np.arange(NKEY, dtype=np.float32)[None, :],
    }
    arrays = {k: np.ascontiguousarray(v) for k, v in arrays.items()}
    nc = bacc.Bacc("TRN2", target_bir_lowering=False, num_devices=1)
    aps = {k: nc.dram_tensor(k, v.shape, F32, kind="ExternalInput").ap() for k, v in arrays.items()}
    out = nc.dram_tensor("out", [P, NB, D], F32, kind="ExternalOutput").ap()
    build(nc, out=out, **aps)
    r = run_bass_kernel_spmd(nc, [arrays], core_ids=[0])
    got = r.results[0]["out"]
    return np.ascontiguousarray(np.asarray(got).reshape(P, NB, D).transpose(1, 0, 2)).reshape(1, L, D)
```

```python
from contextlib import ExitStack
import math

import numpy as np

import concourse.bass as bass
from concourse import mybir

F32 = mybir.dt.float32
F32R = mybir.dt.float32r
U32 = mybir.dt.uint32
ALU = mybir.AluOpType
ACT = mybir.ActivationFunctionType
AX = mybir.AxisListType.X

P = 128
DEPTH, D, L = 2, 2048, 256
NB = L // P
DC = D // P
W = 512
HD = 64
HALF = HD // 2
TILE = 2048
HT = TILE // 2
NRAW, NSPLIT = 4, 4
BODY = 2 * NRAW
ALPHA = (2 * DEPTH) ** 0.25
NEG = -1e30
TAKEN = -3e38
EPS = 1e-5
SCALE = HD ** -0.5
TOPK = min(256, L // 4)
PH, PK, NKEY = 8, 16, 128
NSEL = PH * PK
NE = NKEY * NKEY

G_AQ, G_BQ, G_BK, G_CQ, G_CK, G_DQ, G_IQ, G_MIX, G_BV, G_CV = range(10)
NG_IN = 10
KC = HT // W
HPG = DC // KC
NT = NE // P
N_IN, N_OUT, N_WQ, N_U, N_V = NG_IN * HPG, D // W * HPG, D // W * HPG, 2 * NT, 2 * NT
AT_IN = 0
AT_OUT = AT_IN + N_IN
AT_WQ = AT_OUT + N_OUT
AT_U = AT_WQ + N_WQ
AT_V = AT_U + N_U
N_HALVES = AT_V + N_V
PAIR = {"aq": 0, "bq": 4, "bk": 8, "cq": 12, "ck": 16, "dq": 20, "iq": 24, "ak": 28, "dk": 30, "ik": 31}
V_A, V_D, V_IW, V_B, V_C, V_END = 0, 128, 192, 200, 712, 1224
MIX_A, MIX_B, MIX_C, MIX_D = 0, 512, 1024, 1536
N_IHEADS = 8 * NB
TOP_STEPS = 2 * (TOPK // 8 + 1)
TOP_UNITS = [17, 19, 21] + list(range(23, 23 + TOP_STEPS - 3))
AT_SQUARES = 28
AT_ROOT = 38
SPLIT_UNITS = [40, 43, 46, 49]


def units():
    out = []
    item = 0
    for kind, heads in (("A", 8), ("B", 4), ("C", 8), ("D", 8)):
        for h in range(heads):
            for b in range(NB):
                n = 2 if kind == "B" else 1
                out.append((kind, h, b, list(range(item, item + n))))
                item += n
    return out, item


def score_operands(kind, h, part):
    if kind == "A":
        return PAIR["aq"] + h // 2, PAIR["ak"] + h // 4, h % 2
    if kind == "B":
        return PAIR["bq"] + h, PAIR["bk"] + h, part
    if kind == "C":
        return PAIR["cq"] + h // 2, PAIR["ck"] + h // 2, h % 2
    return PAIR["dq"] + h // 2, PAIR["dk"], h % 2


def build(nc, x_in, w_in, w_out, wq, keys, u_t, v_t, ln, sinks, lamp, subg, layer_consts,
          rope, masks, eye, iota, out):
    UNITS, N_ITEMS = units()
    n_units = len(UNITS)
    a_dram = nc.dram_tensor("gates_scratch", [NKEY, P, P], F32, kind="Internal").ap()
    g_dram = nc.dram_tensor("gelu_scratch", [NKEY, P, L], F32, kind="Internal").ap()

    with ExitStack() as ctx:
        def sb(name, shape, dt=F32):
            return ctx.enter_context(nc.sbuf_tensor(name, shape, dt))

        x = sb("x", [P, NB, D])
        xh = sb("xh", [P, DC, L], F32R)
        xl = sb("xl", [P, DC, L], F32R)
        raw = [sb(f"raw{i}", [P, TILE]) for i in range(NRAW)]
        hi = [sb(f"hi{i}", [P, HT], F32R) for i in range(NSPLIT)]
        lo = [sb(f"lo{i}", [P, HT], F32R) for i in range(NSPLIT)]
        arena = sb("arena", [P, 16384])
        scr = sb("scr", [P, 4096])
        ident = sb("ident", [P, P])
        iota_k = sb("iota_k", [P, NKEY])
        par = sb("par", [P, 8 + 128 + 4])
        st = sb("st", [P, 4, N_ITEMS])
        small = sb("small", [P, 80])
        key_cols = [small[:, 64 + i * 4:68 + i * 4] for i in range(2)]
        stats = sb("stats", [P, NB, 4, 6])
        norm = sb("norm", [P, NB, 5])
        sel = sb("sel", [P, 3, NB, NSEL])
        sel_t = sb("sel_t", [P, 3, L])
        gelu_out = [sb(f"gelu_out{i}", [P, L]) for i in range(2)]
        key_now = sb("key_now", [P, 2, NKEY])
        cand = sb("cand", [P, PK * PK])
        top_v = sb("top_v", [P, 2, PK])
        top_i = sb("top_i", [P, 2, PK], U32)
        key_num = sb("key_num", [P, 2, PK])
        pos = sb("pos", [P, 2, PK], U32)
        pos_num = sb("pos_num", [P, PK])
        ah = [xh[:, i, :] for i in range(2)]
        al = [xl[:, i, :] for i in range(2)]

        sinks_b = par[:, 0:8]
        subg_b = par[:, 8:136]
        lay_b = par[:, 136:140]

        def region(base, *shape):
            n = int(np.prod(shape))
            v = arena[:, base:base + n]
            if len(shape) == 1:
                return v, base + n
            names = "abc"[:len(shape)]
            return v.rearrange(f"p ({' '.join(names)}) -> p {' '.join(names)}",
                               **{k: s for k, s in zip(names, shape)}), base + n

        qk_t, at = region(0, 32, L)
        vals, at = region(at, NB, V_END)
        mixed, at = region(at, NB, D)
        bias_causal, at = region(at, L)
        bias_swa, at = region(at, L)
        bias_dil, at = region(at, L)
        count_dil, at = region(at, L)
        trig, at = region(at, NB, 2, HD)
        lamp_b, at = region(at, 4 * HD)
        assert at <= 16384
        ln_gb, at = region(0, 2, D)
        q_t, at = region(at, 2 * PH, L)
        keys_sb, at = region(at, 2 * PH, NKEY)
        assert at <= 16384
        gates = arena[:, :].rearrange("p (i t) -> p i t", t=P)

        ra = [scr[:, b * W:(b + 1) * W] for b in range(NB)]
        rb = [scr[:, 1024 + b * W:1024 + (b + 1) * W] for b in range(NB)]
        rt = [scr[:, 2048 + b * W:2048 + (b + 1) * W] for b in range(NB)]
        masked = [scr[:, i * L:(i + 1) * L] for i in range(2)]
        probs = [scr[:, 512 + i * L:512 + (i + 1) * L] for i in range(4)]
        probs_t = [scr[:, 1536 + i * L:1536 + (i + 1) * L] for i in range(2)]
        relu = [scr[:, 2048 + i * L:2048 + (i + 1) * L] for i in range(2)]
        iscore = [scr[:, 2560 + b * L:2560 + (b + 1) * L] for b in range(NB)]
        iwork = [scr[:, 3072 + b * L:3072 + (b + 1) * L] for b in range(NB)]
        bias_dsa = [scr[:, 3584 + b * L:3584 + (b + 1) * L] for b in range(NB)]
        key_s = [scr[:, b * 2048:(b + 1) * 2048].rearrange("p (a n) -> p a n", n=NKEY) for b in range(NB)]
        TG = 4
        STEPS = P // TG
        quarter = N_U // BODY // 4
        assert quarter == PH and STEPS == quarter * NRAW
        LAST_STEPS = (1, 3, 5, 6)
        PIECES = 16
        ROWS = NKEY // PIECES
        oh1 = [scr[:, i * 512:(i + 1) * 512].rearrange("p (t n) -> p t n", n=NKEY) for i in range(2)]
        oh2 = [scr[:, 1024 + i * 512:1024 + (i + 1) * 512].rearrange("p (t n) -> p t n", n=NKEY)
               for i in range(2)]
        gelu_in = [scr[:, 2048 + i * L:2048 + (i + 1) * L] for i in range(4)]
        gate_in = [scr[:, 3072 + i * P:3072 + (i + 1) * P] for i in range(4)]
        prod = [scr[:, 3584 + i * L:3584 + (i + 1) * L] for i in range(2)]

        bank = [ctx.enter_context(nc.psum_tensor(f"bank{i}", [P, W], F32)) for i in range(8)]

        first_sem = ctx.enter_context(nc.semaphore("setup_loaded"))
        first_in = [ctx.enter_context(nc.semaphore(f"first_in{i}")) for i in range(NRAW)]
        sems = []

        def sem(name):
            s = ctx.enter_context(nc.semaphore(name))
            sems.append(s)
            return s

        raw_in = [sem(f"raw_in{i}") for i in range(NRAW)]
        hi_done, lo_done, half_used = sem("hi_done"), sem("lo_done"), sem("half_used")
        par_in, mask_in = sem("par_in"), sem("mask_in")
        turned, turn_hi, turn_lo = sem("turned"), sem("turn_hi"), sem("turn_lo")
        rope_parts, rope_evac = sem("rope_parts"), sem("rope_evac")
        roped, rope_turned, qk_stored, v_stored = sem("roped"), sem("rope_turned"), sem("qk_stored"), sem("v_stored")
        iscored, irelu, iacc, bias_ready = sem("iscored"), sem("irelu"), sem("iacc"), sem("bias_ready")
        scored, masked_done, nbias_done = sem("scored"), sem("masked_done"), sem("nbias_done")
        exp_done, sink_exp = sem("exp_done"), sem("sink_exp")
        mixed_probs, p_turned, p_stored = sem("mixed_probs"), sem("p_turned"), sem("p_stored")
        pv_done, head_out = sem("pv_done"), sem("head_out")
        rms_sum, rms_root, rms_scaled, mixed_done = sem("rms_sum"), sem("rms_root"), sem("rms_scaled"), sem("mixed_done")
        lam_sum, lam_exp = sem("lam_sum"), sem("lam_exp")
        out_evac = sem("out_evac")
        ln_in, ln_var, ln_root, ln_factors = sem("ln_in"), sem("ln_var"), sem("ln_root"), sem("ln_factors")
        ln_normed, ln_scaled = sem("ln_normed"), sem("ln_scaled")
        ln_done, ln_done_pool, ln_done_last = sem("ln_done"), sem("ln_done_pool"), sem("ln_done_last")
        keys_in, q_group, q_stored = sem("keys_in"), sem("q_group"), sem("q_stored")
        keyed, keys_stored = sem("keyed"), sem("keys_stored")
        key_copied, key_read = sem("key_copied"), sem("key_read")
        gate_arg, gate_exp, routed = sem("gate_arg"), sem("gate_exp"), sem("routed")
        route_step = sem("route_step")
        sel_turned, sel_stored = sem("sel_turned"), sem("sel_stored")
        oh1_done, oh2_done, gate_mm, gate_evac = sem("oh1_done"), sem("oh2_done"), sem("gate_mm"), sem("gate_evac")
        gates_out, cols_done = sem("gates_out"), sem("cols_done")
        gelu_done = sem("gelu_done")
        gelu_stored = [sem(f"gelu_stored{i}") for i in range(2)]
        gelu_got = [sem(f"gelu_got{i}") for i in range(4)]
        gate_got = [sem(f"gate_got{i}") for i in range(4)]
        prod_done, ah_done, al_done = sem("prod_done"), sem("ah_done"), sem("al_done")
        y_done = sem("y_done")
        dve_step = sem("dve_step")

        with nc.Block() as block:
            @block.sync
            def _(sp):
                sp.dma_start(x[:], x_in).then_inc(first_sem, 16)
                sp.dma_start(ident[:], eye).then_inc(first_sem, 16)
                sp.dma_start(iota_k[:], iota.partition_broadcast(P)).then_inc(first_sem, 16)
                for j in range(NRAW):
                    sp.dma_start(raw[j][:], w_in[0, j]).then_inc(first_in[j], 16)
                sp.wait_ge(first_sem, 48)

        with nc.Fori(0, DEPTH) as layer:
            def of_layer(t):
                s = t[bass.ds(layer, 1)]
                if len(t.shape) == 2:
                    return s
                names = [f"d{i}" for i in range(len(t.shape) - 1)]
                return s.rearrange(f"a {' '.join(names)} -> (a {names[0]}) {' '.join(names[1:])}")

            with nc.Block() as block:
                @block.sync
                def _(sp):
                    def load(src, at, i, j):
                        sp.wait_ge(lo_done, i * BODY + (at + 2 * j + 2 - BODY))
                        sp.dma_start(raw[j][:], src(i * NRAW + j)).then_inc(raw_in[j], 16)

                    def tiles(t):
                        def src(m):
                            return t[bass.ds(layer, 1), bass.ds(m, 1)].rearrange("a b p n -> (a b p) n")
                        return src

                    def stream(t, at, count, lo_i=0):
                        with sp.Fori(lo_i, count // BODY) as i:
                            for j in range(NRAW):
                                load(tiles(t), at, i, j)

                    sp.dma_start(sinks_b, sinks[bass.ds(layer, 1)].partition_broadcast(P)).then_inc(par_in, 16)
                    sp.dma_start(lamp_b, lamp[bass.ds(layer, 1)].partition_broadcast(P)).then_inc(par_in, 16)
                    sp.dma_start(subg_b, subg[bass.ds(layer, 1)].partition_broadcast(P)).then_inc(par_in, 16)
                    sp.dma_start(lay_b, layer_consts[bass.ds(layer, 1)].partition_broadcast(P)).then_inc(par_in, 16)
                    sp.dma_start(trig.rearrange("p a b c -> p (a b c)"), rope).then_inc(par_in, 16)
                    sp.dma_start(bias_causal, masks[0]).then_inc(mask_in, 16)
                    sp.dma_start(bias_swa, masks[1]).then_inc(mask_in, 16)
                    sp.dma_start(bias_dil, masks[2]).then_inc(mask_in, 16)
                    sp.dma_start(count_dil, masks[3]).then_inc(mask_in, 16)
                    stream(w_in, AT_IN, N_IN, 1)
                    stream(w_out, AT_OUT, N_OUT)
                    sp.wait_ge(turn_lo, 16)
                    sp.dma_start(ln_gb, ln[bass.ds(layer, 1), 0:1].rearrange("a b c n -> (a b) (c n)").partition_broadcast(P)
                                 ).then_inc(ln_in, 16)
                    sp.dma_start(keys_sb, of_layer(keys)).then_inc(keys_in, 16)
                    stream(wq, AT_WQ, N_WQ)
                    with sp.Fori(0, 2 * quarter + 1) as i:
                        for j in range(NRAW):
                            load(tiles(u_t), AT_U, i, j)
                    sp.wait_ge(gate_evac, STEPS)
                    with sp.Fori(0, PIECES // NRAW) as i:
                        for j in range(NRAW):
                            load(tiles(u_t), AT_U, i + (2 * quarter + 1), j)
                            row = i * (NRAW * ROWS) + j * ROWS
                            sp.dma_start(a_dram[bass.ds(row, ROWS)].rearrange("i p t -> p i t"),
                                         gates[:, bass.ds(row, ROWS), :]).then_inc(gates_out, 16)
                    with sp.Fori(2 * quarter + 1 + PIECES // NRAW, 4 * quarter) as i:
                        for j in range(NRAW):
                            load(tiles(u_t), AT_U, i, j)
                    sp.wait_ge(gates_out, 16 * PIECES)

                    def side(m, j, first=False):
                        if not first:
                            sp.wait_ge(prod_done, m - 3)
                        sp.dma_start(gelu_in[j], g_dram[bass.ds(m, 1)].rearrange("a p t -> (a p) t")).then_inc(gelu_got[j], 16)
                        sp.dma_start(gate_in[j], a_dram[bass.ds(m, 1)].rearrange("a p t -> (a p) t")).then_inc(gate_got[j], 16)

                    sp.wait_ge(key_copied, NB * PH)
                    for s in gelu_stored:
                        sp.wait_ge(s, 16 * (NT // 2 - 2 * NRAW))
                    for j in range(NRAW):
                        side(j, j, first=True)
                    for j in range(NRAW):
                        load(tiles(v_t), AT_V, 0, j)
                    for s in gelu_stored:
                        sp.wait_ge(s, 16 * (NT // 2))

                    def second(i):
                        for j in range(NRAW):
                            side(i * NRAW + j, j)
                            load(tiles(v_t), AT_V, i, j)

                    with sp.Fori(1, 12) as i:
                        second(i)
                    sp.dma_start(ln_gb, ln[bass.ds(layer, 1), 1:2].rearrange("a b c n -> (a b) (c n)").partition_broadcast(P)
                                 ).then_inc(ln_in, 16)
                    with sp.Fori(12, NT // NRAW) as i:
                        second(i)
                    for j in range(NRAW):
                        sp.wait_ge(lo_done, N_HALVES - BODY + 2 * j + 2)
                        sp.dma_start(raw[j][:], w_in[bass.ds((layer + 1) % DEPTH, 1), j].rearrange("a p n -> (a p) n")
                                     ).then_inc(first_in[j], 16)

                @block.tensor
                def _(pe):
                    def turn(r, src):
                        for k in range(DC // 2):
                            n = r * (DC // 2) + k
                            if n >= 4:
                                pe.wait_ge(turn_lo, n - 3)
                            if r == 2 and k % 2 == 0:
                                q = k // 2
                                pe.wait_ge(ln_done, q + 1)
                                if q < 2:
                                    pe.wait_ge(ln_done_pool, q + 1)
                                else:
                                    pe.wait_ge(ln_done_last, q - 1)
                            for c in (2 * k, 2 * k + 1):
                                for b in range(NB):
                                    last = pe.transpose(bank[4 + k % 4][:, (c % 2) * L + b * P:(c % 2) * L + (b + 1) * P],
                                                        src[:, b, c * P:(c + 1) * P], ident[:])
                            last.then_inc(turned, 1)

                    def tokens_by_half(n, j, kc, banks, first_c, last_c, width=W):
                        pe.wait_ge(lo_done, n + 1)
                        for c4 in range(KC):
                            c = kc * KC + c4
                            for b in range(NB):
                                st_h, st_l = xh[:, c, b * P:(b + 1) * P], xl[:, c, b * P:(b + 1) * P]
                                mh = hi[j % NSPLIT][:, c4 * W:c4 * W + width]
                                ml = lo[j % NSPLIT][:, c4 * W:c4 * W + width]
                                pe.matmul(banks[b][:, 0:width], st_h, mh, start=(c == first_c), stop=False)
                                pe.matmul(banks[b][:, 0:width], st_h, ml, start=False, stop=False)
                                last = pe.matmul(banks[b][:, 0:width], st_l, mh, start=False, stop=(c == last_c))
                        last.then_inc(half_used, 1)

                    def turn_rope(g, b):
                        pe.wait_ge(roped, g * NB + (b + 1))
                        if b_free_known(g):
                            pe.wait_ge(qk_stored, g * NB + (b + 1 - NB))
                        for j in range(4):
                            last = pe.transpose(bank[4 + b][:, j * P:(j + 1) * P], rt[b][:, j * P:(j + 1) * P], ident[:])
                        last.then_inc(rope_turned, 1)

                    def b_free_known(g):
                        return not (isinstance(g, int) and g == 0)

                    def in_group(g, par_, prev, free=True, width=W):
                        banks = [bank[2 * par_], bank[2 * par_ + 1]]
                        if free:
                            pe.wait_ge(rope_evac, g * NB - NB)
                        for kc in range(HPG):
                            tokens_by_half(g * HPG + (AT_IN + kc), kc, kc, banks, 0, DC - 1, width)
                            if prev is not None and kc in (2, 3):
                                turn_rope(prev, kc - 2)

                    turn(0, x)
                    pe.wait_ge(turn_lo, 8)
                    in_group(0, 0, None, free=False)
                    in_group(1, 1, 0, free=False)
                    with pe.Fori(1, 3) as i:
                        in_group(i * 2, 0, i * 2 - 1)
                        in_group(i * 2 + 1, 1, i * 2)
                    in_group(6, 0, 5)
                    in_group(G_MIX, 1, 6, width=4 * HD + V_B)
                    in_group(8, 0, 7)
                    in_group(9, 1, None)

                    def indexer_scores(k):
                        b, h = k // 8, k % 8
                        K = (b + 1) * P
                        rows = slice(HD * (h % 2), HD * (h % 2) + HD)
                        if k >= 2:
                            pe.wait_ge(irelu, k - 1)
                            pe.wait_ge(head_out, k - 1)
                        pe.matmul(bank[6 + k % 2][:, 0:K], qk_t[rows, PAIR["iq"] + h // 2, b * P:(b + 1) * P],
                                  qk_t[rows, PAIR["ik"], 0:K], start=True, stop=True).then_inc(iscored, 1)

                    def scores(u):
                        kind, h, b, items = UNITS[u]
                        K = (b + 1) * P
                        for part, n in enumerate(items):
                            qp, kp, half = score_operands(kind, h, part)
                            rows = slice(HD * half, HD * half + HD)
                            if n >= 4:
                                pe.wait_ge(masked_done, n - 3)
                            pe.matmul(bank[n % 4][:, 0:K], qk_t[rows, qp, b * P:(b + 1) * P], qk_t[rows, kp, 0:K],
                                      start=True, stop=True).then_inc(scored, 1)

                    def turn_probs(u):
                        kind, h, b, items = UNITS[u]
                        if kind in "AD":
                            pe.wait_ge(exp_done, items[-1] + 1)
                        else:
                            pe.wait_ge(mixed_probs, n_mixed(u))
                        if u >= 2:
                            pe.wait_ge(p_stored, u - 1)
                        for kb in range(b + 1):
                            last = pe.transpose(bank[4 + u % 2][:, kb * P:(kb + 1) * P],
                                                probs[items[0] % 4][:, kb * P:(kb + 1) * P], ident[:])
                        last.then_inc(p_turned, 1)

                    def values(u):
                        kind, h, b, items = UNITS[u]
                        pe.wait_ge(p_stored, u + 1)
                        if u >= 2:
                            pe.wait_ge(head_out, u - 1)
                        if u < N_IHEADS:
                            pe.wait_ge(irelu, u + 1)
                        at, width = value_columns(kind, h)
                        for kb in range(b + 1):
                            last = pe.matmul(bank[6 + u % 2][:, 0:width], probs_t[u % 2][:, kb * P:(kb + 1) * P],
                                             vals[:, kb, at:at + width], start=(kb == 0), stop=(kb == b))
                        last.then_inc(pv_done, 1)

                    def n_mixed(u):
                        return sum(UNITS[i][0] in "BC" for i in range(u + 1))

                    def value_columns(kind, h):
                        return {"A": (V_A + HD * (h // 4), HD), "B": (V_B + 2 * HD * h, 2 * HD),
                                "C": (V_C + HD * h, HD), "D": (V_D, HD)}[kind]

                    pe.wait_ge(qk_stored, 8 * NB)
                    pe.wait_ge(rope_evac, 8 * NB)
                    pe.wait_ge(v_stored, NB)
                    scores(0)
                    scores(1)
                    pe.wait_ge(v_stored, 2 * NB)
                    for u in range(n_units + 1):
                        if u + 2 < n_units:
                            scores(u + 2)
                        if u < n_units:
                            turn_probs(u)
                        if u >= 1:
                            values(u - 1)
                        if u < N_IHEADS:
                            indexer_scores(u)

                    pe.wait_ge(mixed_done, 1)
                    turn(1, mixed)
                    pe.wait_ge(turn_lo, 16)
                    for g in range(D // W):
                        if g >= 2:
                            pe.wait_ge(out_evac, NB * (g - 1))
                        for kc in range(HPG):
                            tokens_by_half(AT_OUT + g * HPG + kc, kc, kc, [bank[2 * (g % 2)], bank[2 * (g % 2) + 1]], 0, DC - 1)

                    turn(2, x)
                    pe.wait_ge(turn_lo, 24)
                    for g in range(D // W):
                        if g >= 2:
                            pe.wait_ge(q_stored, 4 * (g - 1))
                        for kc in range(HPG):
                            pe.wait_ge(lo_done, AT_WQ + g * HPG + kc + 1)
                            for j in range(4):
                                q_bank = bank[4 * (g % 2) + j][:, 0:L]
                                for c4 in range(KC):
                                    c = kc * KC + c4
                                    at = c4 * W + j * P
                                    wh, wl = hi[kc % NSPLIT][:, at:at + P], lo[kc % NSPLIT][:, at:at + P]
                                    pe.matmul(q_bank, wh, xh[:, c, :], start=(c == 0), stop=False)
                                    pe.matmul(q_bank, wh, xl[:, c, :], start=False, stop=False)
                                    last = pe.matmul(q_bank, wl, xh[:, c, :], start=False, stop=(c == DC - 1))
                            last.then_inc(half_used, 1)

                    pe.wait_ge(keys_in, 16)
                    for b in range(NB):
                        for k in range(4):
                            pe.wait_ge(q_stored, max(12, 4 * k + 4) if b == 0 else 16)
                            for j in range(4):
                                last = pe.matmul(bank[4 * b + k][:, j * P:(j + 1) * P], q_t[:, 4 * k + j, b * P:(b + 1) * P],
                                                 keys_sb[:, 4 * k + j, :], start=True, stop=True)
                            last.then_inc(keyed, 1)

                    def hidden(i, j, first=False):
                        pe.wait_ge(lo_done, i * BODY + (AT_U + j + 1))
                        if j % 2 == 0 and not first:
                            pe.wait_ge(gelu_done, i * NRAW + (j // 2 - 1))
                        h = bank[j // 2 % 2][:, 0:L]
                        for c8 in range(DC // 2):
                            c = (j % 2) * (DC // 2) + c8
                            wh, wl = hi[j % NSPLIT][:, c8 * P:(c8 + 1) * P], lo[j % NSPLIT][:, c8 * P:(c8 + 1) * P]
                            pe.matmul(h, wh, xh[:, c, :], start=(c == 0), stop=False)
                            pe.matmul(h, wh, xl[:, c, :], start=False, stop=False)
                            last = pe.matmul(h, wl, xh[:, c, :], start=False, stop=(c == DC - 1))
                        last.then_inc(half_used, 1)

                    def gate_step(s, p, first=False):
                        pe.wait_ge(oh1_done, s + 1)
                        pe.wait_ge(oh2_done, s + 1)
                        if not first:
                            pe.wait_ge(gate_evac, s - 1)
                        for t in range(TG):
                            last = pe.matmul(bank[4 + p][:, t * P:(t + 1) * P], oh1[p][:, t, :], oh2[p][:, t, :],
                                             start=True, stop=True)
                        last.then_inc(gate_mm, 1)

                    pe.wait_ge(keys_stored, 8)
                    for b in range(NB):
                        if b == 0:
                            for j in range(BODY):
                                hidden(0, j, first=j < 4)
                        with pe.Fori(2 * b * quarter + (b == 0), (2 * b + 1) * quarter) as i:
                            for j in range(BODY):
                                hidden(i, j)
                        for j in range(BODY):
                            hidden((2 * b + 1) * quarter, j)
                            if j == 3:
                                pe.wait_ge(routed, b + 1)
                                for k in range(3):
                                    last = pe.transpose(bank[2][:, k * P:(k + 1) * P], sel[:, k, b, :], ident[:])
                                last.then_inc(sel_turned, 1)
                            if j >= 4:
                                gate_step(b * STEPS + j - 4, j % 2, first=(b == 0 and j < 6))
                        with pe.Fori(1, quarter - b) as i:
                            for j in range(BODY):
                                hidden(i + (2 * b + 1) * quarter, j)
                                if j % 2:
                                    gate_step(i * 4 + (b * STEPS + j // 2), j // 2 % 2)
                    for j in range(BODY):
                        hidden(4 * quarter - 1, j)
                        if j in LAST_STEPS:
                            gate_step(2 * STEPS - 4 + j // 2, j // 2 % 2)

                    def products(b, j, slot, start=False, stop=False):
                        a_h, a_l = ah[slot][:, b * P:(b + 1) * P], al[slot][:, b * P:(b + 1) * P]
                        for q in range(2):
                            y = bank[4 * b + 2 * (j % 2) + q][:]
                            vh, vl = hi[j % NSPLIT][:, q * W:(q + 1) * W], lo[j % NSPLIT][:, q * W:(q + 1) * W]
                            pe.matmul(y, a_h, vh, start=start, stop=False)
                            pe.matmul(y, a_h, vl, start=False, stop=False)
                            last = pe.matmul(y, a_l, vh, start=False, stop=stop)
                        return last

                    def gather(i, j, start=False):
                        m, half = j // 2, j % 2
                        pe.wait_ge(lo_done, i * BODY + (AT_V + j + 1))
                        if half == 0:
                            pe.wait_ge(al_done, i * NRAW + (m + 1))
                        for b in range(NB):
                            last = products(b, j, m % 2, start=start)
                        last.then_inc(half_used, 1)

                    pe.wait_ge(gelu_done, NT)
                    for j in range(BODY):
                        gather(0, j, start=(j < 2))
                    with pe.Fori(1, N_V // BODY - 1) as i:
                        for j in range(BODY):
                            gather(i, j)
                    for j in range(BODY - 4):
                        gather(N_V // BODY - 1, j)
                    for b in range(NB):
                        for j in range(BODY - 4, BODY):
                            pe.wait_ge(lo_done, N_HALVES - BODY + j + 1)
                            pe.wait_ge(al_done, NT - NRAW + j // 2 + 1)
                            last = products(b, j, j // 2 % 2, stop=j >= BODY - 2)
                            if j >= BODY - 2:
                                last.then_inc(y_done, 1)

                @block.scalar
                def _(act):
                    def split_hi(at, i, j, first=False):
                        if at == AT_IN and isinstance(i, int) and i == 0:
                            act.wait_ge(first_in[j // 2], layer * 16 + 16)
                        else:
                            act.wait_ge(raw_in[j // 2], i * 16 + at // BODY * 16)
                        if not first:
                            act.wait_ge(half_used, i * BODY + (at + j + 1 - NSPLIT))
                        half = raw[j // 2][:, (j % 2) * HT:(j % 2 + 1) * HT]
                        act.activation(hi[j % NSPLIT][:], half, ACT.Copy).then_inc(hi_done, 1)

                    def turn_high(r):
                        for k in range(DC // 2):
                            act.wait_ge(turned, r * (DC // 2) + k + 1)
                            act.activation(xh[:, 2 * k:2 * k + 2, :].rearrange("p a b -> p (a b)"), bank[4 + k % 4][:],
                                           ACT.Copy).then_inc(turn_hi, 1)

                    def store_qk(g, b):
                        act.wait_ge(rope_turned, NB * g + b + 1)
                        act.activation(qk_t[:, 4 * g:4 * g + 4, b * P:(b + 1) * P],
                                       bank[4 + b][:].rearrange("p (a b) -> p a b", a=4), ACT.Copy).then_inc(qk_stored, 1)

                    def store_v(g, at):
                        act.wait_ge(half_used, AT_IN + HPG * (g + 1))
                        for b in range(NB):
                            act.activation(vals[:, b, at:at + W], bank[2 * (g % 2) + b][:], ACT.Copy).then_inc(v_stored, 1)

                    def store_q_group(g):
                        act.wait_ge(half_used, AT_WQ + HPG * (g + 1))
                        for j in range(4):
                            act.activation(q_t[:, 4 * g + j, :], bank[4 * (g % 2) + j][:, 0:L], ACT.Copy).then_inc(q_stored, 1)

                    turn_high(0)
                    for j in range(NSPLIT):
                        split_hi(AT_IN, 0, j, first=True)
                    for g in range(NG_IN):
                        for kc in range(HPG):
                            if g or kc >= NSPLIT:
                                split_hi(AT_IN, g, kc)
                            if (g, kc) == (2, 0):
                                act.wait_ge(lam_sum, 2)
                                act.activation(small[:, 2:4], small[:, 0:2], ACT.Exp).then_inc(lam_exp, 1)
                            if 1 <= g <= 8 and kc >= 6:
                                store_qk(g - 1, kc - 6)
                            if g == 9 and kc == 4:
                                store_v(8, V_B)
                    store_v(9, V_C)


                    def indexer_relu(k):
                        K = (k // 8 + 1) * P
                        act.wait_ge(iscored, k + 1)
                        if k >= 2:
                            act.wait_ge(iacc, k - 1)
                        act.activation(relu[k % 2][:, 0:K], bank[6 + k % 2][:, 0:K], ACT.Relu).then_inc(irelu, 1)

                    def exps(u):
                        kind, h, b, items = UNITS[u]
                        K = (b + 1) * P
                        for n in items:
                            act.wait_ge(nbias_done, n + 1)
                            if n >= 4:
                                act.wait_ge(p_turned, unit_of(n - 4) + 1)
                            act.activation(probs[n % 4][:, 0:K], masked[n % 2][:, 0:K], ACT.Exp, bias=st[:, 1, n:n + 1],
                                           scale=SCALE, accum_out=st[:, 2, n:n + 1]).then_inc(exp_done, 1)
                            if kind == "A":
                                act.activation(small[:, 16 + n:17 + n], sinks_b[:, h:h + 1], ACT.Exp,
                                               bias=st[:, 1, n:n + 1]).then_inc(sink_exp, 1)

                    def unit_of(n):
                        return next(i for i, w in enumerate(UNITS) if n in w[3])

                    exps(0)
                    for u in range(n_units):
                        if u + 1 < n_units:
                            exps(u + 1)
                        K = (UNITS[u][2] + 1) * P
                        act.wait_ge(p_turned, u + 1)
                        if u >= 2:
                            act.wait_ge(pv_done, u - 1)
                        act.activation(probs_t[u % 2][:, 0:K], bank[4 + u % 2][:, 0:K], ACT.Copy).then_inc(p_stored, 1)
                        if u < N_IHEADS:
                            indexer_relu(u)
                        if u == AT_ROOT:
                            act.wait_ge(rms_sum, 8)
                            act.activation(small[:, 48:56], small[:, 40:48], ACT.Sqrt, bias=lay_b[:, 2:3],
                                           scale=1.0 / (2 * HD)).then_inc(rms_root, 1)
                        if u in SPLIT_UNITS:
                            split_hi(AT_OUT, 0, SPLIT_UNITS.index(u))
                    turn_high(1)
                    for m in range(NSPLIT, N_OUT):
                        split_hi(AT_OUT, m // BODY, m % BODY)
                    for j in range(NSPLIT):
                        split_hi(AT_WQ, 0, j)

                    def layer_norm(k):
                        for b in range(NB):
                            act.wait_ge(ln_var, k * NB + b + 1)
                            act.activation(norm[:, b, 2:3], norm[:, b, 1:2], ACT.Sqrt, bias=lay_b[:, 2:3]).then_inc(ln_root, 1)
                        act.wait_ge(ln_factors, k + 1)
                        for q in range(2):
                            cols = x[:, 1, q * W:(q + 1) * W]
                            act.activation(cols, cols, ACT.Identity, bias=norm[:, 1, 4:5], scale=norm[:, 1, 3:4]).then_inc(ln_normed, 1)

                    layer_norm(0)
                    turn_high(2)
                    for m in range(NSPLIT, N_WQ):
                        split_hi(AT_WQ, m // BODY, m % BODY)
                        if m >= BODY and m % BODY == NSPLIT - 1:
                            store_q_group(m // BODY - 1)
                    for j in range(NSPLIT - 1):
                        split_hi(AT_U, 0, j)
                    store_q_group(3)
                    split_hi(AT_U, 0, NSPLIT - 1)
                    for k in range(8):
                        act.wait_ge(keyed, k + 1)
                        act.activation(key_s[k // 4][:, 4 * (k % 4):4 * (k % 4) + 4, :],
                                       bank[k][:].rearrange("p (a n) -> p a n", a=4), ACT.Copy).then_inc(keys_stored, 1)

                    def gelu(i, m, rounds, first=False):
                        act.wait_ge(half_used, i * BODY + (AT_U + 2 * m + 2))
                        if not first:
                            act.wait_ge(gelu_stored[m % 2], rounds * 16)
                        act.activation(gelu_out[m % 2][:], bank[m % 2][:, 0:L], ACT.Gelu).then_inc(gelu_done, 1)
                        act.wait_ge(gelu_done, i * NRAW + (m + 1))
                        act.dma_start(g_dram[bass.ds(i * NRAW + m, 1)].rearrange("a p t -> (a p) t"), gelu_out[m % 2][:]
                                      ).then_inc(gelu_stored[m % 2], 16)

                    def place_gates(s, col, p, b):
                        act.wait_ge(gate_mm, s + 1)
                        if b:
                            act.wait_ge(gates_out, 16 * PIECES)
                        else:
                            act.wait_ge(keyed, 8)
                        act.activation(gates.rearrange("p i t -> p t i")[:, bass.ds(col, TG), :],
                                       bank[4 + p][:].rearrange("p (t i) -> p t i", t=TG), ACT.Copy).then_inc(gate_evac, 1)

                    def half_body(i, j, first=False, last=False):
                        if j % 2:
                            gelu(i, j // 2, i * 2 + j // 2 // 2, first=first and j < 4)
                        ahead = j + NSPLIT
                        if not last or ahead < BODY:
                            split_hi(AT_U, i + ahead // BODY, ahead % BODY)
                        else:
                            split_hi(AT_V, 0, ahead % BODY)

                    for b in range(NB):
                        if b == 0:
                            for j in range(BODY):
                                half_body(0, j, first=True)
                        with act.Fori(2 * b * quarter + (b == 0), (2 * b + 1) * quarter) as i:
                            for j in range(BODY):
                                half_body(i, j)
                        for j in range(BODY):
                            half_body((2 * b + 1) * quarter, j)
                            if j == 1:
                                act.wait_ge(gate_arg, b + 1)
                                act.activation(sel[:, 2, b, :], sel[:, 2, b, :], ACT.Exp).then_inc(gate_exp, 1)
                            if j == 3:
                                act.wait_ge(sel_turned, b + 1)
                                act.activation(sel_t[:, :, b * P:(b + 1) * P], bank[2][:, 0:3 * P].rearrange("p (s t) -> p s t", s=3),
                                               ACT.Copy).then_inc(sel_stored, 1)
                            if j >= 4:
                                place_gates(b * STEPS + j - 4, (j - 4) * TG, j % 2, b)
                        with act.Fori(1, quarter - (b == 1)) as i:
                            for j in range(BODY):
                                half_body(i + (2 * b + 1) * quarter, j)
                                if j % 2:
                                    place_gates(i * 4 + (b * STEPS + j // 2), i * (4 * TG) + j // 2 * TG, j // 2 % 2, b)
                    def a_high(i, m):
                        act.wait_ge(prod_done, i * NRAW + (m + 1))
                        act.activation(ah[m % 2], prod[m % 2], ACT.Copy).then_inc(ah_done, 1)

                    for j in range(BODY):
                        half_body(4 * quarter - 1, j, last=True)
                        if j in LAST_STEPS:
                            place_gates(2 * STEPS - 4 + j // 2, P - 4 * TG + j // 2 * TG, j // 2 % 2, 1)
                        if j == BODY - 2:
                            a_high(0, 0)


                    def second_body(i, j, last=False):
                        if j % 2 == 0 and not (last and j + 2 >= BODY):
                            act.wait_ge(half_used, i * BODY + (AT_V + j))
                            a_high(i + (j // 2 + 1) // NRAW, (j // 2 + 1) % NRAW)
                        ahead = j + NSPLIT
                        if not last or ahead < BODY:
                            split_hi(AT_V, i + ahead // BODY, ahead % BODY)

                    with act.Fori(0, N_V // BODY - 1) as i:
                        for j in range(BODY):
                            second_body(i, j)
                    for j in range(BODY):
                        second_body(N_V // BODY - 1, j, last=True)
                    layer_norm(1)

                @block.gpsimd
                def _(pool):
                    for g in range(8):
                        for b in range(NB):
                            pool.wait_ge(rope_parts, NB * g + b + 1)
                            if g:
                                pool.wait_ge(rope_turned, NB * (g - 1) + b + 1)
                            if g < G_MIX:
                                pool.tensor_tensor(rt[b], ra[b], rb[b], ALU.add).then_inc(roped, 1)
                            else:
                                dup = rt[b].rearrange("p (h r e) -> p h r e", r=2, e=HD)
                                a4 = ra[b][:, 0:4 * HD].rearrange("p (h e) -> p h e", e=HD)
                                b4 = rb[b][:, 0:4 * HD].rearrange("p (h e) -> p h e", e=HD)
                                pool.tensor_tensor(dup[:, :, 0, :], a4, b4, ALU.add)
                                pool.tensor_tensor(dup[:, :, 1, :], a4, b4, ALU.add).then_inc(roped, 1)

                    def first_keys(s, p, first=False):
                        if not first:
                            pool.wait_ge(gate_mm, s - 1)
                        pool.tensor_copy(key_cols[p], sel_t[:, 0, bass.ds(s * TG, TG)]).then_inc(cols_done, 1)
                        pool.wait_ge(cols_done, 1)
                        for t in range(TG):
                            last = pool.tensor_scalar(oh1[p][:, t, :], iota_k[:], key_cols[p][:, t:t + 1], None, ALU.is_equal)
                        last.then_inc(oh1_done, 1)
                        pool.sem_clear(cols_done)

                    def layer_norm(k):
                        pool.wait_ge(ln_in, 16 * (k + 1))
                        for q in range(2):
                            cols = x[:, 1, q * W:(q + 1) * W]
                            pool.wait_ge(ln_normed, 2 * k + q + 1)
                            pool.tensor_tensor(cols, cols, ln_gb[:, 0, q * W:(q + 1) * W], ALU.mult).then_inc(ln_scaled, 1)
                            pool.wait_ge(ln_scaled, 2 * k + q + 1)
                            pool.tensor_tensor(cols, cols, ln_gb[:, 1, q * W:(q + 1) * W], ALU.add).then_inc(ln_done_pool, 1)

                    layer_norm(0)
                    pool.wait_ge(keys_stored, 8)
                    for b in range(NB):
                        def copy_keys(h):
                            pool.tensor_copy(key_now[:], key_s[b][:, bass.ds(h * 2, 2), :]).then_inc(key_copied, 1)
                        if b:
                            pool.wait_ge(key_read, PH)
                        copy_keys(0)
                        with pool.Fori(1, PH) as h:
                            pool.wait_ge(key_read, h + b * PH)
                            copy_keys(h)
                        pool.wait_ge(key_copied, (b + 1) * PH)
                        pool.wait_ge(sel_stored, b + 1)
                        first_keys(b * STEPS, 0, first=(b == 0))
                        first_keys(b * STEPS + 1, 1, first=(b == 0))
                        with pool.Fori(1, STEPS // 2) as i:
                            first_keys(i * 2 + b * STEPS, 0)
                            first_keys(i * 2 + (b * STEPS + 1), 1)
                    layer_norm(1)

                @block.vector
                def _(dve):
                    step = [0]

                    def mark(ins):
                        step[0] += 1
                        ins.then_inc(dve_step, 1)
                        return step[0]

                    def own(n):
                        dve.wait_ge(dve_step, n)

                    def split_lo(at, i, j):
                        dve.wait_ge(hi_done, i * BODY + (at + j + 1))
                        half = raw[j // 2][:, (j % 2) * HT:(j % 2 + 1) * HT]
                        dve.tensor_tensor(lo[j % NSPLIT][:], half, hi[j % NSPLIT][:].bitcast(F32), ALU.subtract).then_inc(lo_done, 1)

                    def turn_low(r):
                        for k in range(DC // 2):
                            dve.wait_ge(turn_hi, r * (DC // 2) + k + 1)
                            two = slice(2 * k, 2 * k + 2)
                            dve.tensor_tensor(xl[:, two, :].rearrange("p a b -> p (a b)"), bank[4 + k % 4][:],
                                              xh[:, two, :].rearrange("p a b -> p (a b)").bitcast(F32),
                                              ALU.subtract).then_inc(turn_lo, 1)

                    def rotate(g, b, heads=8, first=False):
                        dve.wait_ge(half_used, g * HPG + (AT_IN + HPG))
                        if not first:
                            dve.wait_ge(roped, g * NB + (b + 1 - NB))
                        src = bank[2 * parity(g) + b][:, 0:heads * HD].rearrange("p (h e) -> p h e", e=HD)
                        a = ra[b][:, 0:heads * HD].rearrange("p (h e) -> p h e", e=HD)
                        r = rb[b][:, 0:heads * HD].rearrange("p (h e) -> p h e", e=HD)
                        cos = trig[:, b, 0:1, :].to_broadcast([P, heads, HD])
                        sin = trig[:, b, 1:2, :].to_broadcast([P, heads, HD])
                        dve.tensor_tensor(a, src, cos, ALU.mult)
                        dve.tensor_tensor(r[:, :, 0:HALF], src[:, :, HALF:HD], sin[:, :, 0:HALF], ALU.mult)
                        return dve.tensor_tensor(r[:, :, HALF:HD], src[:, :, 0:HALF], sin[:, :, HALF:HD], ALU.mult
                                                 ).then_inc(rope_parts, 1)

                    def parity(g):
                        return g % 2 if isinstance(g, int) else g.par

                    turn_low(0)
                    for j in range(NSPLIT):
                        split_lo(AT_IN, 0, j)
                    dve.wait_ge(par_in, 16 * 5)
                    mark(dve.tensor_tensor_reduce(out=lamp_b[:, 0:HD], in0=lamp_b[:, 0:HD], in1=lamp_b[:, HD:2 * HD], scale=1.0,
                                                  scalar=0.0, op0=ALU.mult, op1=ALU.add, accum_out=small[:, 0:1]))
                    dve.tensor_tensor_reduce(out=lamp_b[:, 2 * HD:3 * HD], in0=lamp_b[:, 2 * HD:3 * HD], in1=lamp_b[:, 3 * HD:4 * HD],
                                             scale=1.0, scalar=0.0, op0=ALU.mult, op1=ALU.add,
                                             accum_out=small[:, 1:2]).then_inc(lam_sum, 2)
                    neg_lam = small[:, 5:6]

                    def head_constants():
                        dve.wait_ge(lam_exp, 1)
                        own(mark(dve.tensor_tensor(small[:, 4:5], small[:, 2:3], small[:, 3:4], ALU.subtract)))
                        own(mark(dve.tensor_tensor(neg_lam, small[:, 4:5], lay_b[:, 0:1], ALU.add)))
                        own(mark(dve.tensor_scalar(neg_lam, neg_lam, -1.0, None, ALU.mult)))
                        own(mark(dve.tensor_scalar(subg_b, subg_b, lay_b[:, 1:2], None, ALU.mult)))
                        own(mark(dve.tensor_scalar(small[:, 32:40], sinks_b, 1.0 / SCALE, None, ALU.mult)))

                    def indexer_weights():
                        dve.wait_ge(rope_evac, 8 * NB)
                        for b in range(NB):
                            n = mark(dve.tensor_scalar(small[:, 56:64] if b else small[:, 6:14], vals[:, b, V_IW:V_IW + 8],
                                                       8 ** -0.5 * SCALE, None, ALU.mult))
                        own(n)

                    for g in range(NG_IN):
                        for kc in range(HPG):
                            if g or kc >= NSPLIT:
                                split_lo(AT_IN, g, kc)
                            if (g, kc) == (3, 0):
                                head_constants()
                            if (g, kc) == (9, 0):
                                indexer_weights()
                            if 1 <= g <= 8 and kc in (3, 4):
                                pg, b = g - 1, kc - 3
                                rotate(pg, b, heads=8 if pg < G_MIX else 4, first=pg == 0)
                                if pg < G_MIX:
                                    dve.wait_ge(rope_parts, NB * pg + b + 1)
                                    dve.sem_inc(rope_evac, 1)
                                else:
                                    dve.tensor_copy(vals[:, b, 0:V_B], bank[2 * (pg % 2) + b][:, 4 * HD:4 * HD + V_B]
                                                    ).then_inc(rope_evac, 1)

                    dve.wait_ge(mask_in, 16 * 4)

                    def indexer_add(k):
                        b, h = k // 8, k % 8
                        K = (b + 1) * P
                        iw = small[:, 56:64] if b else small[:, 6:14]
                        dve.wait_ge(irelu, k + 1)
                        if h:
                            dve.wait_ge(iacc, k)
                        dve.scalar_tensor_tensor(out=iscore[b][:, 0:K], in0=relu[k % 2][:, 0:K], scalar=iw[:, h:h + 1],
                                                 in1=iscore[b][:, 0:K] if h else bias_causal[:, L - K:L], op0=ALU.mult,
                                                 op1=ALU.add).then_inc(iacc, 1)

                    width = [(b + 1) * P for b in range(NB)]
                    best = [small[:, 16:24], small[:, 24:32]]
                    top_step = [0]

                    def top_round(r):
                        if r == 0:
                            dve.wait_ge(iacc, N_IHEADS)
                        else:
                            own(top_step[0])
                        for b in range(NB):
                            scores = iscore[b][:, 0:width[b]]
                            if r == 2 * TOPK // 8:
                                last = dve.tensor_scalar(iwork[b][:, 0:width[b]], scores, TAKEN / 2, NEG, ALU.is_gt, ALU.mult)
                            elif r > 2 * TOPK // 8:
                                last = dve.tensor_tensor(bias_dsa[b][:, 0:width[b]], iwork[b][:, 0:width[b]],
                                                         bias_causal[:, L - width[b]:L], ALU.add)
                            elif r % 2 == 0:
                                last = dve.max(out=best[b], in_=scores)
                            else:
                                last = dve.match_replace(out=scores, in_to_replace=best[b], in_values=scores, imm_value=TAKEN)
                            top_step[0] = mark(last)
                        if r == TOP_STEPS - 1:
                            own(top_step[0])

                    def row_max(u):
                        kind, h, b, items = UNITS[u]
                        K = (b + 1) * P
                        for i in items:
                            dve.wait_ge(scored, i + 1)
                            if i >= 2:
                                dve.wait_ge(exp_done, i - 1)
                            bias = {"A": bias_swa, "B": bias_causal, "C": bias_dil}.get(kind)
                            bias = bias_dsa[b][:, 0:K] if bias is None else bias[:, L - K:L]
                            dve.tensor_tensor_reduce(out=masked[i % 2][:, 0:K], in0=bank[i % 4][:, 0:K], in1=bias, scale=1.0,
                                                     scalar=small[:, 32 + h:33 + h] if kind == "A" else TAKEN,
                                                     op0=ALU.add, op1=ALU.max, accum_out=st[:, 0, i:i + 1]).then_inc(masked_done, 1)

                    def exp_bias(u):
                        for i in UNITS[u][3]:
                            dve.wait_ge(masked_done, i + 1)
                            dve.tensor_scalar(st[:, 1, i:i + 1], st[:, 0, i:i + 1], -SCALE, None, ALU.mult).then_inc(nbias_done, 1)

                    inverse = {}

                    def sums(u):
                        kind, h, b, items = UNITS[u]
                        K = (b + 1) * P
                        i = items[0]
                        dve.wait_ge(exp_done, items[-1] + 1)
                        if kind == "A":
                            dve.wait_ge(sink_exp, i + 1)
                            return mark(dve.tensor_tensor(st[:, 2, i:i + 1], st[:, 2, i:i + 1], small[:, 16 + i:17 + i], ALU.add))
                        if kind == "C":
                            dve.scalar_tensor_tensor(out=probs[i % 4][:, 0:K], in0=probs[i % 4][:, 0:K], scalar=1.0,
                                                     in1=count_dil[:, L - K:L], op0=ALU.mult, op1=ALU.mult,
                                                     accum_out=st[:, 2, i:i + 1]).then_inc(mixed_probs, 1)
                        if kind == "B":
                            return mark(dve.reciprocal(st[:, 3, i:i + 2], st[:, 2, i:i + 2]))

                    def finish_probs(u, n):
                        kind, h, b, items = UNITS[u]
                        K = (b + 1) * P
                        i = items[0]
                        if kind in "AB":
                            own(n)
                        if kind == "B":
                            j = items[1]
                            own(mark(dve.tensor_scalar(probs[j % 4][:, 0:K], probs[j % 4][:, 0:K], st[:, 3, j:j + 1], neg_lam,
                                                       ALU.mult, ALU.mult)))
                            dve.scalar_tensor_tensor(out=probs[i % 4][:, 0:K], in0=probs[i % 4][:, 0:K], scalar=st[:, 3, i:i + 1],
                                                     in1=probs[j % 4][:, 0:K], op0=ALU.mult, op1=ALU.add).then_inc(mixed_probs, 1)
                            return
                        if kind == "C":
                            dve.wait_ge(mixed_probs, n_mixed(u))
                        inverse[u] = mark(dve.reciprocal(st[:, 3, i:i + 1], st[:, 2, i:i + 1]))

                    def n_mixed(u):
                        return sum(UNITS[i][0] in "BC" for i in range(u + 1))

                    def take_out(u):
                        kind, h, b, items = UNITS[u]
                        dve.wait_ge(pv_done, u + 1)
                        src = bank[6 + u % 2]
                        if kind == "B":
                            at = MIX_B + 2 * HD * h
                            dve.tensor_copy(mixed[:, b, at:at + 2 * HD], src[:, 0:2 * HD]).then_inc(head_out, 1)
                        else:
                            at = {"A": MIX_A, "C": MIX_C, "D": MIX_D}[kind] + HD * h
                            own(inverse[u])
                            dve.tensor_scalar(mixed[:, b, at:at + HD], src[:, 0:HD], st[:, 3, items[0]:items[0] + 1], None,
                                              ALU.mult).then_inc(head_out, 1)

                    def square_sum(j):
                        h, b = j // 2, j % 2
                        at = MIX_B + 2 * HD * h
                        if j == 0:
                            dve.wait_ge(head_out, 24)
                        dve.tensor_tensor_reduce(out=relu[j % 2][:, 0:2 * HD], in0=mixed[:, b, at:at + 2 * HD],
                                                 in1=mixed[:, b, at:at + 2 * HD], scale=1.0, scalar=0.0, op0=ALU.mult, op1=ALU.add,
                                                 accum_out=small[:, 40 + j:41 + j]).then_inc(rms_sum, 1)
                        dve.wait_ge(rms_sum, j + 1)

                    def rms_scale(j):
                        h, b = j // 2, j % 2
                        at = MIX_B + 2 * HD * h
                        dve.scalar_tensor_tensor(out=mixed[:, b, at:at + 2 * HD], in0=mixed[:, b, at:at + 2 * HD],
                                                 scalar=small[:, 40 + j:41 + j], in1=subg_b, op0=ALU.mult, op1=ALU.mult
                                                 ).then_inc(rms_scaled, 1)

                    row_max(0)
                    exp_bias(0)
                    for u in range(n_units + 2):
                        if u + 1 < n_units:
                            row_max(u + 1)
                        if u < n_units:
                            n = sums(u)
                        if u + 1 < n_units:
                            exp_bias(u + 1)
                        if u < n_units:
                            finish_probs(u, n)
                        if u >= 2:
                            take_out(u - 2)
                        if 0 <= u - 1 < N_IHEADS:
                            indexer_add(u - 1)
                        if u in TOP_UNITS:
                            top_round(TOP_UNITS.index(u))
                        if 0 <= u - AT_SQUARES < 8:
                            square_sum(u - AT_SQUARES)
                        if u == AT_ROOT + 3:
                            dve.wait_ge(rms_root, 1)
                            own(mark(dve.reciprocal(small[:, 40:48], small[:, 48:56])))
                        if 0 <= u - (AT_ROOT + 4) < 8:
                            rms_scale(u - (AT_ROOT + 4))
                        if u - 2 in SPLIT_UNITS:
                            split_lo(AT_OUT, 0, SPLIT_UNITS.index(u - 2))
                    dve.wait_ge(head_out, n_units)
                    dve.wait_ge(rms_scaled, 8)
                    dve.sem_inc(mixed_done, 1)
                    turn_low(1)

                    def onto_residual(b, q, src):
                        cols = x[:, b, q * W:(q + 1) * W]
                        return mark(dve.scalar_tensor_tensor(out=cols, in0=cols, scalar=ALPHA, in1=src, op0=ALU.mult, op1=ALU.add))

                    def moments(b, q, n):
                        own(n)
                        return mark(dve.bn_stats(stats[:, b, q, :], x[:, b, q * W:(q + 1) * W]))

                    def layer_norm(k, n):
                        own(n)
                        for b in range(NB):
                            dve.bn_aggr(norm[:, b, 0:2], stats[:, b, :, :].rearrange("p q s -> p (q s)")).then_inc(ln_var, 1)
                        for b in (1, 0):
                            dve.wait_ge(ln_root, k * NB + b + 1)
                            own(mark(dve.reciprocal(norm[:, b, 3:4], norm[:, b, 2:3])))
                            if b == 1:
                                dve.scalar_tensor_tensor(out=norm[:, b, 4:5], in0=norm[:, b, 0:1], scalar=-1.0, in1=norm[:, b, 3:4],
                                                         op0=ALU.mult, op1=ALU.mult).then_inc(ln_factors, 1)
                        dve.wait_ge(ln_in, 16 * (k + 1))

                        def center(b, q):
                            cols = x[:, b, q * W:(q + 1) * W]
                            return mark(dve.scalar_tensor_tensor(out=cols, in0=cols, scalar=norm[:, b, 0:1],
                                                                 in1=ln_gb[:, 0, q * W:(q + 1) * W], op0=ALU.subtract, op1=ALU.mult))

                        pieces = [(0, 0), (0, 1), (0, 2), (1, 2), (0, 3), (1, 3)]
                        n = center(*pieces[0])
                        for at, (b, q) in enumerate(pieces):
                            ahead = center(*pieces[at + 1]) if at + 1 < len(pieces) else None
                            own(n)
                            cols = x[:, b, q * W:(q + 1) * W]
                            dve.scalar_tensor_tensor(out=cols, in0=cols, scalar=norm[:, b, 3:4], in1=ln_gb[:, 1, q * W:(q + 1) * W],
                                                     op0=ALU.mult, op1=ALU.add).then_inc(ln_done_last if b else ln_done, 1)
                            n = ahead

                    def take_out_group(g):
                        dve.wait_ge(half_used, AT_OUT + HPG * (g + 1))
                        n = []
                        for b in range(NB):
                            n.append(onto_residual(b, g, bank[2 * (g % 2) + b][:]))
                        for b in range(NB):
                            last = moments(b, g, n[b])
                            if g < 2:
                                dve.sem_inc(out_evac, 1)
                        return last

                    for m in range(NSPLIT, N_OUT):
                        split_lo(AT_OUT, m // BODY, m % BODY)
                        if m >= BODY and m % BODY == NSPLIT - 1:
                            take_out_group(m // BODY - 1)
                    for j in range(NSPLIT - 1):
                        split_lo(AT_WQ, 0, j)
                    layer_norm(0, take_out_group(3))
                    split_lo(AT_WQ, 0, NSPLIT - 1)
                    turn_low(2)
                    for m in range(NSPLIT, N_WQ):
                        split_lo(AT_WQ, m // BODY, m % BODY)
                    for j in range(NSPLIT):
                        split_lo(AT_U, 0, j)

                    def route_body(i, b, h):
                        done = [0]

                        def then(ins):
                            done[0] += 1
                            ins.then_inc(route_step, 1)
                            dve.wait_ge(route_step, done[0])

                        def top8(src, v, idx, k):
                            then(dve.max(out=v[:, k:k + 8], in_=src))
                            then(dve.max_index(out=idx[:, k:k + 8], in_max=v[:, k:k + 8], in_values=src))

                        def drop8(src, v):
                            then(dve.match_replace(out=src, in_to_replace=v[:, 0:8], in_values=src, imm_value=TAKEN))

                        def side(s):
                            return key_now[:, s, :], top_v[:, s, :], top_i[:, s, :]

                        def lookup(s):
                            oh = cand[:].rearrange("p (k c) -> p k c", c=PK)
                            then(dve.tensor_copy(pos_num[:], pos[:, s, :]))
                            then(dve.tensor_tensor(oh, iota_k[:, 0:PK].unsqueeze(1).to_broadcast([P, PK, PK]),
                                                   pos_num[:].unsqueeze(2).to_broadcast([P, PK, PK]), ALU.is_equal))
                            then(dve.tensor_tensor(oh, oh, key_num[:, s, :].unsqueeze(1).to_broadcast([P, PK, PK]), ALU.mult))
                            then(dve.reduce_sum(sel[:, s, b, bass.ds(h * PK, PK)], oh, AX))

                        dve.wait_ge(key_copied, h + (b * PH + 1))
                        for j in range(BODY):
                            ahead = j + NSPLIT
                            split_lo(AT_U, i + ahead // BODY, ahead % BODY)
                            if j == 0:
                                top8(*side(0), 0)
                                drop8(side(0)[0], side(0)[1])
                            elif j == 1:
                                top8(*side(0), 8)
                                top8(*side(1), 0)
                            elif j == 2:
                                drop8(side(1)[0], side(1)[1])
                                top8(*side(1), 8)
                                dve.tensor_copy(key_num[:], top_i[:]).then_inc(key_read, 1)
                                dve.wait_ge(key_read, h + (b * PH + 1))
                            elif j == 3:
                                then(dve.tensor_tensor(cand[:].rearrange("p (a c) -> p a c", c=PK),
                                                       top_v[:, 0, :].unsqueeze(2).to_broadcast([P, PK, PK]),
                                                       top_v[:, 1, :].unsqueeze(1).to_broadcast([P, PK, PK]), ALU.add))
                                top8(cand[:], top_v[:, 0, :], top_i[:, 0, :], 0)
                            elif j == 4:
                                drop8(cand[:], top_v[:, 0, :])
                                top8(cand[:], top_v[:, 0, :], top_i[:, 0, :], 8)
                            elif j == 5:
                                then(dve.tensor_copy(sel[:, 2, b, bass.ds(h * PK, PK)], top_v[:, 0, :]))
                                then(dve.tensor_scalar(pos[:, 0, :], top_i[:, 0, :], 4, None, ALU.logical_shift_right))
                                then(dve.tensor_scalar(pos[:, 1, :], top_i[:, 0, :], PK - 1, None, ALU.bitwise_and))
                            else:
                                lookup(j - 6)
                        dve.sem_clear(route_step)

                    def gate_weights(b):
                        top_s = sel[:, 2, b, :].rearrange("p (h k) -> p h k", k=PK)
                        own(mark(dve.tensor_copy(small[:, 40:48], top_s[:, :, 0])))
                        dve.tensor_tensor(top_s, top_s, small[:, 40:48].unsqueeze(2).to_broadcast([P, PH, PK]),
                                          ALU.subtract).then_inc(gate_arg, 1)

                    def gate_sums(b):
                        top_s = sel[:, 2, b, :].rearrange("p (h k) -> p h k", k=PK)
                        dve.wait_ge(gate_exp, b + 1)
                        own(mark(dve.reduce_sum(small[:, 48:56], top_s, AX)))
                        own(mark(dve.reciprocal(small[:, 56:64], small[:, 48:56])))
                        dve.tensor_tensor(top_s, top_s, small[:, 56:64].unsqueeze(2).to_broadcast([P, PH, PK]),
                                          ALU.mult).then_inc(routed, 1)

                    def second_keys(s, p, first=False):
                        if not first:
                            dve.wait_ge(gate_mm, s - 1)
                        for t in range(TG):
                            col = s * TG + t
                            last = dve.tensor_scalar(oh2[p][:, t, :], iota_k[:], sel_t[:, 1, bass.ds(col, 1)],
                                                     sel_t[:, 2, bass.ds(col, 1)], ALU.is_equal, ALU.mult)
                        last.then_inc(oh2_done, 1)

                    def product(i, m, first=False):
                        dve.wait_ge(gelu_got[m], i * 16 + 16)
                        dve.wait_ge(gate_got[m], i * 16 + 16)
                        if not first:
                            dve.wait_ge(al_done, i * NRAW + (m - 1))
                        dve.tensor_tensor(prod[m % 2][:, 0:P], gelu_in[m][:, 0:P], gate_in[m], ALU.mult)
                        dve.tensor_tensor(prod[m % 2][:, P:L], gelu_in[m][:, P:L], gates[:, i * NRAW + m, :] if isinstance(i, int)
                                          else gates[:, bass.ds(i * NRAW + m, 1), :].rearrange("p a t -> p (a t)"),
                                          ALU.mult).then_inc(prod_done, 1)

                    def a_low(i, m):
                        dve.wait_ge(ah_done, i * NRAW + (m + 1))
                        dve.tensor_tensor(al[m % 2], prod[m % 2], ah[m % 2].bitcast(F32), ALU.subtract).then_inc(al_done, 1)

                    def build_split(i, b, j, last=False):
                        ahead = j + NSPLIT
                        if b == NB - 1 and last and ahead >= BODY:
                            split_lo(AT_V, 0, ahead % BODY)
                        else:
                            split_lo(AT_U, i + (2 * b + 1) * quarter + ahead // BODY, ahead % BODY)

                    def build_body(i, b, last=False):
                        for j in range(BODY):
                            if b == NB - 1 and last and j == BODY - 1:
                                dve.wait_ge(gate_evac, NB * STEPS)
                                product(0, 0, first=True)
                                product(0, 1, first=True)
                                a_low(0, 0)
                            build_split(i, b, j, last=last)
                            if j % 2 and not (last and j == BODY - 1):
                                second_keys(i * NRAW + (b * STEPS + j // 2 + 1), (j // 2 + 1) % 2)

                    def first_build_body(b):
                        gate_weights(b)
                        for j in range(BODY):
                            build_split(0, b, j)
                            if j == 2:
                                gate_sums(b)
                            if j == 3:
                                dve.wait_ge(sel_stored, b + 1)
                            if j >= 3:
                                second_keys(b * STEPS + j - 3, (j - 3) % 2, first=(b == 0 and j < 5))

                    for b in range(NB):
                        with dve.Fori(0, PH) as h:
                            route_body(h + 2 * b * quarter, b, h)
                        first_build_body(b)
                        with dve.Fori(1, quarter - 1) as i:
                            build_body(i, b)
                        build_body(quarter - 1, b, last=True)

                    def second_body(i, last=False):
                        for j in range(BODY):
                            m = j // 2
                            if j % 2 == 0 and not (last and m + 2 >= NRAW):
                                product(i + (m + 2) // NRAW, (m + 2) % NRAW)
                            if j % 2 == 0 and not (last and m + 1 >= NRAW):
                                a_low(i + (m + 1) // NRAW, (m + 1) % NRAW)
                            ahead = j + NSPLIT
                            if not last or ahead < BODY:
                                split_lo(AT_V, i + ahead // BODY, ahead % BODY)

                    with dve.Fori(0, N_V // BODY - 1) as i:
                        second_body(i)
                    second_body(N_V // BODY - 1, last=True)
                    pending = []
                    for b in range(NB):
                        for q in range(4):
                            dve.wait_ge(y_done, 2 * b + q // 2 + 1)
                            pending.append((b, q, onto_residual(b, q, bank[4 * b + q][:])))
                            if len(pending) > 1:
                                moments(*pending.pop(0))
                    layer_norm(1, moments(*pending.pop(0)))

            nc.all_engine_barrier()
            nc.gpsimd.sem_clear(range(sems[0].num, sems[-1].num + 1))
            nc.all_engine_barrier()

        with nc.Block() as block:
            @block.sync
            def _(sp):
                sp.dma_start(out, x[:]).then_inc(first_sem, 16)
                sp.wait_ge(first_sem, 48 + 16)
                for s in first_in:
                    sp.wait_ge(s, 16 * (DEPTH + 1))


_SPLITS = (512, 128, 128, 512, 512, 512, 512, 512, 512, 512, 64, 64, 512, 64, 8)


def _masks():
    q, k = np.arange(P)[:, None] + P, np.arange(2 * P)[None, :]
    d = q - k
    causal = d >= 0
    count = (causal & (d <= 128)).astype(np.float32) + (causal & (d % 4 == 0)) + (causal & (d % 16 == 0))
    swa = causal & (d <= 127)
    return np.stack([np.where(causal, 0, NEG), np.where(swa, 0, NEG), np.where(count > 0, 0, NEG), count]).astype(np.float32)


def _rope():
    inv = (10000.0 ** (-np.arange(HALF, dtype=np.float32) / np.float32(HALF))).astype(np.float32)
    ang = np.arange(L, dtype=np.float32)[:, None] * inv[None, :]
    c, s = np.cos(ang).astype(np.float32), np.sin(ang).astype(np.float32)
    t = np.stack([np.concatenate([c, c], -1), np.concatenate([-s, s], -1)], 1)
    return np.ascontiguousarray(t.reshape(NB, P, 2, HD).transpose(1, 0, 2, 3).reshape(P, NB * 2 * HD))


def _row_tiles(w):
    n = w.shape[-1] // W
    rows = TILE // W
    t = w.reshape(DEPTH, DC // rows, rows, P, n, W).transpose(0, 4, 1, 3, 2, 5)
    return np.ascontiguousarray(t).reshape(DEPTH, n * DC // rows, P, TILE)


def kernel(x, w_in, attn_sinks, diff_lambda, diff_norm_g, w_out, ln1_g, ln1_b, peer_wq, peer_keys, peer_u, peer_v,
           ln2_g, ln2_b):
    import concourse.bacc as bacc
    from concourse.bass_utils import run_bass_kernel_spmd

    x, w_in, w_out, peer_wq, peer_keys, peer_u, peer_v = (
        np.asarray(a) for a in (x, w_in, w_out, peer_wq, peer_keys, peer_u, peer_v))
    cuts = np.cumsum(_SPLITS)[:-1]
    aq, ak, av, bq, bk, bv, cq, ck, cv, dq, dk, dv, iq, ik, iw = np.split(w_in, cuts, axis=-1)
    pad = np.zeros((DEPTH, D, NG_IN * W - w_in.shape[-1]), np.float32)
    w_in_cols = np.concatenate([aq, bq, bk, cq, ck, dq, iq, ak, dk, ik, av, dv, iw, pad, bv, cv], -1)
    lam_init = [0.8 - 0.6 * math.exp(-0.3 * i) for i in range(DEPTH)]
    arrays = {
        "x_in": x.reshape(NB, P, D).transpose(1, 0, 2),
        "w_in": _row_tiles(w_in_cols),
        "w_out": _row_tiles(w_out),
        "wq": _row_tiles(peer_wq),
        "keys": peer_keys.reshape(DEPTH, 2 * PH, NKEY, P).transpose(0, 3, 1, 2),
        "u_t": peer_u.reshape(DEPTH, NKEY, NKEY, DC, P).transpose(0, 2, 4, 3, 1).reshape(DEPTH, NKEY, P, DC * NKEY),
        "v_t": peer_v.reshape(DEPTH, NKEY, NKEY, D).transpose(0, 2, 1, 3),
        "ln": np.stack([np.stack([ln1_g, ln1_b], 1), np.stack([ln2_g, ln2_b], 1)], 1),
        "sinks": np.asarray(attn_sinks),
        "lamp": np.asarray(diff_lambda).reshape(DEPTH, 4 * HD),
        "subg": np.asarray(diff_norm_g),
        "layer_consts": np.array([[v, 1.0 - v, EPS, 0.0] for v in lam_init], np.float32),
        "rope": _rope(),
        "masks": _masks(),
        "eye": np.eye(P, dtype=np.float32),
        "iota": np.arange(NKEY, dtype=np.float32)[None, :],
    }
    arrays = {k: np.ascontiguousarray(v) for k, v in arrays.items()}
    nc = bacc.Bacc("TRN2", target_bir_lowering=False, num_devices=1)
    aps = {k: nc.dram_tensor(k, v.shape, F32, kind="ExternalInput").ap() for k, v in arrays.items()}
    out = nc.dram_tensor("out", [P, NB, D], F32, kind="ExternalOutput").ap()
    build(nc, out=out, **aps)
    r = run_bass_kernel_spmd(nc, [arrays], core_ids=[0])
    got = r.results[0]["out"]
    return np.ascontiguousarray(np.asarray(got).reshape(P, NB, D).transpose(1, 0, 2)).reshape(1, L, D)
```
